# Optimizing a Trainium2 kernel written in Bass

```python
import jax, jax.numpy as jnp
from jax import lax
import numpy as np

D_MODEL = 1024
BATCH = 1
SEQ = 1024
DEPTH = 2
DEC_BATCH = 8
DEC_SEQ = 16
PAST_LEN = 128

CHUNK = 64
N_MIXERS = 2
N_A = (DEPTH + 1) // 2
N_B = DEPTH // 2
H_A = 4
DK = D_MODEL // (2 * H_A)
DV = D_MODEL // H_A
QK_W = H_A * DK
V_W = H_A * DV
A_PROJ = 2 * QK_W + 2 * V_W + 2 * H_A
GATE_CAP = 15.0
F_BIAS = 3.0
MLP_CHUNK = 128
G_B = 4
MLP_INNER = 2 * D_MODEL
DG = MLP_INNER // G_B
D_FF = -(-8 * D_MODEL // (3 * 256)) * 256
EPS = 1e-6

kernel_name = 'hybrid_mlstm_chunkmlp_stream_step'

def rmsnorm(x, g):
    xf = x.astype(jnp.float32)
    y = xf * lax.rsqrt(jnp.mean(xf * xf, axis=-1, keepdims=True) + EPS)
    return (y * g.astype(jnp.float32)).astype(x.dtype)

def layernorm(x, g):
    xf = x.astype(jnp.float32)
    xc = xf - jnp.mean(xf, axis=-1, keepdims=True)
    y = xc * lax.rsqrt(jnp.mean(xc * xc, axis=-1, keepdims=True) + EPS)
    return (y * g.astype(jnp.float32)).astype(x.dtype)

def soft_cap(x):
    return GATE_CAP * jnp.tanh(x / GATE_CAP)

def mlstm_chunk(carry, inp):
    C, n, m = carry
    q, k, v, ig, lf = inp
    L = q.shape[2]
    b = jnp.cumsum(lf, axis=-1)
    causal = jnp.tril(jnp.ones((L, L), dtype=bool))
    log_d = jnp.where(causal, b[..., :, None] - b[..., None, :] + ig[..., None, :], -jnp.inf)
    log_inter = b + m[..., None]
    m_t = jnp.maximum(log_inter, jnp.max(log_d, axis=-1))
    d = jnp.exp(log_d - m_t[..., None])
    s = jnp.einsum('bhtd,bhsd->bhts', q, k) * d
    w_inter = jnp.exp(log_inter - m_t)
    num = jnp.einsum('bhts,bhsv->bhtv', s, v) + w_inter[..., None] * jnp.einsum('bhvd,bhtd->bhtv', C, q)
    den = jnp.sum(s, axis=-1) + w_inter * jnp.einsum('bhd,bhtd->bht', n, q)
    h = num / jnp.maximum(jnp.abs(den), jnp.exp(-m_t))[..., None]
    m_new = m_t[..., -1]
    decay = jnp.exp(b[..., -1] + m - m_new)
    w_s = jnp.exp(b[..., -1:] - b + ig - m_new[..., None])
    C_new = decay[..., None, None] * C + jnp.einsum('bhs,bhsv,bhsd->bhvd', w_s, v, k)
    n_new = decay[..., None] * n + jnp.einsum('bhs,bhsd->bhd', w_s, k)
    return (C_new, n_new, m_new), h

def mlstm_mixer(xn, state, w_in, b_gate, g_out, w_out):
    B, S, _ = xn.shape
    p = (xn @ w_in).astype(jnp.float32)
    q, k, v, o, gi, gf = jnp.split(
        p, [QK_W, 2 * QK_W, 2 * QK_W + V_W, 2 * QK_W + 2 * V_W, 2 * QK_W + 2 * V_W + H_A], axis=-1)
    gates = soft_cap(jnp.concatenate([gi, gf], axis=-1) + b_gate.astype(jnp.float32))
    ig = gates[..., :H_A]
    lf = jax.nn.log_sigmoid(gates[..., H_A:])
    L = min(CHUNK, S)
    nc = S // L

    def heads(t, dh):
        return t.reshape(B, nc, L, H_A, dh).transpose(1, 0, 3, 2, 4)

    def gate_heads(t):
        return t.reshape(B, nc, L, H_A).transpose(1, 0, 3, 2)

    xs = (heads(q, DK) * (DK ** -0.5), heads(k, DK), heads(v, DV), gate_heads(ig), gate_heads(lf))
    final, h = lax.scan(mlstm_chunk, state, xs)
    h = h.transpose(1, 0, 3, 2, 4).reshape(B, S, H_A, DV)
    h = h * lax.rsqrt(jnp.mean(h * h, axis=-1, keepdims=True) + EPS)
    h = h.reshape(B, S, V_W) * g_out.astype(jnp.float32) * jax.nn.sigmoid(o)
    return h.astype(xn.dtype) @ w_out, final

def chunk_mlp_mixer(xn, w_in, g_v, w_s, b_s, w_out):
    B, S, _ = xn.shape
    uv = jax.nn.gelu(xn @ w_in)
    u, v = jnp.split(uv, 2, axis=-1)
    v = layernorm(v, g_v)
    L = min(MLP_CHUNK, S)
    nc = S // L
    mix = jnp.tril(w_s[:, :L, :L])
    vg = v.reshape(B, nc, L, G_B, DG)
    sv = jnp.einsum('gts,bcsgd->bctgd', mix, vg) + b_s[:, :L].T[None, None, :, :, None]
    out = (u * sv.reshape(B, S, MLP_INNER)) @ w_out
    return out, v

def swiglu(xn, w_gu, w_down):
    g, up = jnp.split(xn @ w_gu, 2, axis=-1)
    return (jax.nn.silu(g) * up) @ w_down

def trunk(x, C0, n0, m0, g_mix, g_ffn, g_final, a_w_in, a_b_gate, a_g_out, a_w_out,
          b_w_in, b_g_v, b_w_s, b_b_s, b_w_out, f_w_gu, f_w_down):
    C_out, n_out, m_out, v_rows = [], [], [], []
    for i in range(DEPTH):
        xn = rmsnorm(x, g_mix[i])
        j = i // N_MIXERS
        if i % N_MIXERS == 0:
            y, (C, n, m) = mlstm_mixer(xn, (C0[:, j], n0[:, j], m0[:, j]),
                                       a_w_in[j], a_b_gate[j], a_g_out[j], a_w_out[j])
            C_out.append(C)
            n_out.append(n)
            m_out.append(m)
        else:
            y, v = chunk_mlp_mixer(xn, b_w_in[j], b_g_v[j], b_w_s[j], b_b_s[j], b_w_out[j])
            v_rows.append(v)
        x = x + y.astype(x.dtype)
        x = x + swiglu(rmsnorm(x, g_ffn[i]), f_w_gu[i], f_w_down[i]).astype(x.dtype)
    y = rmsnorm(x, g_final)
    return y, jnp.stack(C_out, axis=1), jnp.stack(n_out, axis=1), jnp.stack(m_out, axis=1), v_rows

def setup_inputs(seed: int = 0) -> dict:
    key = jax.random.key(seed)
    ks = jax.random.split(key, 24)
    f32 = jnp.float32
    nrm = lambda k, s, sc: jax.random.normal(k, s, f32) * sc
    a_b_gate = jnp.concatenate([
        nrm(ks[8], (N_A, H_A), 0.1),
        F_BIAS + nrm(ks[9], (N_A, H_A), 0.5)], axis=-1)
    return {
        'x_prompt': nrm(ks[0], (BATCH, SEQ, D_MODEL), 1.0),
        'x_sample': nrm(ks[1], (DEC_BATCH, DEC_SEQ, D_MODEL), 1.0),
        'state_C': nrm(ks[2], (DEC_BATCH, N_A, H_A, DV, DK), 0.1),
        'state_n': nrm(ks[3], (DEC_BATCH, N_A, H_A, DK), 0.5),
        'state_m': nrm(ks[4], (DEC_BATCH, N_A, H_A), 0.5),
        'g_mix': 1.0 + nrm(ks[5], (DEPTH, D_MODEL), 0.02),
        'g_ffn': 1.0 + nrm(ks[6], (DEPTH, D_MODEL), 0.02),
        'g_final': 1.0 + nrm(ks[7], (D_MODEL,), 0.02),
        'a_w_in': nrm(ks[10], (N_A, D_MODEL, A_PROJ), D_MODEL ** -0.5),
        'a_b_gate': a_b_gate,
        'a_g_out': 1.0 + nrm(ks[11], (N_A, V_W), 0.02),
        'a_w_out': nrm(ks[12], (N_A, V_W, D_MODEL), V_W ** -0.5),
        'b_w_in': nrm(ks[13], (N_B, D_MODEL, 2 * MLP_INNER), D_MODEL ** -0.5),
        'b_g_v': 1.0 + nrm(ks[14], (N_B, MLP_INNER), 0.02),
        'b_w_s': nrm(ks[15], (N_B, G_B, MLP_CHUNK, MLP_CHUNK), MLP_CHUNK ** -0.5),
        'b_b_s': 1.0 + nrm(ks[16], (N_B, G_B, MLP_CHUNK), 0.02),
        'b_w_out': nrm(ks[17], (N_B, MLP_INNER, D_MODEL), MLP_INNER ** -0.5),
        'f_w_gu': nrm(ks[18], (DEPTH, D_MODEL, 2 * D_FF), D_MODEL ** -0.5),
        'f_w_down': nrm(ks[19], (DEPTH, D_FF, D_MODEL), D_FF ** -0.5),
    }

def reference(x_prompt, x_sample, state_C, state_n, state_m, g_mix, g_ffn, g_final,
              a_w_in, a_b_gate, a_g_out, a_w_out, b_w_in, b_g_v, b_w_s, b_b_s, b_w_out,
              f_w_gu, f_w_down):
    f32 = jnp.float32
    bp = x_prompt.shape[0]
    C0 = jnp.zeros((bp, N_A, H_A, DV, DK), f32)
    n0 = jnp.zeros((bp, N_A, H_A, DK), f32)
    m0 = jnp.zeros((bp, N_A, H_A), f32)
    y_prompt, C_prompt, n_prompt, m_prompt, _ = trunk(
        x_prompt, C0, n0, m0, g_mix, g_ffn, g_final, a_w_in, a_b_gate, a_g_out, a_w_out,
        b_w_in, b_g_v, b_w_s, b_b_s, b_w_out, f_w_gu, f_w_down)
    y_sample, C_sample, n_sample, m_sample, v_list = trunk(
        x_sample, state_C.astype(f32), state_n.astype(f32), state_m.astype(f32),
        g_mix, g_ffn, g_final, a_w_in, a_b_gate, a_g_out, a_w_out,
        b_w_in, b_g_v, b_w_s, b_b_s, b_w_out, f_w_gu, f_w_down)
    v_rows_sample = jnp.stack(v_list, axis=1)
    return (y_prompt, y_sample, C_prompt, n_prompt, m_prompt, C_sample, n_sample, m_sample, v_rows_sample)


_drawn_inputs = setup_inputs


def setup_inputs(seed=0):
    import zlib

    import numpy as np

    out = dict(_drawn_inputs(seed))
    spreads = {}
    factors = {'g_ffn': 2.974, 'g_final': 2.865, 'a_g_out': 4.658, 'b_g_v': 2.786, 'b_b_s': 5.418}
    for name, (base, spread) in spreads.items():
        noise = np.random.default_rng([zlib.crc32(name.encode()), seed]).standard_normal(out[name].shape)
        drawn = base * np.exp(spread * noise) if base else spread * noise
        out[name] = __import__('jax').numpy.asarray(drawn.astype(out[name].dtype))
    for name, factor in factors.items():
        out[name] = (out[name] * factor).astype(out[name].dtype)
    return out
```

```python
from contextlib import ExitStack

import concourse.bass as bass
import concourse.mybir as mybir
from concourse.alu_op_type import AluOpType as ALU

ACT = mybir.ActivationFunctionType
F32 = mybir.dt.float32
F32R = mybir.dt.float32r
AX_X = mybir.AxisListType.X

P = 128
D = 1024
KD = D // P
SEQ = 1024
DEC_B, DEC_S = 8, 16
NT = (SEQ + DEC_B * DEC_S) // P
NP = SEQ // P
TOK = NT * P
NG = 3
TG = TOK // NG
TPG = NT // NG
H, DK, DV = 4, 128, 256
QK_W, V_W = H * DK, H * DV
A_PROJ = 2 * QK_W + 2 * V_W + 2 * H
CAP = 15.0
INNER = 2 * D
NF = INNER // P
G_B = 4
FPG = NF // G_B
D_FF = 2816
EPS = 1e-6
BIG = 1e30
FREE_UNITS = 5

G_MIX, G_FFN, G_FINAL, G_OUT, G_V, G_ALL = 0, 2 * KD, 4 * KD, 5 * KD, 6 * KD, 6 * KD + NF
Q_A, Q_M, Q_WI, Q_EMT, Q_WS, Q_DECAY, NQ = 0, 1, 2, 3, 4, 5, 6


class WeightPhase:

    def __init__(self, before, iterations, slots, back):
        self.base = before.end if before else 0
        self.n, self.slots = len(slots), slots
        self.end = self.base + iterations * self.n
        self.back = back

    def count(self, i, u, add=0):
        return i * self.n + (self.base + u + add)

    def raw(self, u):
        return (self.base + u) % 2

    def loads(self, i, u):
        return i * (self.n // 2) + ((self.base + u) // 2 + 1)


N_FFN = D_FF // (2 * P)
W_GATES = WeightPhase(None, 1, [0], [5])
W_HEADS = WeightPhase(W_GATES, H, [2, 1, 0, 2, 0, 2, 1, 0], [3, 3, 3, 3, 2, 2, 5, 3])
W_FFN0 = WeightPhase(W_HEADS, N_FFN, [2, 1, 0, 2, 1, 0], [3] * 6)
W_BV = WeightPhase(W_FFN0, NF // 4, [2, 1, 0, 1], [3, 2, 3, 2])
W_BU = WeightPhase(W_BV, NF // 4, [2, 1, 0, 1], [3, 2, 3, 2])
W_BO = WeightPhase(W_BU, KD // 2, [2, 0, 2, 0], [2] * 4)
W_FFN1 = WeightPhase(W_BO, N_FFN, [1, 2, 0, 1, 2, 0], [3] * 6)

TICKETS = (["mb"] * 3 + ["wib"] * 3 + ["s"] * 3 + ["ctr"] * 4 + ["nt"] + ["u"] * NP + ["cfin"]
           + ["us"] * 4 + ["un"] + ["pv"] * NT + ["ht"] * 6)
BY_ACT = {"ctr", "nt", "cfin"}


def ticket(name, k=0):
    return TICKETS.index(name) + k


def taken(t):
    mine = TICKETS[t] in BY_ACT
    return sum((x in BY_ACT) == mine for x in TICKETS[:t + 1])


NTICK = len(TICKETS)
N_ACT = sum(x in BY_ACT for x in TICKETS)
N_DVE = NTICK - N_ACT


def build(nc, x_prompt, x_sample, state_C, state_n, state_m, g_mix, g_ffn, g_final,
          a_w_in, a_b_gate, a_g_out, a_w_out, b_w_in, b_g_v, b_w_s, b_b_s, b_w_out,
          f_w_gu, f_w_down,
          y_prompt, y_sample, C_prompt, n_prompt, m_prompt, C_sample, n_sample, m_sample, v_rows):
    ctx = ExitStack()
    with ctx:
        def sb(name, shape, dt=F32, stack=ctx):
            return stack.enter_context(nc.sbuf_tensor(name, shape, dt))

        def sem(name):
            return ctx.enter_context(nc.semaphore(name))

        xT = sb("xT", [P, KD, TOK])
        w_raw = [sb(f"w_raw{r}", [P, KD, P]) for r in range(2)]
        w_hi = [sb(f"w_hi{s}", [P, KD, P], F32R) for s in range(3)]
        w_lo = [sb(f"w_lo{s}", [P, KD, P], F32R) for s in range(3)]
        ident = sb("ident", [P, P])
        ones = sb("ones", [P, P])
        gains = sb("gains", [P, G_ALL])
        tri = sb("tri", [P, P])
        tri_s = sb("tri_s", [P, P])
        eps_t = sb("eps_t", [P, 1])

        with ExitStack() as part:
            xn_hi = sb("xn_hi", [P, KD, TOK], F32R, part)
            xn_lo = sb("xn_lo", [P, KD, TOK], F32R, part)
        with ExitStack() as part:
            x_in = sb("x_in", [P, NT, D], F32, part)
            gain_rows = sb("gain_rows", [G_ALL, P], F32, part)
        with ExitStack() as part:
            y_out = sb("y_out", [P, NT, D], F32, part)
        with ExitStack() as part:
            p_lo = sb("p_lo", [P, NF, TOK], F32R, part)
        hold = sb("hold_xn", [P, 2 * KD * TOK])

        with ExitStack() as part:
            def pa(name, shape, dt=F32):
                return sb(name, shape, dt, part)
            sq_a = pa("sq_a", [P, KD, TG])
            ssum_a = pa("ssum_a", [P, TG])
            rstd_a = pa("rstd_a", [P, TG])
        with ExitStack() as part:
            def pa(name, shape, dt=F32):
                return sb(name, shape, dt, part)
            qT = pa("qT", [P, TOK])
            kT = pa("kT", [P, TOK])
            k_tok = pa("k_tok", [P, NT, DK])
            v_tok = pa("v_tok", [P, NT, DV + 1])
            sig_o = pa("sig_o", [P, 2, TOK])
            dmat = pa("dmat", [P, NT, P])
            qw = pa("qw", [P, TOK])
            num = pa("num", [P, NT, DV + 1])
            c_nat = pa("c_nat", [P, 2, DEC_B, DK])
            c_out = pa("c_out", [P, 3, P])
            with ExitStack() as sub:
                state = sb("state", [P, NT, DV + 1], F32, sub)
                c_smp = sb("c_smp", [P, DEC_B, DV + 1], F32, sub)
            with ExitStack() as sub:
                h_hi = sb("h_hi", [P, 2, TOK], F32R, sub)
                h_lo = sb("h_lo", [P, 2, TOK], F32R, sub)
            hold_h = pa("hold_h", [P, 4 * TOK])
            pack = pa("pack", [P, H, NQ, NT])
            cur = pa("cur", [P, NQ, NT])
            dec_s = pa("dec_s", [P, H, DEC_B])
            dec8 = pa("dec8", [P, H])
            b_first = pa("b_first", [P, DEC_B])
            b_mem = pa("b_mem", [P, DEC_B])
            n_nat = pa("n_nat", [DEC_B, DK])
            g_bias = pa("g_bias", [2 * H, 1])
            g_h = pa("g_h", [P, 2])
            nstat = pa("nstat", [P, 6, NT])
            m_out = pa("m_out", [P, 2, H])
            m_in = pa("m_in", [P, H])
        num_flat = num[:, :, :].rearrange("p c v -> p (c v)")
        diag = num_flat[:, 0:NT * P].rearrange("p (c t) -> p c t", c=NT)
        diag2 = qw[:, :].rearrange("p (c t) -> p c t", c=NT)
        k_blk = num_flat[:, NT * P:NT * P + DEC_B * DK].rearrange("p (b d) -> p b d", b=DEC_B)
        v_tmp = dmat[:, :, :].rearrange("p c t -> p (c t)")
        q_blk = kT[:, 0:DEC_B * P].rearrange("p (b t) -> p b t", b=DEC_B)
        c_flat = c_nat[:, :, :, :].rearrange("p j b d -> p (j b d)")
        blk, blk_last, last = (c_flat[:, k * P:(k + 1) * P] for k in range(3))
        reset = c_flat[0:H * NT, 3 * P:4 * P]
        small = num_flat[:, 0:8 * H * NT].rearrange("p (q h c) -> p q h c", q=8, h=H)
        gtok = num_flat[:, 8 * H * NT:8 * H * NT + NT * 2 * H].rearrange("p (c g) -> p c g", c=NT)
        gT = qT
        aT = qw
        h_f = dmat[:, :, :].rearrange("p c t -> p (c t)")

        with ExitStack() as part:
            hg_hi = sb("hg_hi", [P, 2, TOK], F32R, part)
            hg_lo = sb("hg_lo", [P, 2, TOK], F32R, part)
            silu = sb("silu", [P, 2, NG, TG], F32, part)
            h_tmp = sb("h_tmp", [P, 2, TG], F32, part)
            sq_f = sb("sq_f", [P, KD, TG], F32, part)
            ssum_f = sb("ssum_f", [P, TG], F32, part)
            rstd_f = sb("rstd_f", [P, TG], F32, part)

        with ExitStack() as part:
            vs = sb("vs", [P, NT, NF, P], F32, part)
        with ExitStack() as part:
            p_hi = sb("p_hi", [P, NT, NF, P], F32R, part)
            mix = sb("mix", [P, 2, G_B, P], F32, part)
            with ExitStack() as sub:
                bias_b = sb("bias_b", [P, G_B, P], F32, sub)
            with ExitStack() as sub:
                w_s_in = sb("w_s_in", [P, G_B, P], F32, sub)
            hold_b = sb("hold_b", [P, G_B * P], F32, part)
            with ExitStack() as sub:
                w_s_smp = sb("w_s_smp", [P, G_B, P], F32, sub)
            t_b = sb("t_b", [P, 2, TG], F32, part)
        RQ = INNER // 4
        row_buf = [w_s_in[:, :, :].rearrange("p g s -> p (g s)"), t_b[:, :, :].rearrange("p a t -> p (a t)")[:, 0:RQ]]
        with ExitStack() as part:
            vs_pad = sb("vs_pad", [P, NT, NF, P], F32, part)
            stat = sb("stat", [P, NT, 4, 6], F32, part)
            mv = sb("mv", [P, NT, 2], F32, part)
            rs_v = sb("rs_v", [P, NT, 2], F32, part)

        ps = [ctx.enter_context(nc.psum_tensor(f"ps{b}", [P, 512], F32)) for b in range(8)]

        def bank(b, n=TG):
            return ps[b % 8][:, 0:n]

        const_ok = sem("const_ok")
        x_loaded = [sem(f"x_loaded{g}") for g in range(NG)]
        rows_loaded = sem("rows_loaded")
        small_loaded = sem("small_loaded")
        xt_pe, xt_dve, xt_act = sem("xt_pe"), sem("xt_dve"), sem("xt_act")
        raw_loaded = [sem("raw_loaded0"), sem("raw_loaded1")]
        raw_clear = sem("raw_clear")
        hi_split, split, used = sem("hi_split"), sem("units_split"), sem("units_used")
        squared, summed, mean_sq, rooted = sem("squared"), sem("summed"), sem("mean_sq"), sem("rooted")
        n_full, n_hi, n_lo = sem("n_full"), sem("n_hi"), sem("n_lo")
        dve_step = sem("dve_step")
        act_step = sem("act_step")
        pool_step = sem("pool_step")
        gt_mm, gt_act, gt_scaled, gt_tr, gate_pe, gate_dve, gate_act = (
            sem(x) for x in ("gt_mm", "gt_act", "gt_scaled", "gt_tr", "gate_pe", "gate_dve", "gate_act"))
        a_mm, a_evac, a_vtmp, a_sig = sem("a_mm"), sem("a_evac"), sem("a_vtmp"), sem("a_sig")
        a_tr, a_ktok, a_vtok = sem("a_tr"), sem("a_ktok"), sem("a_vtok")
        t_pe, t_act, t_dve = sem("t_pe"), sem("t_act"), sem("t_dve")
        a_cur, a_diag, a_dargs, a_exp, a_dve, a_kb = (
            sem(x) for x in ("a_cur", "a_diag", "a_dargs", "a_exp", "a_dve", "a_kb"))
        a_ssq, a_fac, a_hlo, a_sqrt = sem("a_ssq"), sem("a_fac"), sem("a_hlo"), sem("a_sqrt")
        wd_mm, wd_add = sem("wd_mm"), sem("wd_add")
        c_loaded, n_loaded, c_stored = sem("c_loaded"), sem("n_loaded"), sem("c_stored")
        stored = sem("stored")
        g_mm = [sem(f"g_mm{x}") for x in range(2)]
        u_mm = [sem(f"u_mm{x}") for x in range(2)]
        g_silu = [sem(f"g_silu{x}") for x in range(2)]
        h_full = [sem(f"h_full{x}") for x in range(2)]
        h_his = [sem(f"h_his{x}") for x in range(2)]
        h_los = [sem(f"h_los{x}") for x in range(2)]
        d_mm = [sem(f"d_mm{x}") for x in range(2)]
        d_add = [sem(f"d_add{x}") for x in range(2)]
        bv_mm, bv_gelu, bv_tr, bv_tok = sem("bv_mm"), sem("bv_gelu"), sem("bv_tr"), sem("bv_tok")
        b_loaded, b_mixed = sem("b_loaded"), sem("b_mixed")
        bw_tr, bw_copied, mix_ok = sem("bw_tr"), sem("bw_copied"), sem("mix_ok")
        ln_stat, ln_root, ln_done = sem("ln_stat"), sem("ln_root"), sem("ln_done")
        mx_mm, mx_act, mx_dve = sem("mx_mm"), sem("mx_act"), sem("mx_dve")
        gv_loaded, row_stored = ([sem(f"{x}{r}") for r in range(2)] for x in ("gv_loaded", "row_stored"))
        gv_done = sem("gv_done")
        bu_mm, bu_gelu, bu_gate, bu_bias = sem("bu_mm"), sem("bu_gelu"), sem("bu_gate"), sem("bu_bias")
        ps_hi, ps_lo, ps_in = sem("ps_hi"), sem("ps_lo"), sem("ps_in")
        bo_mm, bo_add = sem("bo_mm"), sem("bo_add")
        yt_pe, yt_act, yt_dve = sem("yt_pe"), sem("yt_act"), sem("yt_dve")

        block = ctx.enter_context(nc.Block())

        def tok(t, g):
            return t[..., g * TG:(g + 1) * TG]

        def tiles(ap):
            return ap.rearrange("p (c t) -> p c t", c=TPG)

        @block.sync
        def _(sp):
            for g in range(NG):
                for c in range(TPG * g, TPG * g + TPG):
                    src = x_prompt[0, c * P:(c + 1) * P, :] if c < NP else x_sample.rearrange("b s d -> (b s) d")
                    sp.dma_start(x_in[:, c, :], src).then_inc(x_loaded[g], 16)
                if g == 0:
                    for at, src, n in ((G_MIX, g_mix.rearrange("l (k p) -> (l k) p", p=P), 2 * KD),
                                       (G_FFN, g_ffn.rearrange("l (k p) -> (l k) p", p=P), 2 * KD),
                                       (G_FINAL, g_final.rearrange("(k p) -> k p", p=P), KD),
                                       (G_OUT, a_g_out.rearrange("l (k p) -> (l k) p", p=P), KD),
                                       (G_V, b_g_v.rearrange("l (k p) -> (l k) p", p=P), NF)):
                        sp.dma_start(gain_rows[at:at + n, :], src).then_inc(rows_loaded, 16)

            def load(phase, i, u, src, width=P):
                if phase is not W_GATES:
                    sp.wait_ge(split, phase.count(i, u, -1))
                r = phase.raw(u)
                dst = w_raw[r][:, :, 0:width]
                if len(src.shape) == 2:
                    dst = w_raw[r][:, :, :].rearrange("p k n -> p (k n)")
                sp.dma_start(dst, src).then_inc(raw_loaded[r], 16)

            a_in = a_w_in[0].rearrange("(k p) n -> p k n", p=P)
            sp.wait_ge(raw_clear, 1)
            load(W_GATES, 0, 0, a_in[:, :, A_PROJ - 2 * H:A_PROJ], 2 * H)
            sp.dma_start(m_in[:, :], state_m[:, 0, :].unsqueeze(1).to_broadcast([DEC_B, DEC_S, H]))\
                .then_inc(small_loaded, 16)
            sp.dma_start(g_bias[:, :], a_b_gate.rearrange("l (g o) -> (l g) o", o=1)).then_inc(small_loaded, 16)

            a_out = a_w_out[0].rearrange("(k p) n -> k p n", p=P)
            c_in = state_C[:, 0].rearrange("b h (j v) d -> h j v b d", j=2)
            c_to = C_sample[:, 0].rearrange("b h (j v) d -> h j v b d", j=2)
            n_in = state_n[:, 0].rearrange("b h d -> h b d")
            n_to = n_sample[:, 0].rearrange("b h d -> h b d")
            sp.wait_ge(gate_dve, 6)
            sp.dma_start(m_prompt[0], m_out[0:1, 0, :]).then_inc(stored, 16)
            sp.dma_start(m_sample[:, 0, :], m_out[0:P:DEC_S, 1, :]).then_inc(stored, 16)
            with sp.Fori(0, H) as h:
                for u, col in enumerate((h * DK, h * DK + QK_W)):
                    load(W_HEADS, h, u, a_in[:, :, bass.ds(col, P)])
                sp.wait_ge(c_stored, h * (16 * 5))
                for j in range(2):
                    sp.dma_start(c_nat[:, j, :, :], c_in[bass.ds(h, 1), j].rearrange("o v b d -> (o v) b d"))\
                        .then_inc(c_loaded, 16)
                sp.dma_start(n_nat[:, :], n_in[bass.ds(h, 1)].rearrange("o b d -> (o b) d")).then_inc(n_loaded, 16)
                for u in range(2, 6):
                    at = 2 * QK_W + (u % 2) * P + (V_W if u >= 4 else 0)
                    load(W_HEADS, h, u, a_in[:, :, bass.ds(h * DV + at, P)])
                for u in range(6, 8):
                    load(W_HEADS, h, u, a_out[bass.ds(h * 2 + (u - 6), 1)].rearrange("o p n -> (o p) n"))
                sp.wait_ge(t_act, h * N_ACT + taken(ticket("cfin")))
                sp.dma_start(C_prompt[0, 0].rearrange("h (j v) d -> h v j d", j=2)[bass.ds(h, 1)]
                             .rearrange("o v j d -> (o v) j d"), c_out[:, 0:2, :]).then_inc(c_stored, 16)
                sp.dma_start(n_prompt[0, 0].rearrange("h (d o) -> h d o", o=1)[bass.ds(h, 1)]
                             .rearrange("a d o -> (a d) o"), c_out[:, 2, 0:1]).then_inc(c_stored, 16)
                sp.wait_ge(t_dve, h * N_DVE + taken(ticket("un")))
                for j in range(2):
                    sp.dma_start(c_to[bass.ds(h, 1), j].rearrange("o v b d -> (o v) b d"), c_nat[:, j, :, :])\
                        .then_inc(c_stored, 16)
                sp.dma_start(n_to[bass.ds(h, 1)].rearrange("o b d -> (o b) d"), n_nat[:, :]).then_inc(c_stored, 16)

            def ffn(layer, phase):
                gu = f_w_gu[layer].rearrange("(k p) n -> p k n", p=P)
                down = f_w_down[layer].rearrange("(k p) n -> k p n", p=P)
                with sp.Fori(0, N_FFN) as i:
                    for c in range(2):
                        load(phase, i, 2 * c, gu[:, :, bass.ds(i * (2 * P) + c * P, P)])
                        load(phase, i, 2 * c + 1, gu[:, :, bass.ds(i * (2 * P) + (D_FF + c * P), P)])
                    for c in range(2):
                        load(phase, i, 4 + c, down[bass.ds(i * 2 + c, 1)].rearrange("o p n -> (o p) n"))

            ffn(0, W_FFN0)

            b_in = b_w_in[0].rearrange("(k p) n -> p k n", p=P)
            with sp.Fori(0, NF // 4) as i:
                for u in range(4):
                    load(W_BV, i, u, b_in[:, :, bass.ds(i * (4 * P) + (INNER + u * P), P)])
            sp.wait_ge(bv_tr, 12 * (NF // 4))
            sp.dma_start(w_s_in[:, :, :], b_w_s[0].rearrange("g t s -> t g s")).then_inc(b_loaded, 16)
            for b in range(DEC_B):
                sp.dma_start(w_s_smp[b * DEC_S:(b + 1) * DEC_S, :, 0:DEC_S],
                             b_w_s[0, :, 0:DEC_S, 0:DEC_S].rearrange("g t s -> t g s")).then_inc(b_loaded, 16)
            sp.wait_ge(bw_copied, 2)

            def load_gain(q):
                if q >= 2:
                    sp.wait_ge(row_stored[q % 2], 16)
                sp.dma_start(row_buf[q % 2], b_g_v[0:1, q * RQ:(q + 1) * RQ].to_broadcast([P, RQ]))\
                    .then_inc(gv_loaded[q % 2], 16)

            def store_rows(q):
                sp.wait_ge(gv_done, q + 1)
                sp.dma_start(v_rows.rearrange("b l s f -> (b l s) f")[:, q * RQ:(q + 1) * RQ], row_buf[q % 2])\
                    .then_inc(row_stored[q % 2], 16)

            load_gain(0)
            load_gain(1)
            for q in range(4):
                store_rows(q)
                if q < 2:
                    load_gain(q + 2)
            sp.wait_ge(row_stored[0], 32)
            sp.dma_start(bias_b[:, :, :], b_b_s.unsqueeze(0).to_broadcast([P, 1, G_B, P])
                         .rearrange("p o g t -> p (o g) t")).then_inc(b_mixed, 16)
            with sp.Fori(0, NF // 4) as i:
                for u in range(4):
                    load(W_BU, i, u, b_in[:, :, bass.ds(i * (4 * P) + u * P, P)])
            b_out = b_w_out[0].rearrange("(a k p) n -> a p k n", a=2, p=P)
            with sp.Fori(0, KD // 2) as i:
                for u in range(4):
                    load(W_BO, i, u, b_out[u % 2][:, :, bass.ds(i * (2 * P) + (u // 2) * P, P)])

            ffn(1, W_FFN1)

            for c in range(NT):
                sp.wait_ge(yt_act, c + 1)
                sp.wait_ge(yt_dve, c + 1)
                dst = y_prompt[0, c * P:(c + 1) * P, :] if c < NP else y_sample.rearrange("b s d -> (b s) d")
                sp.dma_start(dst, y_out[:, c, :]).then_inc(stored, 16)
            sp.wait_ge(c_stored, 16 * 5 * H)
            sp.wait_ge(stored, 16 * (2 + NT))

        @block.gpsimd
        def _(pool):
            n = 0

            def link(ins):
                nonlocal n
                n += 1
                ins.then_inc(pool_step, 1)
                pool.wait_ge(pool_step, n)

            nc.gpsimd.memset(w_raw[0][:, :, :], 0.0).then_inc(raw_clear, 1)
            link(nc.gpsimd.memset(ident[:, :], 0.0))
            link(nc.gpsimd.affine_select(out=ident[:, :], in_=ident[:, :], compare_op=ALU.not_equal, fill=1.0,
                                         base=0, pattern=[[-1, P]], channel_multiplier=1))
            nc.gpsimd.memset(eps_t[:, :], EPS)
            link(nc.gpsimd.memset(ones[:, :], 1.0))
            link(nc.gpsimd.affine_select(out=tri[:, :], in_=ones[:, :], compare_op=ALU.is_ge, fill=0.0,
                                         base=0, pattern=[[1, P]], channel_multiplier=-1))

            def by_stream(t):
                return t.rearrange("p (b s) -> p b s", b=DEC_B)

            for dst, src in ((tri_s, tri), (blk, ones)):
                link(nc.gpsimd.affine_select(out=by_stream(dst[:, :]), in_=by_stream(src[:, :]), compare_op=ALU.is_ge,
                                             fill=0.0, base=0, pattern=[[-DEC_S, DEC_B], [0, DEC_S]],
                                             channel_multiplier=1))
            link(nc.gpsimd.affine_select(out=by_stream(blk[:, :]), in_=by_stream(blk[:, :]), compare_op=ALU.is_ge,
                                         fill=0.0, base=DEC_S - 1, pattern=[[DEC_S, DEC_B], [0, DEC_S]],
                                         channel_multiplier=-1))
            link(nc.gpsimd.memset(blk_last[:, :], 0.0))
            link(nc.gpsimd.affine_select(out=by_stream(blk_last[:, :]), in_=by_stream(blk_last[:, :]),
                                         compare_op=ALU.not_equal, fill=1.0, base=-(DEC_S - 1),
                                         pattern=[[-DEC_S, DEC_B], [0, DEC_S]], channel_multiplier=1))
            link(nc.gpsimd.memset(last[:, :], 0.0))
            link(nc.gpsimd.affine_select(out=last[:, :], in_=last[:, :], compare_op=ALU.not_equal, fill=1.0,
                                         base=-(P - 1), pattern=[[0, P]], channel_multiplier=1))
            link(nc.gpsimd.memset(b_first[:, :], 0.0))
            link(nc.gpsimd.affine_select(out=b_first[:, :], in_=b_first[:, :], compare_op=ALU.not_equal, fill=1.0,
                                         base=0, pattern=[[-DEC_S, DEC_B]], channel_multiplier=1))
            link(nc.gpsimd.affine_select(out=b_mem[:, :], in_=ones[:, 0:DEC_B], compare_op=ALU.is_ge, fill=0.0,
                                         base=0, pattern=[[-DEC_S, DEC_B]], channel_multiplier=1))
            link(nc.gpsimd.affine_select(out=b_mem[:, :], in_=b_mem[:, :], compare_op=ALU.is_ge, fill=0.0,
                                         base=DEC_S - 1, pattern=[[DEC_S, DEC_B]], channel_multiplier=-1))
            link(nc.gpsimd.memset(reset[:, :], BIG))
            for h in range(H):
                link(nc.gpsimd.affine_select(out=by_stream(reset[:, :]), in_=by_stream(reset[:, :]),
                                             compare_op=ALU.not_equal, fill=-BIG, base=-1000 * (NT * h + NP),
                                             pattern=[[0, DEC_B], [1, DEC_S]], channel_multiplier=1000))
            link(nc.gpsimd.memset(dmat[:, :, :], 0.0))
            nc.gpsimd.drain().then_inc(const_ok, 1)

            def split_unit(phase, i, u):
                r, s = phase.raw(u), phase.slots[u]
                pool.wait_ge(used, phase.count(i, u, 1 + FREE_UNITS - phase.back[u]))
                pool.wait_ge(raw_loaded[r], phase.loads(i, u) * 16)
                nc.gpsimd.tensor_tensor(w_hi[s][:, :, :], w_raw[r][:, :, :],
                                        ones[:, :].unsqueeze(1).to_broadcast([P, KD, P]), ALU.mult)\
                    .then_inc(hi_split, 1)
                pool.wait_ge(hi_split, phase.count(i, u, 1))
                nc.gpsimd.tensor_tensor(w_lo[s][:, :, :], w_raw[r][:, :, :], w_hi[s][:, :, :].bitcast(F32),
                                        ALU.subtract).then_inc(split, 1)

            split_unit(W_GATES, 0, 0)
            with pool.Fori(0, H) as h:
                for u in range(8):
                    split_unit(W_HEADS, h, u)
            with pool.Fori(0, N_FFN) as i:
                for u in range(6):
                    split_unit(W_FFN0, i, u)
            with pool.Fori(0, NF // 4) as i:
                for u in range(4):
                    split_unit(W_BV, i, u)
            with pool.Fori(0, NF // 4) as i:
                for u in range(4):
                    split_unit(W_BU, i, u)
            with pool.Fori(0, KD // 2) as i:
                for u in range(4):
                    split_unit(W_BO, i, u)
            with pool.Fori(0, N_FFN) as i:
                for u in range(6):
                    split_unit(W_FFN1, i, u)

        @block.tensor
        def _(pe):
            for _ in range(FREE_UNITS - 1):
                pe.drain().then_inc(used, 1)

            def passes(out, slot, blocks, hi, lo, first, last_one, frees=False):
                n, total = 0, 3 * len(blocks)
                for k in blocks:
                    for w, x in ((w_hi, hi), (w_hi, lo), (w_lo, hi)):
                        ins = pe.matmul(out, w[slot][:, k, :], x(k), start=(first and n == 0),
                                        stop=(last_one and n == total - 1))
                        if n == 0 and frees:
                            ins.then_inc(used, 1)
                        n += 1
                return ins

            def xn(g):
                return (lambda k: tok(xn_hi[:, k, :], g)), (lambda k: tok(xn_lo[:, k, :], g))

            def unit_piece(phase, u, g, b):
                hi, lo = xn(g)
                return passes(bank(b), phase.slots[u], range(KD), hi, lo, True, True, g == 0)

            def norm(n):
                for g in range(NG):
                    pe.wait_ge(summed, 3 * n + g + 1)
                    pe.matmul(bank(6 + g % 2), ones[:, :], (ssum_a if n == 0 else ssum_f)[:, :],
                              start=True, stop=True).then_inc(mean_sq, 1)

            def xn_ready(n, g):
                pe.wait_ge(n_lo, KD * (NG * n + g + 1))

            pe.wait_ge(const_ok, 1)
            for c in range(NT):
                if c % TPG == 0:
                    pe.wait_ge(x_loaded[c // TPG], 16 * TPG)
                for half in range(2):
                    t = 2 * c + half
                    if t >= 8:
                        pe.wait_ge(xt_act if half else xt_dve, (t - 8) // 2 + 1)
                    for k in range(4):
                        ins = pe.transpose(ps[t % 8][:, k * P:(k + 1) * P],
                                           x_in[:, c, (4 * half + k) * P:(4 * half + k + 1) * P], ident[:, :])
                    ins.then_inc(xt_pe, 1)
            pe.wait_ge(rows_loaded, 16 * 5)
            pe.wait_ge(xt_dve, 6)
            pe.transpose(ps[2][:, 0:G_ALL], gain_rows[:, :], ident[0:G_ALL, 0:G_ALL]).then_inc(xt_pe, 1)
            pe.wait_ge(xt_dve, NT + 1)
            pe.wait_ge(xt_act, NT)
            norm(0)

            pe.wait_ge(split, 1)
            for g in range(NG):
                xn_ready(0, g)
                ins = unit_piece(W_GATES, 0, g, g)
                ins.then_inc(gt_mm, 1)
            pe.wait_ge(gt_scaled, 1)
            for c in range(NT):
                ins = pe.transpose(ps[3][:, c * 8:(c + 1) * 8], gT[0:2 * H, c * P:(c + 1) * P],
                                   ident[0:2 * H, 0:2 * H])
            ins.then_inc(gt_tr, 1)
            lf = small[:, 0, :, :]
            pe.wait_ge(gate_dve, 1)
            for col, whole, own in ((0, tri, tri_s), (64, ones, blk)):
                for c0, c1, m in ((0, NP, whole), (NP, NT, own)):
                    ins = pe.matmul(ps[4][:, col:col + H * NT].rearrange("p (h c) -> p h c", h=H)[:, :, c0:c1],
                                    m[:, :], lf[:, :, c0:c1], start=True, stop=True)
            ins.then_inc(gate_pe, 1)
            pe.wait_ge(gate_dve, 2)
            pe.transpose(ps[5][0:H * NT, 0:P], small[:, 2, :, :].rearrange("p h c -> p (h c)"), ident[:, :])\
                .then_inc(gate_pe, 1)
            pe.wait_ge(gate_dve, 3)
            pe.transpose(ps[6][:, 0:H * NT], aT[0:H * NT, P:2 * P], ident[0:H * NT, 0:H * NT]).then_inc(gate_pe, 1)
            pe.wait_ge(gate_dve, 4)
            cm = small[:, 3, :, :]
            for c0, c1, m in ((0, NP, last), (NP, NT, blk_last)):
                ins = pe.matmul(ps[7][:, 0:H * NT].rearrange("p (h c) -> p h c", h=H)[:, :, c0:c1],
                                m[:, :], cm[:, :, c0:c1], start=True, stop=True)
            ins.then_inc(gate_pe, 1)
            pe.wait_ge(gate_dve, 5)
            pe.matmul(ps[3][:, 128:128 + H * DEC_B], ones[:, :], dmat[:, 0, 0:H * DEC_B], start=True, stop=True)
            pe.matmul(ps[3][0:DEC_B, 192:192 + H], b_first[:, :], pack[:, :, Q_DECAY, NP], start=True, stop=True)\
                .then_inc(gate_pe, 1)
            pe.wait_ge(gate_dve, 6)

            with pe.Fori(0, H) as h:
                hi, lo = xn(0)
                for u in range(6):
                    pe.wait_ge(split, W_HEADS.count(h, u, 1))
                    for g in range(NG):
                        if u < 2:
                            pe.wait_ge(wd_add, h * 24)
                        elif u in (2, 3):
                            pe.wait_ge(a_evac, h * 6 + 3 * (u - 2) + g + 1)
                        elif u in (4, 5):
                            pe.wait_ge(a_vtmp, h * 6 + 3 * (u - 4) + g + 1)
                        ins = unit_piece(W_HEADS, u, g, 3 * (u % 2) + g)
                        ins.then_inc(a_mm, 1)
                        n = 3 * u + g - 1 - 3
                        if 0 <= n < 9:
                            turn = n
                            if n < 3:
                                pe.wait_ge(a_evac, h * 6 + 3 + n + 1)
                                src = tok(kT[:, :], n)
                            else:
                                pe.wait_ge(a_vtmp, h * 6 + (n - 3) + 1)
                                src = v_tmp[:, (n % 2) * TG:(n % 2 + 1) * TG]
                            if turn >= 2:
                                back = turn - 2
                                if back < 3:
                                    pe.wait_ge(a_ktok, h * 3 + back + 1)
                                else:
                                    pe.wait_ge(a_vtok, h * 6 + back - 3 + 1)
                            for c in range(TPG):
                                ins = pe.transpose(bank(6 + turn % 2)[:, c * P:(c + 1) * P],
                                                   src[:, c * P:(c + 1) * P], ident[:, :])
                            ins.then_inc(a_tr, 1)

                def wait_bank(t):
                    if t >= 8:
                        if TICKETS[t - 8] in BY_ACT:
                            pe.wait_ge(t_act, h * N_ACT + taken(t - 8))
                        else:
                            pe.wait_ge(t_dve, h * N_DVE + taken(t - 8))
                    elif t < 6:
                        pe.wait_ge(a_sig, h * 6 + t + 1)
                    else:
                        pe.wait_ge(a_vtok, h * 6 + 6)

                for name, src in (("mb", diag), ("wib", diag2)):
                    pe.wait_ge(a_diag, h * 2 + (1 if name == "mb" else 2))
                    for g in range(NG):
                        t = ticket(name, g)
                        wait_bank(t)
                        pe.matmul(bank(t), ones[:, :], src[:, g * TPG:(g + 1) * TPG, :], start=True, stop=True)\
                            .then_inc(t_pe, 1)
                for g in range(NG):
                    t = ticket("s", g)
                    wait_bank(t)
                    for c in range(g * TPG, (g + 1) * TPG):
                        ins = pe.matmul(bank(t)[:, (c % TPG) * P:(c % TPG + 1) * P], kT[:, c * P:(c + 1) * P],
                                        qT[:, c * P:(c + 1) * P], start=True, stop=True)
                    ins.then_inc(t_pe, 1)
                pe.wait_ge(c_loaded, h * 32 + 32)
                pe.wait_ge(n_loaded, h * 16 + 16)
                wait_bank(ticket("nt"))
                for k in range(4):
                    t = ticket("ctr", k)
                    wait_bank(t)
                    for b in range(2):
                        for j in range(2):
                            ins = pe.transpose(ps[t % 8][:, (2 * b + j) * P:(2 * b + j + 1) * P],
                                               c_nat[:, j, 2 * k + b, :], ident[:, :])
                    ins.then_inc(t_pe, 1)
                t = ticket("nt")
                pe.transpose(ps[t % 8][:, 0:DEC_B], n_nat[:, :], ident[0:DEC_B, 0:DEC_B]).then_inc(t_pe, 1)
                for c in range(NP):
                    t = ticket("u", c)
                    wait_bank(t)
                    pe.matmul(bank(t, DV + 1), k_tok[:, c, :], v_tok[:, c, :], start=True, stop=True)\
                        .then_inc(t_pe, 1)
                t = ticket("cfin")
                wait_bank(t)
                pe.wait_ge(t_dve, h * N_DVE + taken(ticket("u", NP - 1)))
                for j in range(2):
                    ins = pe.transpose(ps[t % 8][:, j * P:(j + 1) * P], state[:, NP, j * P:(j + 1) * P], ident[:, :])
                ins.then_inc(t_pe, 1)
                pe.wait_ge(a_kb, h + 1)
                for j in range(2):
                    for half in range(2):
                        t = ticket("us", 2 * j + half)
                        wait_bank(t)
                        pe.matmul(ps[t % 8][:, :], v_tok[:, NP, j * P:(j + 1) * P],
                                  k_blk[:, 4 * half:4 * half + 4, :], start=True, stop=True).then_inc(t_pe, 1)
                t = ticket("un")
                wait_bank(t)
                pe.matmul(ps[t % 8][0:DEC_B, 0:DK], b_mem[:, :], k_tok[:, NP, :], start=True, stop=True)\
                    .then_inc(t_pe, 1)
                for c in range(NT):
                    t = ticket("pv", c)
                    wait_bank(t)
                    if c == NP:
                        pe.wait_ge(a_dve, h * 2 + 2)
                    pe.matmul(bank(t, DV + 1), dmat[:, c, :], v_tok[:, c, :], start=True, stop=False)
                    if c < NP:
                        ins = pe.matmul(bank(t, DV + 1), qw[:, c * P:(c + 1) * P], state[:, c, :],
                                        start=False, stop=True)
                    else:
                        for b in range(DEC_B):
                            ins = pe.matmul(bank(t, DV + 1), q_blk[:, b, :], c_smp[:, b, :],
                                            start=False, stop=(b == DEC_B - 1))
                    ins.then_inc(t_pe, 1)
                pe.wait_ge(a_fac, h + 1)
                for g in range(NG):
                    for j in range(2):
                        t = ticket("ht", 2 * g + j)
                        wait_bank(t)
                        for c in range(TPG):
                            ins = pe.transpose(bank(t)[:, c * P:(c + 1) * P],
                                               num[:, g * TPG + c, j * P:(j + 1) * P], ident[:, :])
                        ins.then_inc(t_pe, 1)
                pe.wait_ge(split, W_HEADS.count(h, 7, 1))
                for g in range(NG):
                    pe.wait_ge(a_hlo, h * 6 + 2 * g + 2)
                    for j in range(KD):
                        n = KD * g + j
                        if n < 6:
                            pe.wait_ge(t_dve, h * N_DVE + N_DVE)
                        else:
                            pe.wait_ge(wd_add, h * 24 + n - 6 + 1)
                        for a in range(2):
                            ins = passes(bank(n % 6), W_HEADS.slots[6 + a], [j], lambda k: tok(h_hi[:, a, :], g),
                                         lambda k: tok(h_lo[:, a, :], g), a == 0, a == 1,
                                         n == (0, NG * KD - 1)[a])
                        ins.then_inc(wd_mm, 1)

            def ffn(layer, phase, n):
                norm(n)
                gm, um, gs, hf, hl, dm, da = (x[layer] for x in (g_mm, u_mm, g_silu, h_full, h_los, d_mm, d_add))
                for g in range(NG):
                    xn_ready(n, g)
                with pe.Fori(0, N_FFN) as i:
                    for c in range(2):
                        pe.wait_ge(split, phase.count(i, 2 * c, 1))
                        for g in range(NG):
                            if c == 0:
                                pe.wait_ge(da, i * 24 + g + 1)
                            else:
                                pe.wait_ge(gs, i * 6 + g + 1)
                            ins = unit_piece(phase, 2 * c, g, g)
                            ins.then_inc(gm, 1)
                        pe.wait_ge(split, phase.count(i, 2 * c + 1, 1))
                        for g in range(NG):
                            if c == 0:
                                pe.wait_ge(da, i * 24 + 3 + g + 1)
                            else:
                                pe.wait_ge(hf, i * 6 + g + 1)
                            ins = unit_piece(phase, 2 * c + 1, g, 3 + g)
                            ins.then_inc(um, 1)
                    pe.wait_ge(split, phase.count(i, 5, 1))
                    for g in range(NG):
                        pe.wait_ge(hl, i * 6 + 3 + g + 1)
                        for j in range(KD):
                            m = KD * g + j
                            if m < 3:
                                pe.wait_ge(gs, i * 6 + 3 + m + 1)
                            elif m < 6:
                                pe.wait_ge(hf, i * 6 + m + 1)
                            else:
                                pe.wait_ge(da, i * 24 + m + 1)
                            for a in range(2):
                                ins = passes(bank(m % 6), phase.slots[4 + a], [j], lambda k: tok(hg_hi[:, a, :], g),
                                             lambda k: tok(hg_lo[:, a, :], g), a == 0, a == 1,
                                             m == (0, NG * KD - 1)[a])
                            ins.then_inc(dm, 1)

            ffn(0, W_FFN0, 1)

            norm(2)
            for g in range(NG):
                xn_ready(2, g)
            with pe.Fori(0, NF // 4) as i:
                for u in range(4):
                    pe.wait_ge(split, W_BV.count(i, u, 1))
                    for g in range(NG + (u == 3)):
                        n = 3 * u + g
                        if n < 12:
                            if n < 6:
                                pe.wait_ge(bv_gelu, i * 12)
                            else:
                                pe.wait_ge(bv_gelu, i * 12 + n - 6 + 1)
                            ins = unit_piece(W_BV, u, g, n % 6)
                            ins.then_inc(bv_mm, 1)
                        if n >= 1:
                            m = n - 1
                            pe.wait_ge(bv_gelu, i * 12 + m + 1)
                            if m >= 2:
                                pe.wait_ge(bv_tok, i * 12 + m - 2 + 1)
                            else:
                                pe.wait_ge(bv_tok, i * 12)
                            for c in range(TPG):
                                ins = pe.transpose(bank(6 + m % 2)[:, c * P:(c + 1) * P],
                                                   t_b[:, m % 2, c * P:(c + 1) * P], ident[:, :])
                            ins.then_inc(bv_tr, 1)
            pe.wait_ge(b_loaded, 16 * (1 + DEC_B))
            pe.wait_ge(bv_gelu, 12 * (NF // 4))
            pe.wait_ge(bw_copied, 1)
            for a, src in enumerate((w_s_in, w_s_smp)):
                for g in range(G_B):
                    ins = pe.transpose(ps[a][:, g * P:(g + 1) * P], src[:, g, :], ident[:, :])
                ins.then_inc(bw_tr, 1)
            pe.wait_ge(mix_ok, 1)
            pe.wait_ge(bv_tok, 12 * (NF // 4))
            for c in range(NT):
                pe.wait_ge(ln_done, c + 1)
                for q in range(4):
                    t = 4 * c + q
                    if t >= 8:
                        pe.wait_ge(mx_act if t % 2 else mx_dve, (t - 8) // 2 + 1)
                    for k in range(FPG):
                        f = FPG * q + k
                        ins = pe.matmul(ps[t % 8][:, k * P:(k + 1) * P], vs[:, c, f, :], mix[:, c // NP, q, :],
                                        start=True, stop=True)
                    ins.then_inc(mx_mm, 1)
            pe.wait_ge(mx_act, 2 * NT)
            pe.wait_ge(mx_dve, 2 * NT)
            with pe.Fori(0, NF // 4) as i:
                for u in range(4):
                    pe.wait_ge(split, W_BU.count(i, u, 1))
                    for g in range(NG):
                        n = 3 * u + g
                        pe.wait_ge(bu_gate, i * 12 + n + 1)
                        ins = unit_piece(W_BU, u, g, n % 6)
                        ins.then_inc(bu_mm, 1)
            pe.wait_ge(ps_in, NG * FPG)
            with pe.Fori(0, KD // 2) as i:
                for u in range(4):
                    j, a = u // 2, u % 2
                    pe.wait_ge(split, W_BO.count(i, u, 1))
                    for g in range(NG):
                        if a == 0:
                            pe.wait_ge(bo_add, i * 6 + 3 * j + g + 1)
                        ins = passes(bank(3 * j + g), W_BO.slots[u], range(KD),
                                     lambda k: p_hi[:, TPG * g:TPG * (g + 1), KD * a + k, :],
                                     lambda k: tok(p_lo[:, KD * a + k, :], g), a == 0, a == 1, g == 0)
                        if a == 1:
                            ins.then_inc(bo_mm, 1)

            ffn(1, W_FFN1, 3)

            norm(4)
            pe.wait_ge(n_full, NG * KD * 5)
            for c in range(NT):
                for half in range(2):
                    t = 2 * c + half
                    if t >= 8:
                        pe.wait_ge(yt_act if half else yt_dve, (t - 8) // 2 + 1)
                    for k in range(4):
                        ins = pe.transpose(ps[t % 8][:, k * P:(k + 1) * P],
                                           xT[:, 4 * half + k, c * P:(c + 1) * P], ident[:, :])
                    ins.then_inc(yt_pe, 1)

        @block.scalar
        def _(act):
            def norm(n):
                for g in range(NG):
                    sq = sq_a if n == 0 else sq_f
                    std = rstd_a if n == 0 else rstd_f
                    if g:
                        act.wait_ge(n_lo if n < 4 else n_full, KD * (NG * n + g))
                    act.activation(sq[:, :, :], tok(xT[:, :, :], g), ACT.Square).then_inc(squared, 1)
                    act.wait_ge(mean_sq, NG * n + g + 1)
                    act.activation(std[:, :], bank(6 + g % 2), ACT.Sqrt, bias=eps_t[:, :], scale=1.0 / D)\
                        .then_inc(rooted, 1)
                    if n < 4:
                        for k in range(KD):
                            act.wait_ge(n_full, KD * (NG * n + g) + k + 1)
                            act.activation(tok(xn_hi[:, k, :], g), sq[:, k, :], ACT.Copy).then_inc(n_hi, 1)

            for c in range(NT):
                act.wait_ge(xt_pe, 2 * c + 2)
                act.activation(xT[:, 4:8, c * P:(c + 1) * P],
                               ps[(2 * c + 1) % 8][:, :].rearrange("p (k t) -> p k t", k=4), ACT.Copy)\
                    .then_inc(xt_act, 1)
            act.wait_ge(const_ok, 1)
            act.wait_ge(xt_dve, NT + 1)
            act.wait_ge(xt_act, NT)
            norm(0)
            for g in range(NG):
                act.wait_ge(gt_mm, g + 1)
                if g == 0:
                    act.wait_ge(small_loaded, 32)
                    act.activation(g_bias[:, :], g_bias[:, :], ACT.Copy, scale=1.0 / CAP).then_inc(act_step, 1)
                    act.wait_ge(act_step, 1)
                act.activation(tok(gT[0:2 * H, :], g), bank(g)[0:2 * H, :], ACT.Tanh, bias=g_bias[:, :],
                               scale=1.0 / CAP).then_inc(gt_act, 1)
            act.wait_ge(gt_scaled, 2)
            act.activation(small[:, 1, :, :], small[:, 1, :, :], ACT.Exp, scale=-1.0).then_inc(act_step, 1)
            act.wait_ge(act_step, 2)
            act.activation(small[:, 1, :, :], small[:, 1, :, :], ACT.Ln, bias=ones[:, 0:1]).then_inc(gate_act, 1)
            act.wait_ge(gt_scaled, 3)
            act.activation(pack[:, :, Q_WI:NQ, :], pack[:, :, Q_WI:NQ, :], ACT.Exp).then_inc(gate_act, 1)
            act.wait_ge(gate_act, 2)

            with act.Fori(0, H) as h:
                for g in range(NG):
                    act.wait_ge(a_mm, h * 18 + g + 1)
                    act.activation(tok(qT[:, :], g), bank(g), ACT.Copy, scale=float(DK) ** -0.5).then_inc(a_evac, 1)
                for g in range(NG):
                    act.wait_ge(a_mm, h * 18 + 3 + g + 1)
                    act.activation(tok(kT[:, :], g), bank(3 + g), ACT.Copy).then_inc(a_evac, 1)
                for n in range(6):
                    act.wait_ge(a_tr, h * 9 + 3 + n + 1)
                    g, j = n % 3, n // 3
                    act.activation(v_tok[:, g * TPG:(g + 1) * TPG, j * P:(j + 1) * P], tiles(bank(6 + (3 + n) % 2)),
                                   ACT.Copy).then_inc(a_vtok, 1)
                for n in range(6):
                    g, j = n % 3, n // 3
                    act.wait_ge(a_mm, h * 18 + 12 + n + 1)
                    act.activation(tok(sig_o[:, j, :], g), bank(n), ACT.Sigmoid).then_inc(a_sig, 1)
                for g in range(NG):
                    act.wait_ge(a_dargs, h * 3 + g + 1)
                    act.activation(dmat[:, g * TPG:(g + 1) * TPG, :], dmat[:, g * TPG:(g + 1) * TPG, :], ACT.Exp)\
                        .then_inc(a_exp, 1)
                for k in range(4):
                    t = ticket("ctr", k)
                    act.wait_ge(t_pe, h * NTICK + t + 1)
                    act.activation(c_smp[:, 2 * k:2 * k + 2, 0:DV],
                                   ps[t % 8][:, :].rearrange("p (b v) -> p b v", b=2), ACT.Copy).then_inc(t_act, 1)
                t = ticket("nt")
                act.wait_ge(t_pe, h * NTICK + t + 1)
                act.activation(c_smp[:, :, DV], ps[t % 8][:, 0:DEC_B], ACT.Copy).then_inc(t_act, 1)
                t = ticket("cfin")
                act.wait_ge(t_dve, h * N_DVE + taken(ticket("u", NP - 1)))
                act.wait_ge(c_stored, h * 80)
                act.activation(c_out[:, 2, 0:1], state[:, NP, DV:DV + 1], ACT.Copy).then_inc(act_step, 1)
                act.wait_ge(t_pe, h * NTICK + t + 1)
                act.activation(c_out[:, 0:2, :], ps[t % 8][:, 0:DV].rearrange("p (j v) -> p j v", j=2), ACT.Copy)\
                    .then_inc(t_act, 1)
                for c in range(NT):
                    act.wait_ge(t_dve, h * N_DVE + taken(ticket("pv", c)))
                    act.activation(v_tok[:, c, 0:DV], num[:, c, 0:DV], ACT.Square, accum_out=nstat[:, 0, c:c + 1])\
                        .then_inc(a_ssq, 1)
                act.wait_ge(a_dve, h * 2 + 2)
                act.wait_ge(a_fac, h)
                act.wait_ge(a_sqrt, h * 2 + 1)
                act.activation(nstat[:, 3, :], nstat[:, 2, :], ACT.Sqrt, bias=eps_t[:, :], scale=1.0 / DV)\
                    .then_inc(a_sqrt, 1)

            def ffn(layer, n):
                norm(n)
                with act.Fori(0, N_FFN) as i:
                    for c in range(2):
                        for g in range(NG):
                            act.wait_ge(g_mm[layer], i * 6 + 3 * c + g + 1)
                            act.activation(silu[:, c, g, :], bank(g), ACT.Silu).then_inc(g_silu[layer], 1)

            act.wait_ge(wd_add, 24 * H)
            act.wait_ge(c_stored, 80 * H)
            ffn(0, 1)
            act.wait_ge(d_add[0], 6 + 24 * N_FFN)
            norm(2)
            with act.Fori(0, NF // 4) as i:
                for n in range(12):
                    act.wait_ge(bv_mm, i * 12 + n + 1)
                    if n >= 2:
                        act.wait_ge(bv_tr, i * 12 + n - 2 + 1)
                    else:
                        act.wait_ge(bv_tr, i * 12)
                    act.activation(t_b[:, n % 2, :], bank(n % 6), ACT.Gelu_apprx_tanh).then_inc(bv_gelu, 1)
            act.wait_ge(ln_stat, 1)
            act.activation(rs_v[:, :, 0], mv[:, :, 1], ACT.Sqrt, bias=eps_t[:, :]).then_inc(ln_root, 1)
            for c in range(NT):
                for q in range(4):
                    t = 4 * c + q
                    if t % 2:
                        act.wait_ge(mx_mm, 4 * c + 4)
                        if c == NP:
                            act.wait_ge(gv_done, 4)
                        act.activation(vs[:, c, FPG * q:FPG * (q + 1), :],
                                       ps[t % 8][:, :].rearrange("p (f t) -> p f t", f=FPG), ACT.Copy)\
                            .then_inc(mx_act, 1)
            with act.Fori(0, NF // 4) as i:
                for n in range(12):
                    act.wait_ge(bu_mm, i * 12 + n + 1)
                    act.activation(bank(n % 6), bank(n % 6), ACT.Gelu_apprx_tanh).then_inc(bu_gelu, 1)
            act.wait_ge(bu_gate, 6 + 12 * (NF // 4))

            def p_round(n):
                g, q = n // FPG, n % FPG
                for f in range(4 * q, 4 * q + 4):
                    ins = act.activation(tiles(tok(p_lo[:, f, :], g)), vs[:, g * TPG:(g + 1) * TPG, f, :], ACT.Copy)
                ins.then_inc(ps_hi, 1)

            p_round(0)
            for n in range(NG * FPG):
                if n + 1 < NG * FPG:
                    p_round(n + 1)
                act.wait_ge(ps_lo, n + 1)
                g, q = n // FPG, n % FPG
                for c in range(TPG * g, TPG * (g + 1)):
                    ins = act.activation(p_hi[:, c, 4 * q:4 * q + 4, :], vs[:, c, 4 * q:4 * q + 4, :], ACT.Copy)
                ins.then_inc(ps_in, 1)
            act.wait_ge(bo_add, 6 + NG * KD)
            ffn(1, 3)
            act.wait_ge(d_add[1], 6 + 24 * N_FFN)
            norm(4)
            for c in range(NT):
                act.wait_ge(yt_pe, 2 * c + 2)
                act.activation(y_out[:, c, D // 2:D], ps[(2 * c + 1) % 8][:, :], ACT.Copy).then_inc(yt_act, 1)

        @block.vector
        def _(dve):
            n_link = 0

            def link(ins):
                nonlocal n_link
                n_link += 1
                ins.then_inc(dve_step, 1)
                dve.wait_ge(dve_step, n_link)

            def norm(n, gain):
                sq = sq_a if n == 0 else sq_f
                ss = ssum_a if n == 0 else ssum_f
                std = rstd_a if n == 0 else rstd_f
                for g in range(NG):
                    dve.wait_ge(squared, NG * n + g + 1)
                    link(dve.tensor_tensor(sq[:, 0:4, :], sq[:, 0:4, :], sq[:, 4:8, :], ALU.add))
                    link(dve.tensor_tensor(sq[:, 0:2, :], sq[:, 0:2, :], sq[:, 2:4, :], ALU.add))
                    dve.tensor_tensor(ss[:, :], sq[:, 0, :], sq[:, 1, :], ALU.add).then_inc(summed, 1)
                    dve.wait_ge(rooted, NG * n + g + 1)
                    link(dve.reciprocal(std[:, :], std[:, :]))
                    for k in range(KD):
                        out = sq[:, k, :] if n < 4 else tok(xT[:, k, :], g)
                        dve.scalar_tensor_tensor(out, tok(xT[:, k, :], g), gains[:, gain + k:gain + k + 1], std[:, :],
                                                 ALU.mult, ALU.mult).then_inc(n_full, 1)
                        if n < 4 and k >= 1:
                            lo(n, g, k - 1)
                    if n < 4:
                        lo(n, g, KD - 1)

            def lo(n, g, k):
                sq = sq_a if n == 0 else sq_f
                dve.wait_ge(n_hi, KD * (NG * n + g) + k + 1)
                dve.tensor_tensor(tok(xn_lo[:, k, :], g), sq[:, k, :], tok(xn_hi[:, k, :], g).bitcast(F32),
                                  ALU.subtract).then_inc(n_lo, 1)

            for c in range(NT):
                dve.wait_ge(xt_pe, 2 * c + 1)
                dve.tensor_copy(xT[:, 0:4, c * P:(c + 1) * P],
                                ps[(2 * c) % 8][:, :].rearrange("p (k t) -> p k t", k=4)).then_inc(xt_dve, 1)
            dve.wait_ge(xt_pe, 2 * NT + 1)
            dve.tensor_copy(gains[:, :], ps[2][:, 0:G_ALL]).then_inc(xt_dve, 1)
            dve.wait_ge(xt_dve, NT + 1)
            norm(0, G_MIX)

            lf, tmp, a, cm = (small[:, k, :, :] for k in range(4))
            bt, mp, mt, mn = (small[:, k, :, :] for k in range(4, 8))
            dve.wait_ge(gt_act, NG)
            dve.tensor_scalar(gT[0:2 * H, :], gT[0:2 * H, :], CAP, None, ALU.mult).then_inc(gt_scaled, 1)
            dve.wait_ge(gt_tr, 1)
            link(dve.tensor_copy(gtok[:, :, :].rearrange("p c g -> p (c g)"), ps[3][:, 0:NT * 2 * H]))
            ig = gtok[:, :, 0:H].rearrange("p c h -> p h c")
            fg = gtok[:, :, H:2 * H].rearrange("p c h -> p h c")
            link(dve.tensor_scalar(lf, fg, -1.0, None, ALU.mult))
            dve.tensor_tensor(tmp, lf, fg, ALU.max).then_inc(gt_scaled, 1)
            dve.wait_ge(gate_act, 1)
            link(dve.tensor_scalar(lf, fg, 0.0, None, ALU.min))
            dve.tensor_tensor(lf, lf, tmp, ALU.subtract).then_inc(gate_dve, 1)
            dve.wait_ge(gate_pe, 1)
            link(dve.tensor_copy(bt, ps[4][:, 0:H * NT].rearrange("p (h c) -> p h c", h=H)))
            dve.tensor_tensor(a, ig, bt, ALU.subtract).then_inc(gate_dve, 1)
            dve.wait_ge(gate_pe, 2)
            link(dve.tensor_copy(aT[0:H * NT, 0:P], ps[5][0:H * NT, 0:P]))
            dve.tensor_tensor_scan(aT[0:H * NT, P:2 * P], reset[:, :], aT[0:H * NT, 0:P], -BIG, ALU.min, ALU.max)\
                .then_inc(gate_dve, 1)
            dve.wait_ge(gate_pe, 3)
            dve.tensor_copy(cm, ps[6][:, 0:H * NT].rearrange("p (h c) -> p h c", h=H)).then_inc(gate_dve, 1)
            dve.wait_ge(gate_pe, 4)
            bl, cml = tmp, lf
            link(dve.tensor_copy(bl, ps[4][:, 64:64 + H * NT].rearrange("p (h c) -> p h c", h=H)))
            link(dve.tensor_copy(cml, ps[7][:, 0:H * NT].rearrange("p (h c) -> p h c", h=H)))
            link(dve.memset(mp[:, :, 0:1], 0.0))
            link(dve.tensor_copy(mp[:, :, NP], m_in[:, :]))
            for hh in range(H):
                link(dve.tensor_tensor_scan(mn[:, hh, 0:NP], cml[:, hh, 0:NP], bl[:, hh, 0:NP], 0.0, ALU.max, ALU.add))
            link(dve.tensor_copy(mp[:, :, 1:NP], mn[:, :, 0:NP - 1]))
            ml = cml
            link(dve.tensor_tensor(ml, mp, cml, ALU.max))
            link(dve.tensor_tensor(mn[:, :, NP], ml[:, :, NP], bl[:, :, NP], ALU.add))
            link(dve.tensor_tensor(pack[:, :, Q_M, :], mp, cm, ALU.max))
            dve.tensor_copy(pack[:, :, Q_A, :], a)
            dve.tensor_copy(m_out[:, 0, :], mn[:, :, NP - 1])
            link(dve.tensor_copy(m_out[:, 1, :], mn[:, :, NP]))
            dve.tensor_tensor(pack[:, :, Q_WI, :], mp, pack[:, :, Q_M, :], ALU.subtract)
            link(dve.tensor_tensor(mt, bt, pack[:, :, Q_M, :], ALU.add))
            dve.tensor_scalar(pack[:, :, Q_EMT, :], mt, -1.0, None, ALU.mult)
            dve.tensor_tensor(pack[:, :, Q_WS, :], a, ml, ALU.subtract)
            dve.tensor_tensor(pack[:, :, Q_DECAY, :], mp, ml, ALU.subtract)
            dve.drain().then_inc(gt_scaled, 1)
            dve.wait_ge(gate_act, 2)
            dve.tensor_tensor(dmat[:, 0, 0:H * DEC_B].rearrange("p (h b) -> p h b", h=H),
                              b_first[:, :].unsqueeze(1).to_broadcast([P, H, DEC_B]),
                              pack[:, :, Q_DECAY, NP].unsqueeze(2).to_broadcast([P, H, DEC_B]), ALU.mult)\
                .then_inc(gate_dve, 1)
            dve.wait_ge(gate_pe, 5)
            dve.tensor_copy(dec_s[:, :, :].rearrange("p h b -> p (h b)"), ps[3][:, 128:128 + H * DEC_B])
            dve.tensor_copy(dec8[0:DEC_B, :], ps[3][0:DEC_B, 192:192 + H])
            dve.tensor_scalar(tri[:, :], tri[:, :], -BIG, BIG, ALU.mult, ALU.add)
            dve.tensor_scalar(tri_s[:, :], tri_s[:, :], -BIG, BIG, ALU.mult, ALU.add)
            link(dve.memset(v_tok[:, :, DV:DV + 1], 1.0))
            dve.drain().then_inc(gate_dve, 1)

            HS = 24
            base = n_link
            with dve.Fori(0, H) as h:
                step = 0

                def hlink(ins):
                    nonlocal step
                    step += 1
                    ins.then_inc(dve_step, 1)
                    dve.wait_ge(dve_step, h * HS + (base + step))

                hlink(dve.tensor_copy(cur[:, :, :].rearrange("p q c -> p (q c)"),
                                      pack[:, :, :, :].rearrange("p h q c -> p (h q c)")[:, bass.ds(h * (NQ * NT), NQ * NT)]))
                dve.tensor_copy(g_h[:, :], gains[:, bass.ds(h * 2 + G_OUT, 2)])
                dve.tensor_copy(nstat[:, 4, 0:DEC_B], dec_s[:, :, :].rearrange("p h b -> p (h b)")[:, bass.ds(h * DEC_B, DEC_B)])
                hlink(dve.tensor_copy(nstat[0:DEC_B, 5, 0:1], dec8[0:DEC_B, bass.ds(h, 1)]))

                def q(k):
                    return cur[:, k, :].unsqueeze(2)

                for n in range(3):
                    g = n
                    dve.wait_ge(a_tr, h * 9 + n + 1)
                    dve.tensor_tensor(k_tok[:, g * TPG:(g + 1) * TPG, :], tiles(bank(6 + n % 2)),
                                      q(Q_WS)[:, g * TPG:(g + 1) * TPG, :].to_broadcast([P, TPG, P]), ALU.mult)\
                        .then_inc(a_ktok, 1)
                    dve.wait_ge(a_mm, h * 18 + 6 + n + 1)
                    if n >= 2:
                        dve.wait_ge(a_tr, h * 9 + 3 + n - 2 + 1)
                    dve.tensor_copy(v_tmp[:, (n + 1) % 2 * TG:((n + 1) % 2 + 1) * TG], bank(n)).then_inc(a_vtmp, 1)
                for n in range(3, 6):
                    dve.wait_ge(a_mm, h * 18 + 6 + n + 1)
                    dve.wait_ge(a_tr, h * 9 + 3 + n - 2 + 1)
                    dve.tensor_copy(v_tmp[:, (n + 1) % 2 * TG:((n + 1) % 2 + 1) * TG], bank(n)).then_inc(a_vtmp, 1)
                dve.tensor_tensor(k_blk, k_tok[:, NP, :].unsqueeze(1).to_broadcast([P, DEC_B, DK]),
                                  b_mem[:, :].unsqueeze(2).to_broadcast([P, DEC_B, DK]), ALU.mult).then_inc(a_kb, 1)
                eye = ident[:, :].unsqueeze(1).to_broadcast([P, NT, P])
                dve.tensor_tensor(diag, eye, q(Q_M).to_broadcast([P, NT, P]), ALU.mult).then_inc(a_diag, 1)
                dve.tensor_tensor(diag2, eye, q(Q_WI).to_broadcast([P, NT, P]), ALU.mult).then_inc(a_diag, 1)
                dve.wait_ge(a_tr, h * 9 + 9)
                for g in range(NG):
                    t = ticket("mb", g)
                    dve.wait_ge(t_pe, h * NTICK + t + 1)
                    part = dmat[:, g * TPG:(g + 1) * TPG, :]
                    if g < NG - 1:
                        ins = dve.tensor_tensor(part, tri[:, :].unsqueeze(1).to_broadcast([P, TPG, P]), tiles(bank(t)),
                                                ALU.add)
                    else:
                        dve.tensor_tensor(part[:, 0:2, :], tri[:, :].unsqueeze(1).to_broadcast([P, 2, P]),
                                          tiles(bank(t))[:, 0:2, :], ALU.add)
                        ins = dve.tensor_tensor(part[:, 2, :], tri_s[:, :], tiles(bank(t))[:, 2, :], ALU.add)
                    ins.then_inc(t_dve, 1)
                    dve.wait_ge(t_dve, h * N_DVE + taken(t))
                    dve.tensor_tensor(part, q(Q_A)[:, g * TPG:(g + 1) * TPG, :].to_broadcast([P, TPG, P]), part,
                                      ALU.subtract).then_inc(a_dargs, 1)
                for g in range(NG):
                    t = ticket("wib", g)
                    dve.wait_ge(t_pe, h * NTICK + ticket("wib", NG - 1) + 1)
                    dve.tensor_tensor(tok(qw[:, :], g), tok(qT[:, :], g), bank(t), ALU.mult).then_inc(t_dve, 1)
                dve.wait_ge(t_dve, h * N_DVE + taken(ticket("wib", NG - 1)))
                for g in range(NG):
                    t = ticket("s", g)
                    dve.wait_ge(t_pe, h * NTICK + t + 1)
                    dve.wait_ge(a_exp, h * 3 + g + 1)
                    part = dmat[:, g * TPG:(g + 1) * TPG, :]
                    dve.tensor_tensor(part, part, tiles(bank(t)), ALU.mult).then_inc(t_dve, 1)
                hlink(dve.memset(state[:, 0, :], 0.0))
                for c in range(NP):
                    t = ticket("u", c)
                    dve.wait_ge(t_pe, h * NTICK + t + 1)
                    dve.scalar_tensor_tensor(state[:, c + 1, :], state[:, c, :], cur[:, Q_DECAY, c:c + 1],
                                             bank(t, DV + 1), ALU.mult, ALU.add).then_inc(t_dve, 1)
                    dve.wait_ge(t_dve, h * N_DVE + taken(t))
                for j in range(2):
                    for half in range(2):
                        t = ticket("us", 2 * j + half)
                        bs = slice(4 * half, 4 * half + 4)
                        dve.wait_ge(t_pe, h * NTICK + t + 1)
                        hlink(dve.tensor_tensor(c_nat[:, j, bs, :], c_nat[:, j, bs, :],
                                                nstat[:, 4, bs].unsqueeze(2).to_broadcast([P, 4, DK]), ALU.mult))
                        dve.tensor_tensor(c_nat[:, j, bs, :], c_nat[:, j, bs, :],
                                          ps[t % 8][:, :].rearrange("p (b d) -> p b d", b=4), ALU.add)\
                            .then_inc(t_dve, 1)
                t = ticket("un")
                dve.wait_ge(t_pe, h * NTICK + t + 1)
                dve.scalar_tensor_tensor(n_nat[:, :], n_nat[:, :], nstat[0:DEC_B, 5, 0:1], ps[t % 8][0:DEC_B, 0:DK],
                                         ALU.mult, ALU.add).then_inc(t_dve, 1)
                hlink(dve.memset(q_blk[:, :, :], 0.0))
                for b in range(DEC_B):
                    sl = slice(b * DEC_S, (b + 1) * DEC_S)
                    ins = dve.tensor_copy(q_blk[:, b, sl], qw[:, NP * P + b * DEC_S:NP * P + (b + 1) * DEC_S])
                ins.then_inc(a_dve, 1)
                dve.drain().then_inc(a_dve, 1)
                for c in range(NT):
                    t = ticket("pv", c)
                    dve.wait_ge(t_pe, h * NTICK + t + 1)
                    dve.tensor_copy(num[:, c, :], bank(t, DV + 1)).then_inc(t_dve, 1)
                dve.wait_ge(t_dve, h * N_DVE + taken(ticket("pv", NT - 1)))
                ssq, r, t2, std = (nstat[:, k, :] for k in range(4))
                den = num[:, :, DV]
                hlink(dve.tensor_scalar(r, den, -1.0, None, ALU.mult))
                hlink(dve.tensor_tensor(r, r, den, ALU.max))
                hlink(dve.tensor_tensor(r, r, cur[:, Q_EMT, :], ALU.max))
                hlink(dve.reciprocal(r, r))
                dve.wait_ge(a_ssq, h * NT + NT)
                hlink(dve.tensor_tensor(t2, ssq, r, ALU.mult))
                dve.tensor_tensor(t2, t2, r, ALU.mult).then_inc(a_sqrt, 1)
                dve.wait_ge(a_sqrt, h * 2 + 2)
                hlink(dve.reciprocal(std, std))
                hlink(dve.tensor_tensor(r, r, std, ALU.mult))
                dve.tensor_tensor(num[:, :, 0:DV], num[:, :, 0:DV], r.unsqueeze(2).to_broadcast([P, NT, DV]), ALU.mult)\
                    .then_inc(a_fac, 1)
                for g in range(NG):
                    for j in range(2):
                        t = ticket("ht", 2 * g + j)
                        buf = h_f[:, j * TG:(j + 1) * TG]
                        dve.wait_ge(t_pe, h * NTICK + t + 1)
                        dve.scalar_tensor_tensor(buf, bank(t), g_h[:, j:j + 1], tok(sig_o[:, j, :], g),
                                                 ALU.mult, ALU.mult).then_inc(t_dve, 1)
                        dve.wait_ge(t_dve, h * N_DVE + taken(t))
                        hlink(dve.tensor_copy(tok(h_hi[:, j, :], g), buf))
                        dve.tensor_tensor(tok(h_lo[:, j, :], g), buf, tok(h_hi[:, j, :], g).bitcast(F32),
                                          ALU.subtract).then_inc(a_hlo, 1)
                for n in range(24):
                    g, j = n // KD, n % KD
                    dve.wait_ge(wd_mm, h * 24 + n + 1)
                    dve.tensor_tensor(tok(xT[:, j, :], g), tok(xT[:, j, :], g), bank(n % 6), ALU.add).then_inc(wd_add, 1)
                while step < HS:
                    hlink(dve.memset(nstat[:, 2, 0:1], 0.0))
                assert step == HS, step
            n_link = base + HS * H

            def ffn(layer, n):
                norm(n, G_FFN + KD * layer)
                for _ in range(6):
                    dve.drain().then_inc(d_add[layer], 1)
                with dve.Fori(0, N_FFN) as i:
                    for c in range(2):
                        for g in range(NG):
                            m = 3 * c + g
                            buf = h_tmp[:, m % 2, :]
                            dve.wait_ge(u_mm[layer], i * 6 + m + 1)
                            dve.wait_ge(g_silu[layer], i * 6 + m + 1)
                            dve.tensor_tensor(buf, silu[:, c, g, :], bank(3 + g), ALU.mult).then_inc(h_full[layer], 1)
                            dve.wait_ge(h_full[layer], i * 6 + m + 1)
                            dve.tensor_copy(tok(hg_hi[:, c, :], g), buf).then_inc(h_his[layer], 1)
                            dve.wait_ge(h_his[layer], i * 6 + m + 1)
                            dve.tensor_tensor(tok(hg_lo[:, c, :], g), buf, tok(hg_hi[:, c, :], g).bitcast(F32),
                                              ALU.subtract).then_inc(h_los[layer], 1)
                    for m in range(24):
                        g, j = m // KD, m % KD
                        dve.wait_ge(d_mm[layer], i * 24 + m + 1)
                        dve.tensor_tensor(tok(xT[:, j, :], g), tok(xT[:, j, :], g), bank(m % 6), ALU.add)\
                            .then_inc(d_add[layer], 1)

            ffn(0, 1)
            norm(2, G_MIX + KD)
            with dve.Fori(0, NF // 4) as i:
                for n in range(12):
                    u, g = n // 3, n % 3
                    dve.wait_ge(bv_tr, i * 12 + n + 1)
                    dve.tensor_copy(vs[:, g * TPG:(g + 1) * TPG, bass.ds(i * 4 + u, 1), :].rearrange("p c o t -> p c (o t)"),
                                    tiles(bank(6 + n % 2))).then_inc(bv_tok, 1)
            dve.wait_ge(bv_tok, 12 * (NF // 4))
            vrow = vs[:, :, :, :].rearrange("p c f t -> p c (f t)")
            for c in range(NT):
                for q4 in range(4):
                    ins = dve.bn_stats(stat[:, c, q4, :], vrow[:, c, q4 * 512:(q4 + 1) * 512])
            link(ins)
            for c in range(NT):
                ins = dve.bn_aggr(mv[:, c, :], stat[:, c, :, :].rearrange("p q s -> p (q s)"))
            ins.then_inc(ln_stat, 1)
            dve.wait_ge(ln_root, 1)
            link(dve.reciprocal(rs_v[:, :, 1], rs_v[:, :, 0]))
            for c in range(NT):
                dve.tensor_scalar(vrow[:, c, :], vrow[:, c, :], mv[:, c, 0:1], rs_v[:, c, 1:2], ALU.subtract, ALU.mult)\
                    .then_inc(ln_done, 1)
            dve.wait_ge(b_loaded, 16 * (1 + DEC_B))
            dve.wait_ge(ln_done, NT)
            dve.tensor_copy(mix[:, 0, :, 0:DEC_S], w_s_smp[:, :, 0:DEC_S])
            dve.drain().then_inc(dve_step, 1)
            n_link += 1
            dve.wait_ge(dve_step, n_link)
            for b in range(DEC_B):
                ins = dve.tensor_copy(w_s_smp[:, :, b * DEC_S:(b + 1) * DEC_S], mix[:, 0, :, 0:DEC_S])
            ins.then_inc(bw_copied, 1)
            for t_ in (tri, tri_s):
                link(dve.tensor_scalar(t_[:, :], t_[:, :], 0.0, None, ALU.is_equal))
            for k, t_ in enumerate((tri, tri_s)):
                dve.wait_ge(bw_tr, k + 1)
                ins = dve.tensor_tensor(mix[:, k, :, :], ps[k][:, :].rearrange("p (g t) -> p g t", g=G_B),
                                        t_[:, :].unsqueeze(1).to_broadcast([P, G_B, P]), ALU.mult)
                link(ins)
            dve.drain().then_inc(bw_copied, 1)
            dve.drain().then_inc(mix_ok, 1)
            for c in range(NT):
                if c == NP:
                    for q in range(4):
                        dve.wait_ge(gv_loaded[q % 2], 16 * (q // 2 + 1))
                        dve.tensor_tensor(row_buf[q % 2], vrow[:, NP, q * RQ:(q + 1) * RQ], row_buf[q % 2], ALU.mult)\
                            .then_inc(gv_done, 1)
                    dve.wait_ge(gv_done, 4)
                for q4 in range(0, 4, 2):
                    t = 4 * c + q4
                    dve.wait_ge(mx_mm, 4 * c + 4)
                    dve.tensor_copy(vs[:, c, FPG * q4:FPG * (q4 + 1), :],
                                    ps[t % 8][:, :].rearrange("p (f t) -> p f t", f=FPG)).then_inc(mx_dve, 1)
            dve.wait_ge(b_mixed, 16)
            dve.wait_ge(mx_act, 2 * NT)
            dve.wait_ge(row_stored[1], 32)
            for _ in range(6):
                dve.drain().then_inc(bu_gate, 1)
            with dve.Fori(0, NF // 4) as i:
                for n in range(12):
                    u, g = n // 3, n % 3
                    piece = vs[:, g * TPG:(g + 1) * TPG, bass.ds(i * 4 + u, 1), :].rearrange("p c o t -> p c (o t)")
                    buf = t_b[:, n % 2, :]
                    gain = gains[:, bass.ds(i * 4 + (G_V + u), 1)]
                    pr = bias_b[:, bass.ds(i, 1), :]
                    sm = pr[:, :, 0:DEC_S].to_broadcast([P, DEC_B, DEC_S])
                    if g < NG - 1:
                        ins = dve.scalar_tensor_tensor(tiles(buf), piece, gain, pr.to_broadcast([P, TPG, P]),
                                                       ALU.mult, ALU.add)
                    else:
                        dve.scalar_tensor_tensor(tiles(buf)[:, 0:2, :], piece[:, 0:2, :], gain,
                                                 pr.to_broadcast([P, 2, P]), ALU.mult, ALU.add)
                        ins = dve.scalar_tensor_tensor(
                            tiles(buf)[:, 2, :].rearrange("p (b s) -> p b s", b=DEC_B),
                            piece[:, 2, :].rearrange("p (b s) -> p b s", b=DEC_B), gain, sm, ALU.mult, ALU.add)
                    ins.then_inc(bu_bias, 1)
                    dve.wait_ge(bu_bias, i * 12 + n + 1)
                    dve.wait_ge(bu_gelu, i * 12 + n + 1)
                    dve.tensor_tensor(piece, tiles(buf), tiles(bank(n % 6)), ALU.mult).then_inc(bu_gate, 1)
            for g in range(NG):
                for q4 in range(FPG):
                    dve.wait_ge(ps_hi, FPG * g + q4 + 1)
                    for f in range(4 * q4, 4 * q4 + 4):
                        part = tiles(tok(p_lo[:, f, :], g))
                        ins = dve.tensor_tensor(part, vs[:, g * TPG:(g + 1) * TPG, f, :], part.bitcast(F32),
                                                ALU.subtract)
                    ins.then_inc(ps_lo, 1)
            for _ in range(6):
                dve.drain().then_inc(bo_add, 1)
            with dve.Fori(0, KD // 2) as i:
                for n in range(6):
                    j, g = n // 3, n % 3
                    dve.wait_ge(bo_mm, i * 6 + n + 1)
                    out = tok(xT[:, :, :], g)[:, bass.ds(i * 2 + j, 1), :].rearrange("p o t -> p (o t)")
                    dve.tensor_tensor(out, out, bank(n), ALU.add).then_inc(bo_add, 1)

            ffn(1, 3)
            norm(4, G_FINAL)
            for c in range(NT):
                dve.wait_ge(yt_pe, 2 * c + 1)
                dve.tensor_copy(y_out[:, c, 0:D // 2], ps[(2 * c) % 8][:, :]).then_inc(yt_dve, 1)


_INS = ['x_prompt', 'x_sample', 'state_C', 'state_n', 'state_m', 'g_mix', 'g_ffn', 'g_final',
        'a_w_in', 'a_b_gate', 'a_g_out', 'a_w_out', 'b_w_in', 'b_g_v', 'b_w_s', 'b_b_s', 'b_w_out',
        'f_w_gu', 'f_w_down']
_OUTS = [(1, SEQ, D), (DEC_B, DEC_S, D), (1, 1, H, DV, DK), (1, 1, H, DK), (1, 1, H),
         (DEC_B, 1, H, DV, DK), (DEC_B, 1, H, DK), (DEC_B, 1, H), (DEC_B, 1, DEC_S, INNER)]


def kernel(**inputs):
    import numpy as _np
    import concourse.bacc as _bacc
    from concourse.bass_utils import run_bass_kernel_spmd as _run

    nc = _bacc.Bacc("TRN2", target_bir_lowering=False, num_devices=1, dynamic_dma_scratch_size=64)
    arrays, args = {}, []
    for name in _INS:
        a = _np.ascontiguousarray(inputs[name])
        arrays[f"in_{name}_dram"] = a
        args.append(nc.dram_tensor(f"in_{name}_dram", a.shape, mybir.dt.from_np(a.dtype), kind="ExternalInput").ap())
    for i, shape in enumerate(_OUTS):
        args.append(nc.dram_tensor(f"out_{i}_dram", shape, F32, kind="ExternalOutput").ap())
    build(nc, *args)
    r = _run(nc, [arrays], core_ids=[0])
    return tuple(r.results[0][f"out_{i}_dram"] for i in range(len(_OUTS)))
```

```python
from contextlib import ExitStack

import concourse.bass as bass
import concourse.mybir as mybir
from concourse.alu_op_type import AluOpType as ALU

ACT = mybir.ActivationFunctionType
F32 = mybir.dt.float32
F32R = mybir.dt.float32r
AX_X = mybir.AxisListType.X

P = 128
D = 1024
KD = D // P
SEQ = 1024
DEC_B, DEC_S = 8, 16
NT = (SEQ + DEC_B * DEC_S) // P
NP = SEQ // P
TOK = NT * P
NG = 3
TG = TOK // NG
TPG = NT // NG
H, DK, DV = 4, 128, 256
QK_W, V_W = H * DK, H * DV
A_PROJ = 2 * QK_W + 2 * V_W + 2 * H
CAP = 15.0
INNER = 2 * D
NF = INNER // P
G_B = 4
FPG = NF // G_B
D_FF = 2816
EPS = 1e-6
BIG = 1e30
FREE_UNITS = 5

G_OUT, G_MIX, G_FFN, G_FINAL, G_V, G_ALL = 0, KD, 3 * KD, 5 * KD, 6 * KD, 6 * KD + NF
Q_A, Q_M, Q_WI, Q_EMT, Q_WS, Q_DECAY, NQ = 0, 1, 2, 3, 4, 5, 6


class WeightPhase:

    def __init__(self, before, iterations, slots, back):
        self.base = before.end if before else 0
        self.n, self.slots = len(slots), slots
        self.end = self.base + iterations * self.n
        self.back = back

    def count(self, i, u, add=0):
        return i * self.n + (self.base + u + add)

    def raw(self, u):
        return (self.base + u) % 2

    def loads(self, i, u):
        return i * (self.n // 2) + ((self.base + u) // 2 + 1)


N_FFN = D_FF // (2 * P)
W_GATES = WeightPhase(None, 1, [0], [5])
W_HEADS = WeightPhase(W_GATES, H, [2, 1, 0, 2, 0, 2, 1, 0], [3, 3, 3, 3, 2, 2, 5, 3])
W_FFN0 = WeightPhase(W_HEADS, N_FFN, [2, 1, 0, 2, 1, 0], [3] * 6)
W_BV = WeightPhase(W_FFN0, NF // 4, [2, 1, 0, 1], [3, 2, 3, 2])
W_BU = WeightPhase(W_BV, NF // 4, [2, 1, 0, 1], [3, 2, 3, 2])
W_BO = WeightPhase(W_BU, KD // 2, [2, 0, 2, 0], [2] * 4)
W_FFN1 = WeightPhase(W_BO, N_FFN, [1, 2, 0, 1, 2, 0], [3] * 6)

P_ORDER = [(a, g, q) for a in range(2) for g in range(NG) for q in range(FPG // 2 * a, FPG // 2 * (a + 1))]

LN_DVE = [NP, 0, 2, 4, 6]
LN_ACT = [1, 3, 5, 7]

TICKETS = (["mb"] * 3 + ["wib"] * 3 + ["s"] * 3 + ["ctr"] * 4 + ["nt"] + ["u"] * NP + ["us"] * 4 + ["un", "cfin"]
           + ["pv"] * NT + ["o"] * 2 + ["ht"] * 2 + ["o"] + ["ht"] * 4)
BY_ACT = {"ctr", "nt", "cfin", "o"}


def ticket(name, k=0):
    return [t for t, x in enumerate(TICKETS) if x == name][k]


def taken(t):
    mine = TICKETS[t] in BY_ACT
    return sum((x in BY_ACT) == mine for x in TICKETS[:t + 1])


NTICK = len(TICKETS)
N_ACT = sum(x in BY_ACT for x in TICKETS)
N_DVE = NTICK - N_ACT


def build(nc, x_prompt, x_sample, state_C, state_n, state_m, g_mix, g_ffn, g_final,
          a_w_in, a_b_gate, a_g_out, a_w_out, b_w_in, b_g_v, b_w_s, b_b_s, b_w_out,
          f_w_gu, f_w_down,
          y_prompt, y_sample, C_prompt, n_prompt, m_prompt, C_sample, n_sample, m_sample, v_rows):
    ctx = ExitStack()
    with ctx:
        def sb(name, shape, dt=F32, stack=ctx):
            return stack.enter_context(nc.sbuf_tensor(name, shape, dt))

        def sem(name):
            return ctx.enter_context(nc.semaphore(name))

        xT = sb("xT", [P, KD, TOK])
        w_raw = [sb(f"w_raw{r}", [P, KD, P]) for r in range(2)]
        w_hi = [sb(f"w_hi{s}", [P, KD, P], F32R) for s in range(3)]
        w_lo = [sb(f"w_lo{s}", [P, KD, P], F32R) for s in range(3)]
        ident = sb("ident", [P, P])
        ones = sb("ones", [P, P])
        gains = sb("gains", [P, G_ALL])
        r_tok = gains[:, 0:NT]
        tri = sb("tri", [P, P])
        tri_s = sb("tri_s", [P, P])
        eps_t = sb("eps_t", [P, 1])

        with ExitStack() as part:
            xn_hi = sb("xn_hi", [P, KD, TOK], F32R, part)
            xn_lo = sb("xn_lo", [P, KD, TOK], F32R, part)
        with ExitStack() as part:
            x_in = sb("x_in", [P, NT, D], F32, part)
            gain_rows = sb("gain_rows", [G_ALL, P], F32, part)
        with ExitStack() as part:
            y_out = sb("y_out", [P, NT, D], F32, part)
            x_gain = sb("x_gain", [P, KD, TOK], F32, part)
        with ExitStack() as part:
            p_hi = sb("p_hi", [P, NF, TOK], F32R, part)
        hold = sb("hold_xn", [P, 2 * KD * TOK])

        with ExitStack() as part:
            def pa(name, shape, dt=F32):
                return sb(name, shape, dt, part)
            sq_a = pa("sq_a", [P, KD, TG])
            ssum_a = pa("ssum_a", [P, TG])
            rstd_a = pa("rstd_a", [P, TG])
        with ExitStack() as part:
            def pa(name, shape, dt=F32):
                return sb(name, shape, dt, part)
            qT = pa("qT", [P, TOK])
            kT = pa("kT", [P, TOK])
            k_tok = pa("k_tok", [P, NT, DK])
            v_tok = pa("v_tok", [P, NT, DV + 1])
            sig_o = pa("sig_o", [P, 2, TOK])
            dmat = pa("dmat", [P, NT, P])
            qw = pa("qw", [P, TOK])
            num = pa("num", [P, NT, DV + 1])
            c_nat = pa("c_nat", [P, 2, DEC_B, DK])
            c_out = pa("c_out", [P, 3, P])
            with ExitStack() as sub:
                state = sb("state", [P, NT, DV + 1], F32, sub)
                c_smp = sb("c_smp", [P, DEC_B, DV + 1], F32, sub)
            with ExitStack() as sub:
                h_hi = sb("h_hi", [P, 2, TOK], F32R, sub)
                h_lo = sb("h_lo", [P, 2, TOK], F32R, sub)
            hold_h = pa("hold_h", [P, 4 * TOK])
            pack = pa("pack", [P, H, NQ, NT])
            cur = pa("cur", [P, NQ, NT])
            dec_s = pa("dec_s", [P, H, DEC_B])
            dec8 = pa("dec8", [P, H])
            b_first = pa("b_first", [P, DEC_B])
            b_mem = pa("b_mem", [P, DEC_B])
            n_nat = pa("n_nat", [DEC_B, DK])
            g_bias = pa("g_bias", [2 * H, 1])
            g_h = pa("g_h", [P, 2])
            nstat = pa("nstat", [P, 6, NT])
            m_out = pa("m_out", [P, 2, H])
            m_in = pa("m_in", [P, H])
        num_flat = num[:, :, :].rearrange("p c v -> p (c v)")
        diag = num_flat[:, 0:NT * P].rearrange("p (c t) -> p c t", c=NT)
        diag2 = qw[:, :].rearrange("p (c t) -> p c t", c=NT)
        k_blk = num_flat[:, NT * P:NT * P + DEC_B * DK].rearrange("p (b d) -> p b d", b=DEC_B)
        v_tmp = dmat[:, :, :].rearrange("p c t -> p (c t)")
        q_blk = kT[:, 0:DEC_B * P].rearrange("p (b t) -> p b t", b=DEC_B)
        c_flat = c_nat[:, :, :, :].rearrange("p j b d -> p (j b d)")
        blk, blk_last, last = (c_flat[:, k * P:(k + 1) * P] for k in range(3))
        reset = c_flat[0:H * NT, 3 * P:4 * P]
        small = num_flat[:, 0:8 * H * NT].rearrange("p (q h c) -> p q h c", q=8, h=H)
        gtok = num_flat[:, 8 * H * NT:8 * H * NT + NT * 2 * H].rearrange("p (c g) -> p c g", c=NT)
        gT = qT
        aT = qw
        h_f = dmat[:, :, :].rearrange("p c t -> p (c t)")

        with ExitStack() as part:
            hg_hi = sb("hg_hi", [P, 2, TOK], F32R, part)
            hg_lo = sb("hg_lo", [P, 2, TOK], F32R, part)
            silu = sb("silu", [P, 2, NG, TG], F32, part)
            h_tmp = sb("h_tmp", [P, 2, TG], F32, part)
            sq_f = sb("sq_f", [P, KD, TG], F32, part)
            ssum_f = sb("ssum_f", [P, 2, TOK], F32, part)
            rstd_f = sb("rstd_f", [P, TOK], F32, part)

        with ExitStack() as part:
            vs = sb("vs", [P, NT, NF, P], F32, part)
        with ExitStack() as part:
            p_lo = sb("p_lo", [P, NT, NF, P], F32R, part)
            with ExitStack() as sub:
                bias_b = sb("bias_b", [P, G_B, P], F32, sub)
            with ExitStack() as sub:
                stat = sb("stat", [P, NT, NF // 4, 6], F32, sub)
            with ExitStack() as sub:
                w_s_in = sb("w_s_in", [P, G_B, P], F32, sub)
            hold_b = sb("hold_b", [P, G_B * P], F32, part)
            with ExitStack() as sub:
                w_s_smp = sb("w_s_smp", [P, G_B, P], F32, sub)
            t_b = sb("t_b", [P, 2, TG], F32, part)
            with ExitStack() as sub:
                mix = sb("mix", [P, 2, G_B, P], F32, sub)
                mv = sb("mv", [P, NT, 2], F32, sub)
                rs_v = sb("rs_v", [P, NT, 3], F32, sub)
            with ExitStack() as sub:
                rstd_b = sb("rstd_b", [P, TOK], F32, sub)
        RQ = INNER // 4
        row_buf = [w_s_in[:, :, :].rearrange("p g s -> p (g s)"), t_b[:, :, :].rearrange("p a t -> p (a t)")[:, 0:RQ]]

        ps = [ctx.enter_context(nc.psum_tensor(f"ps{b}", [P, 512], F32)) for b in range(8)]

        def bank(b, n=TG):
            return ps[b % 8][:, 0:n]

        const_ok = sem("const_ok")
        x_loaded = [sem(f"x_loaded{g}") for g in range(NG)]
        rows_loaded = sem("rows_loaded")
        small_loaded = sem("small_loaded")
        xt_pe, xt_dve, xt_act = sem("xt_pe"), sem("xt_dve"), sem("xt_act")
        raw_loaded = [sem("raw_loaded0"), sem("raw_loaded1")]
        raw_clear = sem("raw_clear")
        hi_split, split, used = sem("hi_split"), sem("units_split"), sem("units_used")
        squared, summed, mean_sq, rooted = sem("squared"), sem("summed"), sem("mean_sq"), sem("rooted")
        r_sum, r_root, r_done = sem("r_sum"), sem("r_root"), sem("r_done")
        r_diag, r_wide, r_ready = sem("r_diag"), sem("r_wide"), sem("r_ready")
        xn_full, n_full, n_hi, n_lo = sem("xn_full"), sem("n_full"), sem("n_hi"), sem("n_lo")
        dve_step = sem("dve_step")
        act_step = sem("act_step")
        pool_step = sem("pool_step")
        gt_mm, gt_act, gt_scaled, gt_tr, gate_pe, gate_dve, gate_act = (
            sem(x) for x in ("gt_mm", "gt_act", "gt_scaled", "gt_tr", "gate_pe", "gate_dve", "gate_act"))
        a_mm, a_evac, a_vtmp, a_sig = sem("a_mm"), sem("a_evac"), sem("a_vtmp"), sem("a_sig")
        a_tr, a_ktok, a_vtok = sem("a_tr"), sem("a_ktok"), sem("a_vtok")
        t_pe, t_act, t_dve = sem("t_pe"), sem("t_act"), sem("t_dve")
        a_cur, a_diag, a_dargs, a_exp, a_dve, a_kb = (
            sem(x) for x in ("a_cur", "a_diag", "a_dargs", "a_exp", "a_dve", "a_kb"))
        a_ssq, a_fac, a_hlo, a_sqrt = sem("a_ssq"), sem("a_fac"), sem("a_hlo"), sem("a_sqrt")
        wd_mm, wd_add = sem("wd_mm"), sem("wd_add")
        c_loaded, n_loaded, c_stored = sem("c_loaded"), sem("n_loaded"), sem("c_stored")
        stored = sem("stored")
        g_mm = [sem(f"g_mm{x}") for x in range(2)]
        u_mm = [sem(f"u_mm{x}") for x in range(2)]
        g_scaled = [sem(f"g_scaled{x}") for x in range(2)]
        s_scaled = [sem(f"s_scaled{x}") for x in range(2)]
        g_silu = [sem(f"g_silu{x}") for x in range(2)]
        h_full = [sem(f"h_full{x}") for x in range(2)]
        h_his = [sem(f"h_his{x}") for x in range(2)]
        h_los = [sem(f"h_los{x}") for x in range(2)]
        d_mm = [sem(f"d_mm{x}") for x in range(2)]
        d_add = [sem(f"d_add{x}") for x in range(2)]
        bv_scaled, bu_scaled = sem("bv_scaled"), sem("bu_scaled")
        bv_mm, bv_gelu, bv_tr, bv_tok = sem("bv_mm"), sem("bv_gelu"), sem("bv_tr"), sem("bv_tok")
        b_loaded, b_mixed = sem("b_loaded"), sem("b_mixed")
        bw_tr, bw_copied, mix_ok = sem("bw_tr"), sem("bw_copied"), sem("mix_ok")
        ln_stat, ln_root, ln_scale = sem("ln_stat"), sem("ln_root"), sem("ln_scale")
        ln_dve, ln_act = sem("ln_dve"), sem("ln_act")
        bv_stat = sem("bv_stat")
        mx_mm, mx_act, mx_dve = sem("mx_mm"), sem("mx_act"), sem("mx_dve")
        gv_loaded, row_stored = ([sem(f"{x}{r}") for r in range(2)] for x in ("gv_loaded", "row_stored"))
        gv_done = sem("gv_done")
        bu_mm, bu_gelu, bu_gate, bu_bias = sem("bu_mm"), sem("bu_gelu"), sem("bu_gate"), sem("bu_bias")
        ps_hi, ps_lo = sem("ps_hi"), sem("ps_lo")
        bo_mm, bo_add = sem("bo_mm"), sem("bo_add")
        yt_pe, yt_act, yt_dve = sem("yt_pe"), sem("yt_act"), sem("yt_dve")

        block = ctx.enter_context(nc.Block())

        def tok(t, g):
            return t[..., g * TG:(g + 1) * TG]

        def tiles(ap):
            return ap.rearrange("p (c t) -> p c t", c=TPG)

        @block.sync
        def _(sp):
            for g in range(NG):
                for c in range(TPG * g, TPG * g + TPG):
                    src = x_prompt[0, c * P:(c + 1) * P, :] if c < NP else x_sample.rearrange("b s d -> (b s) d")
                    sp.dma_start(x_in[:, c, :], src).then_inc(x_loaded[g], 16)
                if g == 0:
                    for at, src, n in ((G_MIX, g_mix.rearrange("l (k p) -> (l k) p", p=P), 2 * KD),
                                       (G_FFN, g_ffn.rearrange("l (k p) -> (l k) p", p=P), 2 * KD),
                                       (G_FINAL, g_final.rearrange("(k p) -> k p", p=P), KD),
                                       (G_OUT, a_g_out.rearrange("l (k p) -> (l k) p", p=P), KD),
                                       (G_V, b_g_v.rearrange("l (k p) -> (l k) p", p=P), NF)):
                        sp.dma_start(gain_rows[at:at + n, :], src).then_inc(rows_loaded, 16)

            def load(phase, i, u, src, width=P):
                if phase is not W_GATES:
                    sp.wait_ge(split, phase.count(i, u, -1))
                r = phase.raw(u)
                dst = w_raw[r][:, :, 0:width]
                if len(src.shape) == 2:
                    dst = w_raw[r][:, :, :].rearrange("p k n -> p (k n)")
                sp.dma_start(dst, src).then_inc(raw_loaded[r], 16)

            a_in = a_w_in[0].rearrange("(k p) n -> p k n", p=P)
            sp.wait_ge(raw_clear, 1)
            load(W_GATES, 0, 0, a_in[:, :, A_PROJ - 2 * H:A_PROJ], 2 * H)
            sp.dma_start(m_in[:, :], state_m[:, 0, :].unsqueeze(1).to_broadcast([DEC_B, DEC_S, H]))\
                .then_inc(small_loaded, 16)
            sp.dma_start(g_bias[:, :], a_b_gate.rearrange("l (g o) -> (l g) o", o=1)).then_inc(small_loaded, 16)

            a_out = a_w_out[0].rearrange("(k p) n -> k p n", p=P)
            c_in = state_C[:, 0].rearrange("b h (j v) d -> h j v b d", j=2)
            c_to = C_sample[:, 0].rearrange("b h (j v) d -> h j v b d", j=2)
            n_in = state_n[:, 0].rearrange("b h d -> h b d")
            n_to = n_sample[:, 0].rearrange("b h d -> h b d")
            sp.wait_ge(gate_dve, 6)
            sp.dma_start(m_prompt[0], m_out[0:1, 0, :]).then_inc(stored, 16)
            sp.dma_start(m_sample[:, 0, :], m_out[0:P:DEC_S, 1, :]).then_inc(stored, 16)
            with sp.Fori(0, H) as h:
                for u, col in enumerate((h * DK, h * DK + QK_W)):
                    load(W_HEADS, h, u, a_in[:, :, bass.ds(col, P)])
                sp.wait_ge(c_stored, h * (16 * 5) + 1)
                for j in range(2):
                    sp.dma_start(c_nat[:, j, :, :], c_in[bass.ds(h, 1), j].rearrange("o v b d -> (o v) b d"))\
                        .then_inc(c_loaded, 16)
                sp.dma_start(n_nat[:, :], n_in[bass.ds(h, 1)].rearrange("o b d -> (o b) d")).then_inc(n_loaded, 16)
                for u in range(2, 6):
                    at = 2 * QK_W + (u % 2) * P + (V_W if u >= 4 else 0)
                    load(W_HEADS, h, u, a_in[:, :, bass.ds(h * DV + at, P)])
                for u in range(6, 8):
                    load(W_HEADS, h, u, a_out[bass.ds(h * 2 + (u - 6), 1)].rearrange("o p n -> (o p) n"))
                sp.wait_ge(t_act, h * N_ACT + taken(ticket("cfin")))
                sp.dma_start(C_prompt[0, 0].rearrange("h (j v) d -> h v j d", j=2)[bass.ds(h, 1)]
                             .rearrange("o v j d -> (o v) j d"), c_out[:, 0:2, :]).then_inc(c_stored, 16)
                sp.dma_start(n_prompt[0, 0].rearrange("h (d o) -> h d o", o=1)[bass.ds(h, 1)]
                             .rearrange("a d o -> (a d) o"), c_out[:, 2, 0:1]).then_inc(c_stored, 16)
                sp.wait_ge(t_dve, h * N_DVE + taken(ticket("un")))
                for j in range(2):
                    sp.dma_start(c_to[bass.ds(h, 1), j].rearrange("o v b d -> (o v) b d"), c_nat[:, j, :, :])\
                        .then_inc(c_stored, 16)
                sp.dma_start(n_to[bass.ds(h, 1)].rearrange("o b d -> (o b) d"), n_nat[:, :]).then_inc(c_stored, 16)

            def ffn(layer, phase):
                gu = f_w_gu[layer].rearrange("(k p) n -> p k n", p=P)
                down = f_w_down[layer].rearrange("(k p) n -> k p n", p=P)
                with sp.Fori(0, N_FFN) as i:
                    for c in range(2):
                        load(phase, i, 2 * c, gu[:, :, bass.ds(i * (2 * P) + c * P, P)])
                        load(phase, i, 2 * c + 1, gu[:, :, bass.ds(i * (2 * P) + (D_FF + c * P), P)])
                    for c in range(2):
                        load(phase, i, 4 + c, down[bass.ds(i * 2 + c, 1)].rearrange("o p n -> (o p) n"))

            ffn(0, W_FFN0)

            b_in = b_w_in[0].rearrange("(k p) n -> p k n", p=P)
            with sp.Fori(0, NF // 4) as i:
                for u in range(4):
                    load(W_BV, i, u, b_in[:, :, bass.ds(i * (4 * P) + (INNER + u * P), P)])
            def load_u(i, u):
                load(W_BU, i, u, b_in[:, :, bass.ds(i * (4 * P) + u * P, P)])

            load_u(0, 0)
            load_u(0, 1)
            sp.wait_ge(ln_stat, 1)
            sp.dma_start(w_s_in[:, :, :], b_w_s[0].rearrange("g t s -> t g s")).then_inc(b_loaded, 16)
            sp.wait_ge(bv_tr, 2 + 12 * (NF // 4))
            for b in range(DEC_B):
                sp.dma_start(w_s_smp[b * DEC_S:(b + 1) * DEC_S, :, 0:DEC_S],
                             b_w_s[0, :, 0:DEC_S, 0:DEC_S].rearrange("g t s -> t g s")).then_inc(b_loaded, 16)
            load_u(0, 2)
            load_u(0, 3)
            sp.wait_ge(bw_copied, 2)

            def load_gain(q):
                if q >= 2:
                    sp.wait_ge(row_stored[q % 2], 16)
                sp.dma_start(row_buf[q % 2], b_g_v[0:1, q * RQ:(q + 1) * RQ].to_broadcast([P, RQ]))\
                    .then_inc(gv_loaded[q % 2], 16)

            def store_rows(q):
                sp.wait_ge(gv_done, q + 1)
                sp.dma_start(v_rows.rearrange("b l s f -> (b l s) f")[:, q * RQ:(q + 1) * RQ], row_buf[q % 2])\
                    .then_inc(row_stored[q % 2], 16)

            load_gain(0)
            load_gain(1)
            for q in range(4):
                store_rows(q)
                if q < 2:
                    load_gain(q + 2)
            sp.wait_ge(row_stored[0], 32)
            sp.dma_start(bias_b[:, :, :], b_b_s.unsqueeze(0).to_broadcast([P, 1, G_B, P])
                         .rearrange("p o g t -> p (o g) t")).then_inc(b_mixed, 16)
            with sp.Fori(1, NF // 4) as i:
                for u in range(4):
                    load_u(i, u)
            b_out = b_w_out[0].rearrange("(a k p) n -> a p k n", a=2, p=P)
            with sp.Fori(0, KD // 2) as i:
                for u in range(4):
                    load(W_BO, i, u, b_out[u % 2][:, :, bass.ds(i * (2 * P) + (u // 2) * P, P)])

            ffn(1, W_FFN1)

            for c in range(NT):
                sp.wait_ge(yt_act, c + 1)
                sp.wait_ge(yt_dve, c + 1)
                dst = y_prompt[0, c * P:(c + 1) * P, :] if c < NP else y_sample.rearrange("b s d -> (b s) d")
                sp.dma_start(dst, y_out[:, c, :]).then_inc(stored, 16)
            sp.wait_ge(c_stored, 16 * 5 * H + 1)
            sp.wait_ge(stored, 16 * (2 + NT))

        @block.gpsimd
        def _(pool):
            n = 0

            def link(ins):
                nonlocal n
                n += 1
                ins.then_inc(pool_step, 1)
                pool.wait_ge(pool_step, n)

            nc.gpsimd.memset(w_raw[0][:, :, :], 0.0).then_inc(raw_clear, 1)
            link(nc.gpsimd.memset(ident[:, :], 0.0))
            link(nc.gpsimd.affine_select(out=ident[:, :], in_=ident[:, :], compare_op=ALU.not_equal, fill=1.0,
                                         base=0, pattern=[[-1, P]], channel_multiplier=1))
            nc.gpsimd.memset(eps_t[:, :], EPS)
            link(nc.gpsimd.memset(ones[:, :], 1.0))
            link(nc.gpsimd.affine_select(out=tri[:, :], in_=ones[:, :], compare_op=ALU.is_ge, fill=0.0,
                                         base=0, pattern=[[1, P]], channel_multiplier=-1))

            def by_stream(t):
                return t.rearrange("p (b s) -> p b s", b=DEC_B)

            for dst, src in ((tri_s, tri), (blk, ones)):
                link(nc.gpsimd.affine_select(out=by_stream(dst[:, :]), in_=by_stream(src[:, :]), compare_op=ALU.is_ge,
                                             fill=0.0, base=0, pattern=[[-DEC_S, DEC_B], [0, DEC_S]],
                                             channel_multiplier=1))
            link(nc.gpsimd.affine_select(out=by_stream(blk[:, :]), in_=by_stream(blk[:, :]), compare_op=ALU.is_ge,
                                         fill=0.0, base=DEC_S - 1, pattern=[[DEC_S, DEC_B], [0, DEC_S]],
                                         channel_multiplier=-1))
            link(nc.gpsimd.memset(blk_last[:, :], 0.0))
            link(nc.gpsimd.affine_select(out=by_stream(blk_last[:, :]), in_=by_stream(blk_last[:, :]),
                                         compare_op=ALU.not_equal, fill=1.0, base=-(DEC_S - 1),
                                         pattern=[[-DEC_S, DEC_B], [0, DEC_S]], channel_multiplier=1))
            link(nc.gpsimd.memset(last[:, :], 0.0))
            link(nc.gpsimd.affine_select(out=last[:, :], in_=last[:, :], compare_op=ALU.not_equal, fill=1.0,
                                         base=-(P - 1), pattern=[[0, P]], channel_multiplier=1))
            link(nc.gpsimd.memset(b_first[:, :], 0.0))
            link(nc.gpsimd.affine_select(out=b_first[:, :], in_=b_first[:, :], compare_op=ALU.not_equal, fill=1.0,
                                         base=0, pattern=[[-DEC_S, DEC_B]], channel_multiplier=1))
            link(nc.gpsimd.affine_select(out=b_mem[:, :], in_=ones[:, 0:DEC_B], compare_op=ALU.is_ge, fill=0.0,
                                         base=0, pattern=[[-DEC_S, DEC_B]], channel_multiplier=1))
            link(nc.gpsimd.affine_select(out=b_mem[:, :], in_=b_mem[:, :], compare_op=ALU.is_ge, fill=0.0,
                                         base=DEC_S - 1, pattern=[[DEC_S, DEC_B]], channel_multiplier=-1))
            link(nc.gpsimd.memset(reset[:, :], BIG))
            for h in range(H):
                link(nc.gpsimd.affine_select(out=by_stream(reset[:, :]), in_=by_stream(reset[:, :]),
                                             compare_op=ALU.not_equal, fill=-BIG, base=-1000 * (NT * h + NP),
                                             pattern=[[0, DEC_B], [1, DEC_S]], channel_multiplier=1000))
            link(nc.gpsimd.memset(dmat[:, :, :], 0.0))
            nc.gpsimd.drain().then_inc(const_ok, 1)

            def split_unit(phase, i, u):
                r, s = phase.raw(u), phase.slots[u]
                pool.wait_ge(used, phase.count(i, u, 1 + FREE_UNITS - phase.back[u]))
                pool.wait_ge(raw_loaded[r], phase.loads(i, u) * 16)
                nc.gpsimd.tensor_tensor(w_hi[s][:, :, :], w_raw[r][:, :, :],
                                        ones[:, :].unsqueeze(1).to_broadcast([P, KD, P]), ALU.mult)\
                    .then_inc(hi_split, 1)
                pool.wait_ge(hi_split, phase.count(i, u, 1))
                nc.gpsimd.tensor_tensor(w_lo[s][:, :, :], w_raw[r][:, :, :], w_hi[s][:, :, :].bitcast(F32),
                                        ALU.subtract).then_inc(split, 1)

            split_unit(W_GATES, 0, 0)
            with pool.Fori(0, H) as h:
                for u in range(8):
                    split_unit(W_HEADS, h, u)
            with pool.Fori(0, N_FFN) as i:
                for u in range(6):
                    split_unit(W_FFN0, i, u)
            with pool.Fori(0, NF // 4) as i:
                for u in range(4):
                    split_unit(W_BV, i, u)
            with pool.Fori(0, NF // 4) as i:
                for u in range(4):
                    split_unit(W_BU, i, u)
            with pool.Fori(0, KD // 2) as i:
                for u in range(4):
                    split_unit(W_BO, i, u)
            with pool.Fori(0, N_FFN) as i:
                for u in range(6):
                    split_unit(W_FFN1, i, u)

        @block.tensor
        def _(pe):
            for _ in range(FREE_UNITS - 1):
                pe.drain().then_inc(used, 1)

            def passes(out, slot, blocks, hi, lo, first, last_one, frees=False):
                n, total = 0, 3 * len(blocks)
                for k in blocks:
                    for w, x in ((w_hi, hi), (w_hi, lo), (w_lo, hi)):
                        ins = pe.matmul(out, w[slot][:, k, :], x(k), start=(first and n == 0),
                                        stop=(last_one and n == total - 1))
                        if n == 0 and frees:
                            ins.then_inc(used, 1)
                        n += 1
                return ins

            def xn(g):
                return (lambda k: tok(xn_hi[:, k, :], g)), (lambda k: tok(xn_lo[:, k, :], g))

            def unit_piece(phase, u, g, b):
                hi, lo = xn(g)
                return passes(bank(b), phase.slots[u], range(KD), hi, lo, True, True, g == 0)

            def norm0():
                for g in range(NG):
                    pe.wait_ge(summed, g + 1)
                    pe.matmul(bank(6 + g % 2), ones[:, :], ssum_a[:, :], start=True, stop=True).then_inc(mean_sq, 1)

            def row_sums(n):
                for c in range(NT):
                    pe.wait_ge(summed, NG * n + c // TPG + 1)
                    for half in range(2):
                        ins = pe.matmul(bank(6, NT)[:, c:c + 1], ssum_f[:, half, c * P:(c + 1) * P], ones[:, 0:1],
                                        start=half == 0, stop=half == 1)
                ins.then_inc(r_sum, 1)

            def widen(k, src):
                for g in range(NG):
                    pe.wait_ge(r_diag, NG * k + g + 1)
                    if g == 2:
                        pe.wait_ge(r_ready, NG * k + 1)
                    pe.matmul(bank(7 - g % 2), ones[:, :], src(g), start=True, stop=True).then_inc(r_wide, 1)

            def xn_ready(n, g):
                pe.wait_ge(n_lo, KD * (NG * n + g + 1))

            pe.wait_ge(const_ok, 1)
            for c in range(NT):
                if c % TPG == 0:
                    pe.wait_ge(x_loaded[c // TPG], 16 * TPG)
                for half in range(2):
                    t = 2 * c + half
                    if t >= 8:
                        pe.wait_ge(xt_act if half else xt_dve, (t - 8) // 2 + 1)
                    for k in range(4):
                        ins = pe.transpose(ps[t % 8][:, k * P:(k + 1) * P],
                                           x_in[:, c, (4 * half + k) * P:(4 * half + k + 1) * P], ident[:, :])
                    ins.then_inc(xt_pe, 1)
            pe.wait_ge(rows_loaded, 16 * 5)
            pe.wait_ge(xt_dve, 6)
            pe.transpose(ps[2][:, 0:G_ALL], gain_rows[:, :], ident[0:G_ALL, 0:G_ALL]).then_inc(xt_pe, 1)
            pe.wait_ge(xt_dve, NT + 1)
            pe.wait_ge(xt_act, NT)
            norm0()

            pe.wait_ge(split, 1)
            for g in range(NG):
                xn_ready(0, g)
                ins = unit_piece(W_GATES, 0, g, g)
                ins.then_inc(gt_mm, 1)
            pe.wait_ge(gt_scaled, 1)
            for c in range(NT):
                ins = pe.transpose(ps[3][:, c * 8:(c + 1) * 8], gT[0:2 * H, c * P:(c + 1) * P],
                                   ident[0:2 * H, 0:2 * H])
            ins.then_inc(gt_tr, 1)
            lf = small[:, 0, :, :]
            pe.wait_ge(gate_dve, 1)
            for col, whole, own in ((0, tri, tri_s), (64, ones, blk)):
                for c0, c1, m in ((0, NP, whole), (NP, NT, own)):
                    ins = pe.matmul(ps[4][:, col:col + H * NT].rearrange("p (h c) -> p h c", h=H)[:, :, c0:c1],
                                    m[:, :], lf[:, :, c0:c1], start=True, stop=True)
            ins.then_inc(gate_pe, 1)
            pe.wait_ge(gate_dve, 2)
            pe.transpose(ps[5][0:H * NT, 0:P], small[:, 2, :, :].rearrange("p h c -> p (h c)"), ident[:, :])\
                .then_inc(gate_pe, 1)
            pe.wait_ge(gate_dve, 3)
            pe.transpose(ps[6][:, 0:H * NT], aT[0:H * NT, P:2 * P], ident[0:H * NT, 0:H * NT]).then_inc(gate_pe, 1)
            pe.wait_ge(gate_dve, 4)
            cm = small[:, 3, :, :]
            for c0, c1, m in ((0, NP, last), (NP, NT, blk_last)):
                ins = pe.matmul(ps[7][:, 0:H * NT].rearrange("p (h c) -> p h c", h=H)[:, :, c0:c1],
                                m[:, :], cm[:, :, c0:c1], start=True, stop=True)
            ins.then_inc(gate_pe, 1)
            pe.wait_ge(gate_dve, 5)
            pe.matmul(ps[3][:, 128:128 + H * DEC_B], ones[:, :], dmat[:, 0, 0:H * DEC_B], start=True, stop=True)
            pe.matmul(ps[3][0:DEC_B, 192:192 + H], b_first[:, :], pack[:, :, Q_DECAY, NP], start=True, stop=True)\
                .then_inc(gate_pe, 1)
            pe.wait_ge(gate_dve, 6)

            with pe.Fori(0, H) as h:
                hi, lo = xn(0)
                for u in range(5):
                    pe.wait_ge(split, W_HEADS.count(h, u, 1))
                    for g in range(NG):
                        if u < 2:
                            pe.wait_ge(wd_add, h * 24 + (3 * u + g + 1))
                        elif u in (2, 3):
                            pe.wait_ge(a_evac, h * 6 + 3 * (u - 2) + g + 1)
                        elif u == 4:
                            pe.wait_ge(a_vtmp, h * 6 + 3 * (u - 4) + g + 1)
                        ins = unit_piece(W_HEADS, u, g, 3 * (u % 2) + g)
                        ins.then_inc(a_mm, 1)
                        n = 3 * u + g - 1 - 3
                        if 0 <= n < 9:
                            turn = n
                            if n < 3:
                                pe.wait_ge(a_evac, h * 6 + 3 + n + 1)
                                src = tok(kT[:, :], n)
                            else:
                                pe.wait_ge(a_vtmp, h * 6 + (n - 3) + 1)
                                src = v_tmp[:, (n % 2) * TG:(n % 2 + 1) * TG]
                            if turn >= 2:
                                back = turn - 2
                                if back < 3:
                                    pe.wait_ge(a_ktok, h * 3 + back + 1)
                                else:
                                    pe.wait_ge(a_vtok, h * 6 + back - 3 + 1)
                            for c in range(TPG):
                                ins = pe.transpose(bank(6 + turn % 2)[:, c * P:(c + 1) * P],
                                                   src[:, c * P:(c + 1) * P], ident[:, :])
                            ins.then_inc(a_tr, 1)

                def wait_bank(t):
                    if t >= 8:
                        if TICKETS[t - 8] in BY_ACT:
                            pe.wait_ge(t_act, h * N_ACT + taken(t - 8))
                        else:
                            pe.wait_ge(t_dve, h * N_DVE + taken(t - 8))
                    elif t < 3:
                        pe.wait_ge(a_sig, h * 3 + t + 1)
                    elif t < 6:
                        pe.wait_ge(a_vtmp, h * 6 + t + 1)
                    else:
                        pe.wait_ge(a_vtok, h * 6 + 6)

                for name, src in (("mb", diag), ("wib", diag2)):
                    pe.wait_ge(a_diag, h * 2 + (1 if name == "mb" else 2))
                    for g in range(NG):
                        t = ticket(name, g)
                        wait_bank(t)
                        pe.matmul(bank(t), ones[:, :], src[:, g * TPG:(g + 1) * TPG, :], start=True, stop=True)\
                            .then_inc(t_pe, 1)
                for g in range(NG):
                    t = ticket("s", g)
                    wait_bank(t)
                    for c in range(g * TPG, (g + 1) * TPG):
                        ins = pe.matmul(bank(t)[:, (c % TPG) * P:(c % TPG + 1) * P], kT[:, c * P:(c + 1) * P],
                                        qT[:, c * P:(c + 1) * P], start=True, stop=True)
                    ins.then_inc(t_pe, 1)
                pe.wait_ge(c_loaded, h * 32 + 32)
                pe.wait_ge(n_loaded, h * 16 + 16)
                wait_bank(ticket("nt"))
                for k in range(4):
                    t = ticket("ctr", k)
                    wait_bank(t)
                    for b in range(2):
                        for j in range(2):
                            ins = pe.transpose(ps[t % 8][:, (2 * b + j) * P:(2 * b + j + 1) * P],
                                               c_nat[:, j, 2 * k + b, :], ident[:, :])
                    ins.then_inc(t_pe, 1)
                t = ticket("nt")
                pe.transpose(ps[t % 8][:, 0:DEC_B], n_nat[:, :], ident[0:DEC_B, 0:DEC_B]).then_inc(t_pe, 1)
                for c in range(NP):
                    t = ticket("u", c)
                    wait_bank(t)
                    pe.matmul(bank(t, DV + 1), k_tok[:, c, :], v_tok[:, c, :], start=True, stop=True)\
                        .then_inc(t_pe, 1)
                pe.wait_ge(a_kb, h + 1)
                for j in range(2):
                    for half in range(2):
                        t = ticket("us", 2 * j + half)
                        wait_bank(t)
                        pe.matmul(ps[t % 8][:, :], v_tok[:, NP, j * P:(j + 1) * P],
                                  k_blk[:, 4 * half:4 * half + 4, :], start=True, stop=True).then_inc(t_pe, 1)
                t = ticket("un")
                wait_bank(t)
                pe.matmul(ps[t % 8][0:DEC_B, 0:DK], b_mem[:, :], k_tok[:, NP, :], start=True, stop=True)\
                    .then_inc(t_pe, 1)
                t = ticket("cfin")
                wait_bank(t)
                pe.wait_ge(t_dve, h * N_DVE + taken(ticket("u", NP - 1)))
                for j in range(2):
                    ins = pe.transpose(ps[t % 8][:, j * P:(j + 1) * P], state[:, NP, j * P:(j + 1) * P], ident[:, :])
                ins.then_inc(t_pe, 1)
                for c in range(NT):
                    t = ticket("pv", c)
                    wait_bank(t)
                    if c == NP:
                        pe.wait_ge(a_dve, h * 2 + 2)
                    pe.matmul(bank(t, DV + 1), dmat[:, c, :], v_tok[:, c, :], start=True, stop=False)
                    if c < NP:
                        ins = pe.matmul(bank(t, DV + 1), qw[:, c * P:(c + 1) * P], state[:, c, :],
                                        start=False, stop=True)
                    else:
                        for b in range(DEC_B):
                            ins = pe.matmul(bank(t, DV + 1), q_blk[:, b, :], c_smp[:, b, :],
                                            start=False, stop=(b == DEC_B - 1))
                    ins.then_inc(t_pe, 1)
                pe.wait_ge(split, W_HEADS.count(h, 5, 1))

                def o_piece(g):
                    t = ticket("o", g)
                    wait_bank(t)
                    unit_piece(W_HEADS, 5, g, t).then_inc(t_pe, 1)

                def output_turn(g):
                    pe.wait_ge(a_fac, h + 2)
                    for j in range(2):
                        t = ticket("ht", 2 * g + j)
                        wait_bank(t)
                        for c in range(TPG):
                            ins = pe.transpose(bank(t)[:, c * P:(c + 1) * P],
                                               num[:, g * TPG + c, j * P:(j + 1) * P], ident[:, :])
                        ins.then_inc(t_pe, 1)

                o_piece(0)
                o_piece(1)
                output_turn(0)
                o_piece(2)
                output_turn(1)
                output_turn(2)
                pe.wait_ge(split, W_HEADS.count(h, 7, 1))
                for g in range(NG):
                    pe.wait_ge(a_hlo, h * 6 + 2 * g + 2)
                    for j in range(KD):
                        n = KD * g + j
                        if n < 6:
                            wait_bank(max(t for t in range(NTICK) if t % 8 == n) + 8)
                        else:
                            pe.wait_ge(wd_add, h * 24 + n + 1)
                        for a in range(2):
                            ins = passes(bank(n % 6), W_HEADS.slots[6 + a], [j], lambda k: tok(h_hi[:, a, :], g),
                                         lambda k: tok(h_lo[:, a, :], g), a == 0, a == 1,
                                         n == (0, NG * KD - 1)[a])
                        ins.then_inc(wd_mm, 1)

            def ffn(layer, phase, n, k):
                gm, um, gs, hf, hl, dm, da = (x[layer] for x in (g_mm, u_mm, g_silu, h_full, h_los, d_mm, d_add))

                def body(i):
                    first = type(i) is int
                    for c in range(2):
                        pe.wait_ge(split, phase.count(i, 2 * c, 1))
                        for g in range(NG):
                            if first and c == 0:
                                xn_ready(n, g)
                            if c == 0:
                                pe.wait_ge(da, i * 24 + g + 1)
                            else:
                                pe.wait_ge(gs, i * 6 + g + 1)
                            ins = unit_piece(phase, 2 * c, g, g)
                            ins.then_inc(gm, 1)
                        pe.wait_ge(split, phase.count(i, 2 * c + 1, 1))
                        for g in range(NG):
                            if c == 0:
                                pe.wait_ge(da, i * 24 + 3 + g + 1)
                            else:
                                pe.wait_ge(hf, i * 6 + g + 1)
                            ins = unit_piece(phase, 2 * c + 1, g, 3 + g)
                            ins.then_inc(um, 1)
                            if first and c == 0 and g == 0:
                                row_sums(n)
                            if first and c == 0 and g == 1:
                                widen(k, lambda g: sq_f[:, g, :])
                    pe.wait_ge(split, phase.count(i, 5, 1))
                    for g in range(NG):
                        pe.wait_ge(hl, i * 6 + 3 + g + 1)
                        for j in range(KD):
                            m = KD * g + j
                            if m < 3:
                                pe.wait_ge(gs, i * 6 + 3 + m + 1)
                            elif m < 6:
                                pe.wait_ge(hf, i * 6 + m + 1)
                            else:
                                pe.wait_ge(da, i * 24 + m + 1)
                            for a in range(2):
                                ins = passes(bank(m % 6), phase.slots[4 + a], [j], lambda k: tok(hg_hi[:, a, :], g),
                                             lambda k: tok(hg_lo[:, a, :], g), a == 0, a == 1,
                                             m == (0, NG * KD - 1)[a])
                            ins.then_inc(dm, 1)

                body(0)
                with pe.Fori(1, N_FFN) as i:
                    body(i)

            ffn(0, W_FFN0, 1, 0)

            def v_turn(i, m):
                pe.wait_ge(bv_gelu, i * 12 + m + 1)
                if type(i) is not int or m >= 2:
                    pe.wait_ge(bv_tok, i * 12 + (m - 1))
                for c in range(TPG):
                    ins = pe.transpose(bank(6 + m % 2)[:, c * P:(c + 1) * P],
                                       t_b[:, m % 2, c * P:(c + 1) * P], ident[:, :])
                ins.then_inc(bv_tr, 1)

            for _ in range(2):
                pe.drain().then_inc(bv_tr, 1)
            for n in range(12):
                u, g = n // 3, n % 3
                if g == 0:
                    pe.wait_ge(split, W_BV.count(0, u, 1))
                if u == 0:
                    xn_ready(2, g)
                if n == 0:
                    pe.wait_ge(d_add[0], 6 + 24 * N_FFN)
                if n >= 6:
                    pe.wait_ge(bv_gelu, n - 6 + 1)
                unit_piece(W_BV, u, g, n % 6).then_inc(bv_mm, 1)
                if n == 3:
                    row_sums(2)
                if n == 4:
                    widen(1, lambda g: sq_f[:, g, :])
                    pe.wait_ge(r_ready, NG * 2)
                for m in range(min(2 * (n - 5), n - 1), min(2 * (n - 4), n)):
                    if n >= 5:
                        v_turn(0, m)
            with pe.Fori(1, NF // 4) as i:
                for u in range(4):
                    pe.wait_ge(split, W_BV.count(i, u, 1))
                    for g in range(NG):
                        n = 3 * u + g
                        pe.wait_ge(bv_gelu, i * 12 + (n - 5))
                        unit_piece(W_BV, u, g, n % 6).then_inc(bv_mm, 1)
                        if n == 0:
                            v_turn(i - 1, 11)
                        else:
                            v_turn(i, n - 1)

            def u_piece(i, n):
                u, g = n // 3, n % 3
                if g == 0:
                    pe.wait_ge(split, W_BU.count(i, u, 1))
                pe.wait_ge(bu_gate, i * 12 + (n + 1))
                unit_piece(W_BU, u, g, n % 6).then_inc(bu_mm, 1)

            for n in range(6):
                pe.wait_ge(bv_gelu, 12 * (NF // 4) - 6 + n + 1)
                u_piece(0, n)
                if n == 0:
                    v_turn(NF // 4 - 1, 11)
            pe.wait_ge(b_loaded, 16 * (1 + DEC_B))
            pe.wait_ge(bv_tok, 12 * (NF // 4))
            pe.wait_ge(bw_copied, 1)
            for a, src in enumerate((w_s_in, w_s_smp)):
                for g in range(G_B):
                    ins = pe.transpose(ps[6 + a][:, g * P:(g + 1) * P], src[:, g, :], ident[:, :])
                ins.then_inc(bw_tr, 1)
            pe.wait_ge(mix_ok, 1)
            for c in range(NT):
                if c in LN_ACT:
                    pe.wait_ge(ln_act, LN_ACT.index(c) + 1)
                else:
                    pe.wait_ge(ln_dve, LN_DVE.index(c) + 1)
                for q in range(4):
                    t = 4 * c + q
                    if t >= 2:
                        pe.wait_ge(mx_act if t % 2 else mx_dve, t // 2)
                    for k in range(FPG):
                        f = FPG * q + k
                        ins = pe.matmul(ps[6 + t % 2][:, k * P:(k + 1) * P], vs[:, c, f, :], mix[:, c // NP, q, :],
                                        start=True, stop=True)
                    ins.then_inc(mx_mm, 1)
            pe.wait_ge(mx_act, 2 * NT)
            pe.wait_ge(mx_dve, 2 * NT)
            widen(2, lambda g: t_b[:, g % 2, :])
            for n in range(6, 12):
                u_piece(0, n)
            with pe.Fori(1, NF // 4) as i:
                for n in range(12):
                    u_piece(i, n)
            with pe.Fori(0, KD // 2) as i:
                for u in range(4):
                    j, a = u // 2, u % 2
                    pe.wait_ge(split, W_BO.count(i, u, 1))
                    for g in range(NG):
                        pe.wait_ge(ps_lo, FPG // 2 * (NG * a + g + 1))
                        if a == 0:
                            pe.wait_ge(bo_add, i * 6 + 3 * j + g + 1)
                        ins = passes(bank(3 * j + g), W_BO.slots[u], range(KD),
                                     lambda k: tok(p_hi[:, KD * a + k, :], g),
                                     lambda k: p_lo[:, TPG * g:TPG * (g + 1), KD * a + k, :], a == 0, a == 1, g == 0)
                        if a == 1:
                            ins.then_inc(bo_mm, 1)

            ffn(1, W_FFN1, 3, 3)

            pe.wait_ge(d_add[1], 6 + 24 * N_FFN)
            for c in range(NT):
                for half in range(2):
                    t = 2 * c + half
                    if t == 6:
                        row_sums(4)
                        pe.wait_ge(r_done, 4)
                    if t >= 8:
                        pe.wait_ge(yt_act if half else yt_dve, (t - 8) // 2 + 1)
                    pe.wait_ge(n_full, KD * (c // TPG + 1))
                    for k in range(4):
                        ins = pe.transpose(ps[t % 8][:, k * P:(k + 1) * P],
                                           x_gain[:, 4 * half + k, c * P:(c + 1) * P], ident[:, :])
                    ins.then_inc(yt_pe, 1)

        @block.scalar
        def _(act):
            def norm0():
                for g in range(NG):
                    if g:
                        act.wait_ge(n_lo, KD * g)
                    act.activation(sq_a[:, :, :], tok(xT[:, :, :], g), ACT.Square).then_inc(squared, 1)
                    act.wait_ge(mean_sq, g + 1)
                    act.activation(rstd_a[:, :], bank(6 + g % 2), ACT.Sqrt, bias=eps_t[:, :], scale=1.0 / D)\
                        .then_inc(rooted, 1)
                    for k in range(KD):
                        act.wait_ge(xn_full, KD * g + k + 1)
                        act.activation(tok(xn_hi[:, k, :], g), sq_a[:, k, :], ACT.Copy).then_inc(n_hi, 1)

            def norm(n, gain, added, base, late=None):
                done = 0
                for g in range(NG):
                    for k in range(KD):
                        act.wait_ge(added, base + KD * g + k + 1)
                        out, says = (xn_hi, n_hi) if n < 4 else (x_gain, n_full)
                        act.activation(tok(out[:, k, :], g), tok(xT[:, k, :], g), ACT.Copy,
                                       scale=gains[:, gain + k:gain + k + 1]).then_inc(says, 1)
                    if late is None or g == NG - 1:
                        if late is not None:
                            late()
                        while done <= g:
                            if done:
                                act.wait_ge(summed, NG * n + done)
                            act.activation(sq_f[:, :, :], tok(xT[:, :, :], done), ACT.Square).then_inc(squared, 1)
                            done += 1
                act.wait_ge(r_sum, n if n < 4 else 4)
                act.activation(r_tok[:, :], bank(6, NT), ACT.Sqrt, bias=eps_t[:, :], scale=1.0 / D)\
                    .then_inc(r_root, 1)

            for c in range(NT):
                act.wait_ge(xt_pe, 2 * c + 2)
                act.activation(xT[:, 4:8, c * P:(c + 1) * P],
                               ps[(2 * c + 1) % 8][:, :].rearrange("p (k t) -> p k t", k=4), ACT.Copy)\
                    .then_inc(xt_act, 1)
            act.wait_ge(const_ok, 1)
            act.wait_ge(xt_dve, NT + 1)
            act.wait_ge(xt_act, NT)
            norm0()
            for g in range(NG):
                act.wait_ge(gt_mm, g + 1)
                if g == 0:
                    act.wait_ge(small_loaded, 32)
                    act.activation(g_bias[:, :], g_bias[:, :], ACT.Copy, scale=1.0 / CAP).then_inc(act_step, 1)
                    act.wait_ge(act_step, 1)
                act.activation(tok(gT[0:2 * H, :], g), bank(g)[0:2 * H, :], ACT.Tanh, bias=g_bias[:, :],
                               scale=1.0 / CAP).then_inc(gt_act, 1)
            act.wait_ge(gt_scaled, 2)
            act.activation(small[:, 1, :, :], small[:, 1, :, :], ACT.Exp, scale=-1.0).then_inc(act_step, 1)
            act.wait_ge(act_step, 2)
            act.activation(small[:, 1, :, :], small[:, 1, :, :], ACT.Ln, bias=ones[:, 0:1]).then_inc(gate_act, 1)
            act.wait_ge(gt_scaled, 3)
            act.activation(pack[:, :, Q_WI:NQ, :], pack[:, :, Q_WI:NQ, :], ACT.Exp).then_inc(gate_act, 1)
            act.wait_ge(gate_act, 2)

            act.drain().then_inc(c_stored, 1)
            with act.Fori(0, H) as h:
                for g in range(NG):
                    act.wait_ge(a_mm, h * 15 + g + 1)
                    act.activation(tok(qT[:, :], g), bank(g), ACT.Copy, scale=float(DK) ** -0.5).then_inc(a_evac, 1)
                for g in range(NG):
                    act.wait_ge(a_mm, h * 15 + 3 + g + 1)
                    act.activation(tok(kT[:, :], g), bank(3 + g), ACT.Copy).then_inc(a_evac, 1)
                for n in range(6):
                    act.wait_ge(a_tr, h * 9 + 3 + n + 1)
                    g, j = n % 3, n // 3
                    act.activation(v_tok[:, g * TPG:(g + 1) * TPG, j * P:(j + 1) * P], tiles(bank(6 + (3 + n) % 2)),
                                   ACT.Copy).then_inc(a_vtok, 1)
                for g in range(NG):
                    act.wait_ge(a_mm, h * 15 + 12 + g + 1)
                    act.activation(tok(sig_o[:, 0, :], g), bank(g), ACT.Sigmoid).then_inc(a_sig, 1)
                for g in range(NG):
                    act.wait_ge(a_dargs, h * 3 + g + 1)
                    act.activation(dmat[:, g * TPG:(g + 1) * TPG, :], dmat[:, g * TPG:(g + 1) * TPG, :], ACT.Exp)\
                        .then_inc(a_exp, 1)
                for k in range(4):
                    t = ticket("ctr", k)
                    act.wait_ge(t_pe, h * NTICK + t + 1)
                    act.activation(c_smp[:, 2 * k:2 * k + 2, 0:DV],
                                   ps[t % 8][:, :].rearrange("p (b v) -> p b v", b=2), ACT.Copy).then_inc(t_act, 1)
                t = ticket("nt")
                act.wait_ge(t_pe, h * NTICK + t + 1)
                act.activation(c_smp[:, :, DV], ps[t % 8][:, 0:DEC_B], ACT.Copy).then_inc(t_act, 1)
                t = ticket("cfin")
                act.wait_ge(t_dve, h * N_DVE + taken(ticket("u", NP - 1)))
                act.wait_ge(c_stored, h * 80 + 1)
                act.activation(c_out[:, 2, 0:1], state[:, NP, DV:DV + 1], ACT.Copy).then_inc(act_step, 1)
                act.wait_ge(t_pe, h * NTICK + t + 1)
                act.activation(c_out[:, 0:2, :], ps[t % 8][:, 0:DV].rearrange("p (j v) -> p j v", j=2), ACT.Copy)\
                    .then_inc(t_act, 1)
                for c in range(NT):
                    act.wait_ge(t_dve, h * N_DVE + taken(ticket("pv", c)))
                    act.activation(v_tok[:, c, 0:DV], num[:, c, 0:DV], ACT.Square, accum_out=nstat[:, 0, c:c + 1])\
                        .then_inc(a_ssq, 1)
                act.wait_ge(a_dve, h * 2 + 2)
                act.wait_ge(a_fac, h + 1)
                act.wait_ge(a_sqrt, h * 2 + 1)
                act.activation(nstat[:, 3, :], nstat[:, 2, :], ACT.Sqrt, bias=eps_t[:, :], scale=1.0 / DV)\
                    .then_inc(a_sqrt, 1)
                for g in range(NG):
                    t = ticket("o", g)
                    act.wait_ge(t_pe, h * NTICK + t + 1)
                    act.activation(tok(sig_o[:, 1, :], g), bank(t), ACT.Sigmoid).then_inc(t_act, 1)

            def ffn(layer):
                with act.Fori(0, N_FFN) as i:
                    for c in range(2):
                        for g in range(NG):
                            act.wait_ge(g_scaled[layer], i * 6 + 3 * c + g + 1)
                            act.activation(silu[:, c, g, :], bank(g), ACT.Silu).then_inc(g_silu[layer], 1)

            norm(1, G_FFN, wd_add, 6 + 24 * (H - 1), lambda: act.wait_ge(c_stored, 80 * H + 1))
            ffn(0)
            norm(2, G_MIX + KD, d_add[0], 6 + 24 * (N_FFN - 1))
            with act.Fori(0, NF // 4) as i:
                for n in range(12):
                    act.wait_ge(bv_scaled, i * 12 + n + 1)
                    act.wait_ge(bv_tr, i * 12 + n + 1)
                    act.activation(t_b[:, n % 2, :], bank(n % 6), ACT.Gelu_apprx_tanh).then_inc(bv_gelu, 1)
            act.wait_ge(ln_stat, 1)
            act.activation(rs_v[:, :, 0], mv[:, :, 1], ACT.Sqrt, bias=eps_t[:, :]).then_inc(ln_root, 1)
            act.wait_ge(ln_scale, 1)
            for c in LN_ACT:
                tile = vs[:, c, :, :].rearrange("p f t -> p (f t)")
                act.activation(tile, tile, ACT.Identity, scale=rs_v[:, c, 1:2], bias=rs_v[:, c, 2:3])\
                    .then_inc(ln_act, 1)
            act.wait_ge(ln_act, len(LN_ACT))
            for c in range(NT):
                for q in range(1, 4, 2):
                    t = 4 * c + q
                    act.wait_ge(mx_mm, t + 1)
                    if c == NP:
                        act.wait_ge(gv_done, 4)
                    act.activation(vs[:, c, FPG * q:FPG * (q + 1), :],
                                   ps[6 + t % 2][:, :].rearrange("p (f t) -> p f t", f=FPG), ACT.Copy)\
                        .then_inc(mx_act, 1)
            with act.Fori(0, NF // 4) as i:
                for n in range(12):
                    act.wait_ge(bu_scaled, i * 12 + n + 1)
                    act.activation(bank(n % 6), bank(n % 6), ACT.Gelu_apprx_tanh).then_inc(bu_gelu, 1)
            act.wait_ge(bu_gate, 6 + 12 * (NF // 4))
            for a, g, q in P_ORDER:
                for f in range(4 * q, 4 * q + 4):
                    ins = act.activation(tiles(tok(p_hi[:, f, :], g)), vs[:, g * TPG:(g + 1) * TPG, f, :], ACT.Copy)
                ins.then_inc(ps_hi, 1)
            act.wait_ge(bo_add, 6 + NG * KD)
            norm(3, G_FFN + KD, bo_add, 6)
            ffn(1)
            norm(4, G_FINAL, d_add[1], 6 + 24 * (N_FFN - 1))
            act.wait_ge(r_done, 4)
            for c in range(NT):
                act.wait_ge(yt_pe, 2 * c + 2)
                act.activation(y_out[:, c, D // 2:D], ps[(2 * c + 1) % 8][:, :], ACT.Copy, scale=r_tok[:, c:c + 1]).then_inc(yt_act, 1)

        @block.vector
        def _(dve):
            n_link = 0

            def link(ins):
                nonlocal n_link
                n_link += 1
                ins.then_inc(dve_step, 1)
                dve.wait_ge(dve_step, n_link)

            def norm0():
                for g in range(NG):
                    dve.wait_ge(squared, g + 1)
                    link(dve.tensor_tensor(sq_a[:, 0:4, :], sq_a[:, 0:4, :], sq_a[:, 4:8, :], ALU.add))
                    link(dve.tensor_tensor(sq_a[:, 0:2, :], sq_a[:, 0:2, :], sq_a[:, 2:4, :], ALU.add))
                    dve.tensor_tensor(ssum_a[:, :], sq_a[:, 0, :], sq_a[:, 1, :], ALU.add).then_inc(summed, 1)
                    dve.wait_ge(rooted, g + 1)
                    link(dve.reciprocal(rstd_a[:, :], rstd_a[:, :]))
                    for k in range(KD + 1):
                        if k < KD:
                            dve.scalar_tensor_tensor(sq_a[:, k, :], tok(xT[:, k, :], g),
                                                     gains[:, G_MIX + k:G_MIX + k + 1], rstd_a[:, :],
                                                     ALU.mult, ALU.mult).then_inc(xn_full, 1)
                        if k >= 1:
                            dve.wait_ge(n_hi, KD * g + k)
                            dve.tensor_tensor(tok(xn_lo[:, k - 1, :], g), sq_a[:, k - 1, :],
                                              tok(xn_hi[:, k - 1, :], g).bitcast(F32), ALU.subtract).then_inc(n_lo, 1)

            def add_up(n, g):
                dve.wait_ge(squared, NG * n + g + 1)
                link(dve.tensor_tensor(sq_f[:, 0:4, :], sq_f[:, 0:4, :], sq_f[:, 4:8, :], ALU.add))
                dve.tensor_tensor(tok(ssum_f[:, :, :], g), sq_f[:, 0:2, :], sq_f[:, 2:4, :], ALU.add)\
                    .then_inc(summed, 1)

            def invert(k):
                dve.wait_ge(r_root, k)
                dve.reciprocal(r_tok[:, :], r_tok[:, :]).then_inc(r_done, 1)
                dve.wait_ge(r_done, k)

            def widen(k, dst, buf, buffers):
                for g in range(NG):
                    if g >= buffers:
                        dve.wait_ge(r_wide, NG * k + g - buffers + 1)
                    dve.tensor_tensor(tiles(buf(g)), ident[:, :].unsqueeze(1).to_broadcast([P, TPG, P]),
                                      r_tok[:, g * TPG:(g + 1) * TPG].unsqueeze(2).to_broadcast([P, TPG, P]),
                                      ALU.mult).then_inc(r_diag, 1)
                for g in range(NG):
                    dve.wait_ge(r_wide, NG * k + g + 1)
                    dve.tensor_copy(tok(dst[:, :], g), bank(7 - g % 2)).then_inc(r_ready, 1)
                dve.wait_ge(r_ready, NG * k + NG)

            def norm(n, gain, k, dst):
                for g in range(NG):
                    for j in range(KD):
                        dve.wait_ge(n_hi, KD * (NG * n + g) + j + 1)
                        dve.scalar_tensor_tensor(tok(xn_lo[:, j, :], g), tok(xT[:, j, :], g),
                                                 gains[:, gain + j:gain + j + 1],
                                                 tok(xn_hi[:, j, :], g).bitcast(F32), ALU.mult, ALU.subtract)\
                            .then_inc(n_lo, 1)
                    if n != 1:
                        add_up(n, g)
                if n == 1:
                    for g in range(NG):
                        add_up(n, g)
                invert(n)
                widen(k, dst, lambda g: sq_f[:, g, :], 3)

            for c in range(NT):
                dve.wait_ge(xt_pe, 2 * c + 1)
                dve.tensor_copy(xT[:, 0:4, c * P:(c + 1) * P],
                                ps[(2 * c) % 8][:, :].rearrange("p (k t) -> p k t", k=4)).then_inc(xt_dve, 1)
            dve.wait_ge(xt_pe, 2 * NT + 1)
            dve.tensor_copy(gains[:, :], ps[2][:, 0:G_ALL]).then_inc(xt_dve, 1)
            dve.wait_ge(xt_dve, NT + 1)
            norm0()

            lf, tmp, a, cm = (small[:, k, :, :] for k in range(4))
            bt, mp, mt, mn = (small[:, k, :, :] for k in range(4, 8))
            dve.wait_ge(gt_act, NG)
            dve.tensor_scalar(gT[0:2 * H, :], gT[0:2 * H, :], CAP, None, ALU.mult).then_inc(gt_scaled, 1)
            dve.wait_ge(gt_tr, 1)
            link(dve.tensor_copy(gtok[:, :, :].rearrange("p c g -> p (c g)"), ps[3][:, 0:NT * 2 * H]))
            ig = gtok[:, :, 0:H].rearrange("p c h -> p h c")
            fg = gtok[:, :, H:2 * H].rearrange("p c h -> p h c")
            link(dve.tensor_scalar(lf, fg, -1.0, None, ALU.mult))
            dve.tensor_tensor(tmp, lf, fg, ALU.max).then_inc(gt_scaled, 1)
            dve.wait_ge(gate_act, 1)
            link(dve.tensor_scalar(lf, fg, 0.0, None, ALU.min))
            dve.tensor_tensor(lf, lf, tmp, ALU.subtract).then_inc(gate_dve, 1)
            dve.wait_ge(gate_pe, 1)
            link(dve.tensor_copy(bt, ps[4][:, 0:H * NT].rearrange("p (h c) -> p h c", h=H)))
            dve.tensor_tensor(a, ig, bt, ALU.subtract).then_inc(gate_dve, 1)
            dve.wait_ge(gate_pe, 2)
            link(dve.tensor_copy(aT[0:H * NT, 0:P], ps[5][0:H * NT, 0:P]))
            dve.tensor_tensor_scan(aT[0:H * NT, P:2 * P], reset[:, :], aT[0:H * NT, 0:P], -BIG, ALU.min, ALU.max)\
                .then_inc(gate_dve, 1)
            dve.wait_ge(gate_pe, 3)
            dve.tensor_copy(cm, ps[6][:, 0:H * NT].rearrange("p (h c) -> p h c", h=H)).then_inc(gate_dve, 1)
            dve.wait_ge(gate_pe, 4)
            bl, cml = tmp, lf
            link(dve.tensor_copy(bl, ps[4][:, 64:64 + H * NT].rearrange("p (h c) -> p h c", h=H)))
            link(dve.tensor_copy(cml, ps[7][:, 0:H * NT].rearrange("p (h c) -> p h c", h=H)))
            link(dve.memset(mp[:, :, 0:1], 0.0))
            link(dve.tensor_copy(mp[:, :, NP], m_in[:, :]))
            for hh in range(H):
                link(dve.tensor_tensor_scan(mn[:, hh, 0:NP], cml[:, hh, 0:NP], bl[:, hh, 0:NP], 0.0, ALU.max, ALU.add))
            link(dve.tensor_copy(mp[:, :, 1:NP], mn[:, :, 0:NP - 1]))
            ml = cml
            link(dve.tensor_tensor(ml, mp, cml, ALU.max))
            link(dve.tensor_tensor(mn[:, :, NP], ml[:, :, NP], bl[:, :, NP], ALU.add))
            link(dve.tensor_tensor(pack[:, :, Q_M, :], mp, cm, ALU.max))
            dve.tensor_copy(pack[:, :, Q_A, :], a)
            dve.tensor_copy(m_out[:, 0, :], mn[:, :, NP - 1])
            link(dve.tensor_copy(m_out[:, 1, :], mn[:, :, NP]))
            dve.tensor_tensor(pack[:, :, Q_WI, :], mp, pack[:, :, Q_M, :], ALU.subtract)
            link(dve.tensor_tensor(mt, bt, pack[:, :, Q_M, :], ALU.add))
            dve.tensor_scalar(pack[:, :, Q_EMT, :], mt, -1.0, None, ALU.mult)
            dve.tensor_tensor(pack[:, :, Q_WS, :], a, ml, ALU.subtract)
            dve.tensor_tensor(pack[:, :, Q_DECAY, :], mp, ml, ALU.subtract)
            dve.drain().then_inc(gt_scaled, 1)
            dve.wait_ge(gate_act, 2)
            dve.tensor_tensor(dmat[:, 0, 0:H * DEC_B].rearrange("p (h b) -> p h b", h=H),
                              b_first[:, :].unsqueeze(1).to_broadcast([P, H, DEC_B]),
                              pack[:, :, Q_DECAY, NP].unsqueeze(2).to_broadcast([P, H, DEC_B]), ALU.mult)\
                .then_inc(gate_dve, 1)
            dve.wait_ge(gate_pe, 5)
            dve.tensor_copy(dec_s[:, :, :].rearrange("p h b -> p (h b)"), ps[3][:, 128:128 + H * DEC_B])
            dve.tensor_copy(dec8[0:DEC_B, :], ps[3][0:DEC_B, 192:192 + H])
            dve.tensor_scalar(tri[:, :], tri[:, :], -BIG, BIG, ALU.mult, ALU.add)
            dve.tensor_scalar(tri_s[:, :], tri_s[:, :], -BIG, BIG, ALU.mult, ALU.add)
            link(dve.memset(v_tok[:, :, DV:DV + 1], 1.0))
            dve.drain().then_inc(gate_dve, 1)

            HS = 24
            base = n_link
            for _ in range(6):
                dve.drain().then_inc(wd_add, 1)
            dve.drain().then_inc(a_fac, 1)
            with dve.Fori(0, H) as h:
                step = 0

                def hlink(ins):
                    nonlocal step
                    step += 1
                    ins.then_inc(dve_step, 1)
                    dve.wait_ge(dve_step, h * HS + (base + step))

                hlink(dve.tensor_copy(cur[:, :, :].rearrange("p q c -> p (q c)"),
                                      pack[:, :, :, :].rearrange("p h q c -> p (h q c)")[:, bass.ds(h * (NQ * NT), NQ * NT)]))
                dve.tensor_copy(g_h[:, :], gains[:, bass.ds(h * 2 + G_OUT, 2)])
                dve.tensor_copy(nstat[:, 4, 0:DEC_B], dec_s[:, :, :].rearrange("p h b -> p (h b)")[:, bass.ds(h * DEC_B, DEC_B)])
                hlink(dve.tensor_copy(nstat[0:DEC_B, 5, 0:1], dec8[0:DEC_B, bass.ds(h, 1)]))

                def q(k):
                    return cur[:, k, :].unsqueeze(2)

                for n in range(3):
                    g = n
                    dve.wait_ge(a_tr, h * 9 + n + 1)
                    dve.tensor_tensor(k_tok[:, g * TPG:(g + 1) * TPG, :], tiles(bank(6 + n % 2)),
                                      q(Q_WS)[:, g * TPG:(g + 1) * TPG, :].to_broadcast([P, TPG, P]), ALU.mult)\
                        .then_inc(a_ktok, 1)
                    dve.wait_ge(a_mm, h * 15 + 6 + n + 1)
                    if n >= 2:
                        dve.wait_ge(a_tr, h * 9 + 3 + n - 2 + 1)
                    dve.tensor_copy(v_tmp[:, (n + 1) % 2 * TG:((n + 1) % 2 + 1) * TG], bank(n)).then_inc(a_vtmp, 1)
                for n in range(3, 6):
                    dve.wait_ge(a_mm, h * 15 + 6 + n + 1)
                    dve.wait_ge(a_tr, h * 9 + 3 + n - 2 + 1)
                    dve.tensor_copy(v_tmp[:, (n + 1) % 2 * TG:((n + 1) % 2 + 1) * TG], bank(n)).then_inc(a_vtmp, 1)
                dve.tensor_tensor(k_blk, k_tok[:, NP, :].unsqueeze(1).to_broadcast([P, DEC_B, DK]),
                                  b_mem[:, :].unsqueeze(2).to_broadcast([P, DEC_B, DK]), ALU.mult).then_inc(a_kb, 1)
                eye = ident[:, :].unsqueeze(1).to_broadcast([P, NT, P])
                dve.tensor_tensor(diag, eye, q(Q_M).to_broadcast([P, NT, P]), ALU.mult).then_inc(a_diag, 1)
                dve.tensor_tensor(diag2, eye, q(Q_WI).to_broadcast([P, NT, P]), ALU.mult).then_inc(a_diag, 1)
                dve.wait_ge(a_tr, h * 9 + 9)
                for g in range(NG):
                    t = ticket("mb", g)
                    dve.wait_ge(t_pe, h * NTICK + t + 1)
                    part = dmat[:, g * TPG:(g + 1) * TPG, :]
                    if g < NG - 1:
                        ins = dve.tensor_tensor(part, tri[:, :].unsqueeze(1).to_broadcast([P, TPG, P]), tiles(bank(t)),
                                                ALU.add)
                    else:
                        dve.tensor_tensor(part[:, 0:2, :], tri[:, :].unsqueeze(1).to_broadcast([P, 2, P]),
                                          tiles(bank(t))[:, 0:2, :], ALU.add)
                        ins = dve.tensor_tensor(part[:, 2, :], tri_s[:, :], tiles(bank(t))[:, 2, :], ALU.add)
                    ins.then_inc(t_dve, 1)
                    dve.wait_ge(t_dve, h * N_DVE + taken(t))
                    dve.tensor_tensor(part, q(Q_A)[:, g * TPG:(g + 1) * TPG, :].to_broadcast([P, TPG, P]), part,
                                      ALU.subtract).then_inc(a_dargs, 1)
                for g in range(NG):
                    t = ticket("wib", g)
                    dve.wait_ge(t_pe, h * NTICK + ticket("wib", NG - 1) + 1)
                    dve.tensor_tensor(tok(qw[:, :], g), tok(qT[:, :], g), bank(t), ALU.mult).then_inc(t_dve, 1)
                dve.wait_ge(t_dve, h * N_DVE + taken(ticket("wib", NG - 1)))
                for g in range(NG):
                    t = ticket("s", g)
                    dve.wait_ge(t_pe, h * NTICK + t + 1)
                    dve.wait_ge(a_exp, h * 3 + g + 1)
                    part = dmat[:, g * TPG:(g + 1) * TPG, :]
                    dve.tensor_tensor(part, part, tiles(bank(t)), ALU.mult).then_inc(t_dve, 1)
                hlink(dve.memset(state[:, 0, :], 0.0))
                for c in range(NP):
                    t = ticket("u", c)
                    dve.wait_ge(t_pe, h * NTICK + t + 1)
                    dve.scalar_tensor_tensor(state[:, c + 1, :], state[:, c, :], cur[:, Q_DECAY, c:c + 1],
                                             bank(t, DV + 1), ALU.mult, ALU.add).then_inc(t_dve, 1)
                    dve.wait_ge(t_dve, h * N_DVE + taken(t))
                for j in range(2):
                    for half in range(2):
                        t = ticket("us", 2 * j + half)
                        bs = slice(4 * half, 4 * half + 4)
                        dve.wait_ge(t_pe, h * NTICK + t + 1)
                        hlink(dve.tensor_tensor(c_nat[:, j, bs, :], c_nat[:, j, bs, :],
                                                nstat[:, 4, bs].unsqueeze(2).to_broadcast([P, 4, DK]), ALU.mult))
                        dve.tensor_tensor(c_nat[:, j, bs, :], c_nat[:, j, bs, :],
                                          ps[t % 8][:, :].rearrange("p (b d) -> p b d", b=4), ALU.add)\
                            .then_inc(t_dve, 1)
                t = ticket("un")
                dve.wait_ge(t_pe, h * NTICK + t + 1)
                dve.scalar_tensor_tensor(n_nat[:, :], n_nat[:, :], nstat[0:DEC_B, 5, 0:1], ps[t % 8][0:DEC_B, 0:DK],
                                         ALU.mult, ALU.add).then_inc(t_dve, 1)
                hlink(dve.memset(q_blk[:, :, :], 0.0))
                for b in range(DEC_B):
                    sl = slice(b * DEC_S, (b + 1) * DEC_S)
                    ins = dve.tensor_copy(q_blk[:, b, sl], qw[:, NP * P + b * DEC_S:NP * P + (b + 1) * DEC_S])
                ins.then_inc(a_dve, 1)
                dve.drain().then_inc(a_dve, 1)
                for c in range(NT):
                    t = ticket("pv", c)
                    dve.wait_ge(t_pe, h * NTICK + t + 1)
                    dve.tensor_copy(num[:, c, :], bank(t, DV + 1)).then_inc(t_dve, 1)
                dve.wait_ge(t_dve, h * N_DVE + taken(ticket("pv", NT - 1)))
                ssq, r, t2, std = (nstat[:, k, :] for k in range(4))
                den = num[:, :, DV]
                hlink(dve.tensor_scalar(r, den, -1.0, None, ALU.mult))
                hlink(dve.tensor_tensor(r, r, den, ALU.max))
                hlink(dve.tensor_tensor(r, r, cur[:, Q_EMT, :], ALU.max))
                hlink(dve.reciprocal(r, r))
                dve.wait_ge(a_ssq, h * NT + NT)
                hlink(dve.tensor_tensor(t2, ssq, r, ALU.mult))
                dve.tensor_tensor(t2, t2, r, ALU.mult).then_inc(a_sqrt, 1)
                dve.wait_ge(a_sqrt, h * 2 + 2)
                hlink(dve.reciprocal(std, std))
                hlink(dve.tensor_tensor(r, r, std, ALU.mult))
                dve.tensor_tensor(num[:, :, 0:DV], num[:, :, 0:DV], r.unsqueeze(2).to_broadcast([P, NT, DV]), ALU.mult)\
                    .then_inc(a_fac, 1)
                for g in range(NG):
                    for j in range(2):
                        t = ticket("ht", 2 * g + j)
                        buf = h_f[:, j * TG:(j + 1) * TG]
                        dve.wait_ge(t_pe, h * NTICK + t + 1)
                        if j == 1:
                            dve.wait_ge(t_act, h * N_ACT + taken(ticket("o", g)))
                        dve.scalar_tensor_tensor(buf, bank(t), g_h[:, j:j + 1], tok(sig_o[:, j, :], g),
                                                 ALU.mult, ALU.mult).then_inc(t_dve, 1)
                        dve.wait_ge(t_dve, h * N_DVE + taken(t))
                        hlink(dve.tensor_copy(tok(h_hi[:, j, :], g), buf))
                        dve.tensor_tensor(tok(h_lo[:, j, :], g), buf, tok(h_hi[:, j, :], g).bitcast(F32),
                                          ALU.subtract).then_inc(a_hlo, 1)
                for n in range(24):
                    g, j = n // KD, n % KD
                    dve.wait_ge(wd_mm, h * 24 + n + 1)
                    dve.tensor_tensor(tok(xT[:, j, :], g), tok(xT[:, j, :], g), bank(n % 6), ALU.add).then_inc(wd_add, 1)
                while step < HS:
                    hlink(dve.memset(nstat[:, 2, 0:1], 0.0))
                assert step == HS, step
            n_link = base + HS * H

            def ffn(layer, n, k):
                for _ in range(6):
                    dve.drain().then_inc(d_add[layer], 1)
                norm(n, G_FFN + KD * layer, k, rstd_f)
                with dve.Fori(0, N_FFN) as i:
                    for c in range(2):
                        for g in range(NG):
                            m = 3 * c + g
                            dve.wait_ge(g_mm[layer], i * 6 + m + 1)
                            dve.tensor_tensor(bank(g), bank(g), tok(rstd_f[:, :], g), ALU.mult)\
                                .then_inc(g_scaled[layer], 1)
                        for g in range(NG):
                            m = 3 * c + g
                            buf = h_tmp[:, m % 2, :]
                            dve.wait_ge(g_silu[layer], i * 6 + m + 1)
                            dve.tensor_tensor(silu[:, c, g, :], silu[:, c, g, :], tok(rstd_f[:, :], g), ALU.mult)\
                                .then_inc(s_scaled[layer], 1)
                            dve.wait_ge(s_scaled[layer], i * 6 + m + 1)
                            dve.wait_ge(u_mm[layer], i * 6 + m + 1)
                            dve.tensor_tensor(buf, silu[:, c, g, :], bank(3 + g), ALU.mult).then_inc(h_full[layer], 1)
                            dve.wait_ge(h_full[layer], i * 6 + m + 1)
                            dve.tensor_copy(tok(hg_hi[:, c, :], g), buf).then_inc(h_his[layer], 1)
                            dve.wait_ge(h_his[layer], i * 6 + m + 1)
                            dve.tensor_tensor(tok(hg_lo[:, c, :], g), buf, tok(hg_hi[:, c, :], g).bitcast(F32),
                                              ALU.subtract).then_inc(h_los[layer], 1)
                    for m in range(24):
                        g, j = m // KD, m % KD
                        dve.wait_ge(d_mm[layer], i * 24 + m + 1)
                        dve.tensor_tensor(tok(xT[:, j, :], g), tok(xT[:, j, :], g), bank(m % 6), ALU.add)\
                            .then_inc(d_add[layer], 1)

            ffn(0, 1, 0)
            norm(2, G_MIX + KD, 1, rstd_b)
            for _ in range(6):
                dve.drain().then_inc(bu_gate, 1)
            vrow = vs[:, :, :, :].rearrange("p c f t -> p c (f t)")
            with dve.Fori(0, NF // 4) as i:

                def scale_v(n):
                    dve.wait_ge(bv_mm, i * 12 + n + 1)
                    dve.tensor_tensor(bank(n % 6), bank(n % 6), tok(rstd_b[:, :], n % 3), ALU.mult)\
                        .then_inc(bv_scaled, 1)

                scale_v(0)
                for n in range(12):
                    u, g = n // 3, n % 3
                    if n < 11:
                        scale_v(n + 1)
                    dve.wait_ge(bv_tr, i * 12 + n + 3)
                    dve.tensor_copy(vs[:, g * TPG:(g + 1) * TPG, bass.ds(i * 4 + u, 1), :].rearrange("p c o t -> p c (o t)"),
                                    tiles(bank(6 + n % 2))).then_inc(bv_tok, 1)
                    if u == 3:
                        dve.wait_ge(bv_tok, i * 12 + n + 1)
                        for c in range(g * TPG, (g + 1) * TPG):
                            ins = dve.bn_stats(stat[:, c, bass.ds(i, 1), :].rearrange("p o s -> p (o s)"),
                                               vrow[:, c, bass.ds(i * (4 * P), 4 * P)])
                        ins.then_inc(bv_stat, 1)
            dve.wait_ge(bv_stat, NG * (NF // 4))
            dve.wait_ge(bv_gelu, 12 * (NF // 4))
            for c in range(NT):
                ins = dve.bn_aggr(mv[:, c, :], stat[:, c, :, :].rearrange("p q s -> p (q s)"))
            ins.then_inc(ln_stat, 1)
            dve.wait_ge(ln_root, 1)
            link(dve.reciprocal(rs_v[:, :, 1], rs_v[:, :, 0]))
            dve.scalar_tensor_tensor(rs_v[:, :, 2], mv[:, :, 0], -1.0, rs_v[:, :, 1], ALU.mult, ALU.mult)\
                .then_inc(ln_scale, 1)
            for c in LN_DVE:
                dve.tensor_scalar(vrow[:, c, :], vrow[:, c, :], mv[:, c, 0:1], rs_v[:, c, 1:2], ALU.subtract, ALU.mult)\
                    .then_inc(ln_dve, 1)
            dve.wait_ge(b_loaded, 16 * (1 + DEC_B))
            link(dve.tensor_copy(mix[:, 0, :, 0:DEC_S], w_s_smp[:, :, 0:DEC_S]))
            for b in range(DEC_B):
                ins = dve.tensor_copy(w_s_smp[:, :, b * DEC_S:(b + 1) * DEC_S], mix[:, 0, :, 0:DEC_S])
            ins.then_inc(bw_copied, 1)
            for t_ in (tri, tri_s):
                link(dve.tensor_scalar(t_[:, :], t_[:, :], 0.0, None, ALU.is_equal))
            for k, t_ in enumerate((tri, tri_s)):
                dve.wait_ge(bw_tr, k + 1)
                ins = dve.tensor_tensor(mix[:, k, :, :], ps[6 + k][:, :].rearrange("p (g t) -> p g t", g=G_B),
                                        t_[:, :].unsqueeze(1).to_broadcast([P, G_B, P]), ALU.mult)
                link(ins)
            dve.drain().then_inc(bw_copied, 1)
            dve.drain().then_inc(mix_ok, 1)

            def gain_rows_of_v(q):
                dve.wait_ge(gv_loaded[q % 2], 16 * (q // 2 + 1))
                dve.wait_ge(ln_dve, 1)
                dve.tensor_tensor(row_buf[q % 2], vrow[:, NP, q * RQ:(q + 1) * RQ], row_buf[q % 2], ALU.mult)\
                    .then_inc(gv_done, 1)

            for c in range(NT):
                if c in (3, 7):
                    gain_rows_of_v(c // 4 * 2)
                    gain_rows_of_v(c // 4 * 2 + 1)
                if c == NP:
                    dve.wait_ge(gv_done, 4)
                for q in range(0, 4, 2):
                    t = 4 * c + q
                    dve.wait_ge(mx_mm, t + 1)
                    dve.tensor_copy(vs[:, c, FPG * q:FPG * (q + 1), :],
                                    ps[6 + t % 2][:, :].rearrange("p (f t) -> p f t", f=FPG)).then_inc(mx_dve, 1)
            dve.wait_ge(b_mixed, 16)
            dve.wait_ge(mx_act, 2 * NT)
            dve.wait_ge(row_stored[1], 32)
            widen(2, rstd_b, lambda g: t_b[:, g % 2, :], 2)
            with dve.Fori(0, NF // 4) as i:
                for n in range(12):
                    u, g = n // 3, n % 3
                    piece = vs[:, g * TPG:(g + 1) * TPG, bass.ds(i * 4 + u, 1), :].rearrange("p c o t -> p c (o t)")
                    buf = t_b[:, n % 2, :]
                    gain = gains[:, bass.ds(i * 4 + (G_V + u), 1)]
                    pr = bias_b[:, bass.ds(i, 1), :]
                    sm = pr[:, :, 0:DEC_S].to_broadcast([P, DEC_B, DEC_S])
                    if g < NG - 1:
                        ins = dve.scalar_tensor_tensor(tiles(buf), piece, gain, pr.to_broadcast([P, TPG, P]),
                                                       ALU.mult, ALU.add)
                    else:
                        dve.scalar_tensor_tensor(tiles(buf)[:, 0:2, :], piece[:, 0:2, :], gain,
                                                 pr.to_broadcast([P, 2, P]), ALU.mult, ALU.add)
                        ins = dve.scalar_tensor_tensor(
                            tiles(buf)[:, 2, :].rearrange("p (b s) -> p b s", b=DEC_B),
                            piece[:, 2, :].rearrange("p (b s) -> p b s", b=DEC_B), gain, sm, ALU.mult, ALU.add)
                    ins.then_inc(bu_bias, 1)
                    dve.wait_ge(bu_mm, i * 12 + n + 1)
                    dve.tensor_tensor(bank(n % 6), bank(n % 6), tok(rstd_b[:, :], g), ALU.mult).then_inc(bu_scaled, 1)
                    dve.wait_ge(bu_bias, i * 12 + n + 1)
                    dve.wait_ge(bu_gelu, i * 12 + n + 1)
                    dve.tensor_tensor(piece, tiles(buf), tiles(bank(n % 6)), ALU.mult).then_inc(bu_gate, 1)
            for _ in range(6):
                dve.drain().then_inc(bo_add, 1)
            dve.wait_ge(bu_gate, 6 + 12 * (NF // 4))
            for n, (a, g, q) in enumerate(P_ORDER):
                dve.wait_ge(ps_hi, n + 1)
                for f in range(4 * q, 4 * q + 4):
                    ins = dve.tensor_tensor(p_lo[:, g * TPG:(g + 1) * TPG, f, :], vs[:, g * TPG:(g + 1) * TPG, f, :],
                                            tiles(tok(p_hi[:, f, :], g)).bitcast(F32), ALU.subtract)
                ins.then_inc(ps_lo, 1)
            with dve.Fori(0, KD // 2) as i:
                for n in range(6):
                    j, g = n // 3, n % 3
                    dve.wait_ge(bo_mm, i * 6 + n + 1)
                    out = tok(xT[:, :, :], g)[:, bass.ds(i * 2 + j, 1), :].rearrange("p o t -> p (o t)")
                    dve.tensor_tensor(out, out, bank(n), ALU.add).then_inc(bo_add, 1)

            ffn(1, 3, 3)
            for g in range(NG):
                add_up(4, g)
            invert(4)
            for c in range(NT):
                dve.wait_ge(yt_pe, 2 * c + 1)
                dve.tensor_scalar(y_out[:, c, 0:D // 2], ps[(2 * c) % 8][:, :], r_tok[:, c:c + 1], None, ALU.mult).then_inc(yt_dve, 1)


_INS = ['x_prompt', 'x_sample', 'state_C', 'state_n', 'state_m', 'g_mix', 'g_ffn', 'g_final',
        'a_w_in', 'a_b_gate', 'a_g_out', 'a_w_out', 'b_w_in', 'b_g_v', 'b_w_s', 'b_b_s', 'b_w_out',
        'f_w_gu', 'f_w_down']
_OUTS = [(1, SEQ, D), (DEC_B, DEC_S, D), (1, 1, H, DV, DK), (1, 1, H, DK), (1, 1, H),
         (DEC_B, 1, H, DV, DK), (DEC_B, 1, H, DK), (DEC_B, 1, H), (DEC_B, 1, DEC_S, INNER)]


def kernel(**inputs):
    import numpy as _np
    import concourse.bacc as _bacc
    from concourse.bass_utils import run_bass_kernel_spmd as _run

    nc = _bacc.Bacc("TRN2", target_bir_lowering=False, num_devices=1, dynamic_dma_scratch_size=64)
    arrays, args = {}, []
    for name in _INS:
        a = _np.ascontiguousarray(inputs[name])
        arrays[f"in_{name}_dram"] = a
        args.append(nc.dram_tensor(f"in_{name}_dram", a.shape, mybir.dt.from_np(a.dtype), kind="ExternalInput").ap())
    for i, shape in enumerate(_OUTS):
        args.append(nc.dram_tensor(f"out_{i}_dram", shape, F32, kind="ExternalOutput").ap())
    build(nc, *args)
    r = _run(nc, [arrays], core_ids=[0])
    return tuple(r.results[0][f"out_{i}_dram"] for i in range(len(_OUTS)))
```

```python
from contextlib import ExitStack

import concourse.bass as bass
import concourse.mybir as mybir
from concourse.alu_op_type import AluOpType as ALU

ACT = mybir.ActivationFunctionType
F32 = mybir.dt.float32
F32R = mybir.dt.float32r

P = 128
D = 1024
KD = D // P
SEQ = 1024
DEC_B, DEC_S = 8, 16
NT = (SEQ + DEC_B * DEC_S) // P
NP = SEQ // P
TOK = NT * P
NG = 3
TG = TOK // NG
TPG = NT // NG
H, DK, DV = 4, 128, 256
QK_W, V_W = H * DK, H * DV
A_PROJ = 2 * QK_W + 2 * V_W + 2 * H
CAP = 15.0
INNER = 2 * D
NF = INNER // P
G_B = 4
FPG = NF // G_B
D_FF = 2816
EPS = 1e-6
BIG = 1e30
GATE_BANKS = [6, 7, 5]
FREE_UNITS = 5

G_OUT, G_MIX, G_FFN, G_FINAL, G_V, G_ALL = 0, KD, 3 * KD, 5 * KD, 6 * KD, 6 * KD + NF
Q_A, Q_M, Q_WI, Q_EMT, Q_WS, Q_DECAY, NQ = 0, 1, 2, 3, 4, 5, 6


class WeightPhase:

    def __init__(self, before, iterations, slots, back):
        self.base = before.end if before else 0
        self.n, self.slots = len(slots), slots
        self.end = self.base + iterations * self.n
        self.back = back

    def count(self, i, u, add=0):
        return i * self.n + (self.base + u + add)

    def raw(self, u):
        return (self.base + u) % 2

    def loads(self, i, u):
        return i * (self.n // 2) + ((self.base + u) // 2 + 1)


N_FFN = D_FF // (2 * P)
W_GATES = WeightPhase(None, 1, [0], [5])
W_HEADS = WeightPhase(W_GATES, H, [2, 1, 0, 2, 0, 2, 1, 0], [3, 3, 3, 3, 2, 2, 5, 3])
W_FFN0 = WeightPhase(W_HEADS, N_FFN, [2, 1, 0, 2, 1, 0], [3] * 6)
W_BV = WeightPhase(W_FFN0, NF // 4, [2, 1, 0, 1], [3, 2, 3, 2])
W_BU = WeightPhase(W_BV, NF // 4, [2, 1, 0, 1], [3, 2, 3, 2])
W_BO = WeightPhase(W_BU, KD // 2, [2, 0, 2, 0], [2] * 4)
W_FFN1 = WeightPhase(W_BO, N_FFN, [1, 2, 0, 1, 2, 0], [3] * 6)

P_ORDER = [(g, f) for a in range(2) for g in range(NG) for f in range(KD * a, KD * (a + 1))]

LN_DVE = [NP, 0, 2, 4, 6]
LN_ACT = [1, 3, 5, 7]

TICKETS = (["mb"] * 3 + ["wib"] * 3 + ["s"] * 3 + ["ctr"] * 4 + ["nt"] + ["u"] * NP + ["us"] * 4 + ["un", "cfin"]
           + ["pv"] * NT + ["o"] * 2 + ["ht"] * 2 + ["o"] + ["ht"] * 4)
BY_ACT = {"ctr", "nt", "cfin", "o"}


def ticket(name, k=0):
    return [t for t, x in enumerate(TICKETS) if x == name][k]


def taken(t):
    mine = TICKETS[t] in BY_ACT
    return sum((x in BY_ACT) == mine for x in TICKETS[:t + 1])


NTICK = len(TICKETS)
N_ACT = sum(x in BY_ACT for x in TICKETS)
N_DVE = NTICK - N_ACT


def build(nc, x_prompt, x_sample, state_C, state_n, state_m, g_mix, g_ffn, g_final,
          a_w_in, a_b_gate, a_g_out, a_w_out, b_w_in, b_g_v, b_w_s, b_b_s, b_w_out,
          f_w_gu, f_w_down,
          y_prompt, y_sample, C_prompt, n_prompt, m_prompt, C_sample, n_sample, m_sample, v_rows):
    ctx = ExitStack()
    with ctx:
        def sb(name, shape, dt=F32, stack=ctx):
            return stack.enter_context(nc.sbuf_tensor(name, shape, dt))

        def sem(name):
            return ctx.enter_context(nc.semaphore(name))

        xT = sb("xT", [P, KD, TOK])
        w_raw = [sb(f"w_raw{r}", [P, KD, P]) for r in range(2)]
        w_hi = [sb(f"w_hi{s}", [P, KD, P], F32R) for s in range(3)]
        w_lo = [sb(f"w_lo{s}", [P, KD, P], F32R) for s in range(3)]
        ident = sb("ident", [P, P])
        ones = sb("ones", [P, P])
        gains = sb("gains", [P, G_ALL])
        r_tok = gains[:, 0:NT]
        tri = sb("tri", [P, P])
        tri_s = sb("tri_s", [P, P])
        eps_t = sb("eps_t", [P, 1])

        with ExitStack() as part:
            xn_hi = sb("xn_hi", [P, KD, TOK], F32R, part)
            xn_lo = sb("xn_lo", [P, KD, TOK], F32R, part)
        with ExitStack() as part:
            gain_rows = sb("gain_rows", [G_ALL, P], F32, part)
        with ExitStack() as part:
            y_out = sb("y_out", [P, NT, D], F32, part)
            x_gain = sb("x_gain", [P, KD, TOK], F32, part)
        with ExitStack() as part:
            p_hi = sb("p_hi", [P, NF, TOK], F32R, part)
        hold = sb("hold_xn", [P, 2 * KD * TOK])

        with ExitStack() as part:
            rstd_a = sb("rstd_a", [P, TOK], F32, part)
            hold_q = sb("hold_q", [P, TOK], F32, part)
            ssum_a = sb("ssum_a", [P, 2, TOK], F32, part)
            sq_a = sb("sq_a", [P, NG, KD, TG], F32, part)
        with ExitStack() as part:
            sb("hold_x", [P, 7 * TOK], F32, part)
            x_in = sb("x_in", [P, NT, D], F32, part)
        with ExitStack() as part:
            def pa(name, shape, dt=F32):
                return sb(name, shape, dt, part)
            hold_r = pa("hold_r", [P, TOK])
            qT = pa("qT", [P, TOK])
            with ExitStack() as sub:
                kT = sb("kT", [P, TOK], F32, sub)
                k_tok = sb("k_tok", [P, NT, DK], F32, sub)
            with ExitStack() as sub:
                h_lo = sb("h_lo", [P, 2, TOK], F32R, sub)
            hold_k = pa("hold_k", [P, 2 * TOK])
            v_tok = pa("v_tok", [P, NT, DV + 1])
            sig_o = pa("sig_o", [P, 2, TOK])
            dmat = pa("dmat", [P, NT, P])
            qw = pa("qw", [P, TOK])
            num = pa("num", [P, NT, DV + 1])
            c_nat = pa("c_nat", [P, 2, DEC_B, DK])
            with ExitStack() as sub:
                state = sb("state", [P, NT, DV + 1], F32, sub)
                c_smp = sb("c_smp", [P, DEC_B, DV + 1], F32, sub)
            with ExitStack() as sub:
                h_hi = sb("h_hi", [P, 2, TOK], F32R, sub)
            hold_h = pa("hold_h", [P, (NT + DEC_B) * (DV + 1)])
            pack = pa("pack", [P, H, NQ, NT])
            cur = pa("cur", [P, NQ, NT])
            dec_s = pa("dec_s", [P, H, DEC_B])
            dec8 = pa("dec8", [P, H])
            b_first = pa("b_first", [P, DEC_B])
            b_mem = pa("b_mem", [P, DEC_B])
            n_nat = pa("n_nat", [DEC_B, DK])
            g_bias = pa("g_bias", [2 * H, 1])
            g_h = pa("g_h", [P, 2])
            nstat = pa("nstat", [P, 6, NT])
            m_out = pa("m_out", [P, 2, H])
            m_in = pa("m_in", [P, H])
        num_flat = num[:, :, :].rearrange("p c v -> p (c v)")
        diag = num_flat[:, 0:NT * P].rearrange("p (c t) -> p c t", c=NT)
        diag2 = qw[:, :].rearrange("p (c t) -> p c t", c=NT)
        k_blk = num_flat[:, NT * P:NT * P + DEC_B * DK].rearrange("p (b d) -> p b d", b=DEC_B)
        c_out = qT[:, 0:3 * P].rearrange("p (j v) -> p j v", j=3)
        v_tmp = dmat[:, :, :].rearrange("p c t -> p (c t)")
        q_blk = kT[:, 0:DEC_B * P].rearrange("p (b t) -> p b t", b=DEC_B)
        h_tail = hold_h[:, (NT + DEC_B) * (DV + 1) - 4 * P:(NT + DEC_B) * (DV + 1)]
        blk, blk_last, last = (h_tail[:, k * P:(k + 1) * P] for k in range(3))
        reset = h_tail[0:H * NT, 3 * P:4 * P]
        small = num_flat[:, 0:8 * H * NT].rearrange("p (q h c) -> p q h c", q=8, h=H)
        gtok = num_flat[:, 8 * H * NT:8 * H * NT + NT * 2 * H].rearrange("p (c g) -> p c g", c=NT)
        r_tok0 = nstat[:, 0, :]
        gT = qT
        aT = qw
        h_f = dmat[:, :, :].rearrange("p c t -> p (c t)")

        with ExitStack() as part:
            hg_hi = sb("hg_hi", [P, 2, TOK], F32R, part)
            hg_lo = sb("hg_lo", [P, 2, TOK], F32R, part)
            silu = sb("silu", [P, 2, NG, TG], F32, part)
            h_tmp = sb("h_tmp", [P, 2, TG], F32, part)
            rstd_f = sb("rstd_f", [P, TOK], F32, part)
            ssum_f = sb("ssum_f", [P, 2, TOK], F32, part)
            sq_f = sb("sq_f", [P, NG, KD, TG], F32, part)

        with ExitStack() as part:
            vs = sb("vs", [P, NT, NF, P], F32, part)
        with ExitStack() as part:
            p_lo = sb("p_lo", [P, NT, NF, P], F32R, part)
            with ExitStack() as sub:
                bias_b = sb("bias_b", [P, G_B, P], F32, sub)
            with ExitStack() as sub:
                stat = sb("stat", [P, NT, NF // 4, 6], F32, sub)
            with ExitStack() as sub:
                w_s_in = sb("w_s_in", [P, G_B, P], F32, sub)
            hold_b = sb("hold_b", [P, G_B * P], F32, part)
            with ExitStack() as sub:
                w_s_smp = sb("w_s_smp", [P, G_B, P], F32, sub)
            t_b = sb("t_b", [P, 2, TG], F32, part)
            with ExitStack() as sub:
                mix = sb("mix", [P, 2, G_B, P], F32, sub)
                mv = sb("mv", [P, NT, 2], F32, sub)
                rs_v = sb("rs_v", [P, NT, 3], F32, sub)
            with ExitStack() as sub:
                rstd_b = sb("rstd_b", [P, TOK], F32, sub)
        RQ = INNER // 4
        row_buf = [w_s_in[:, :, :].rearrange("p g s -> p (g s)"), t_b[:, :, :].rearrange("p a t -> p (a t)")[:, 0:RQ]]

        ps = [ctx.enter_context(nc.psum_tensor(f"ps{b}", [P, 512], F32)) for b in range(8)]

        def bank(b, n=TG):
            return ps[b % 8][:, 0:n]

        const_ok = sem("const_ok")
        x_loaded = [sem(f"x_loaded{g}") for g in range(NG)]
        rows_loaded = sem("rows_loaded")
        small_loaded = sem("small_loaded")
        xt_pe, xt_dve, xt_act = sem("xt_pe"), sem("xt_dve"), sem("xt_act")
        gains_turned, gains_ready = sem("gains_turned"), sem("gains_ready")
        gt_rms, a_oscaled = sem("gt_rms"), sem("a_oscaled")
        raw_loaded = [sem("raw_loaded0"), sem("raw_loaded1")]
        raw_clear = sem("raw_clear")
        hi_split, split, used = sem("hi_split"), sem("units_split"), sem("units_used")
        squared, summed = sem("squared"), sem("summed")
        r_sum, r_root, r_done = sem("r_sum"), sem("r_root"), sem("r_done")
        r_diag, r_wide, r_ready = sem("r_diag"), sem("r_wide"), sem("r_ready")
        n_full, n_hi, n_lo = sem("n_full"), sem("n_hi"), sem("n_lo")
        dve_step = sem("dve_step")
        act_step = sem("act_step")
        pool_step = sem("pool_step")
        gt_mm, gt_act, gt_scaled, gt_tr, gate_pe, gate_dve, gate_act = (
            sem(x) for x in ("gt_mm", "gt_act", "gt_scaled", "gt_tr", "gate_pe", "gate_dve", "gate_act"))
        a_mm, a_evac, a_vtmp, a_sig = sem("a_mm"), sem("a_evac"), sem("a_vtmp"), sem("a_sig")
        a_tr, a_ktok, a_vtok = sem("a_tr"), sem("a_ktok"), sem("a_vtok")
        t_pe, t_act, t_dve = sem("t_pe"), sem("t_act"), sem("t_dve")
        a_diag, a_dargs, a_exp, a_qblk, a_kb = (
            sem(x) for x in ("a_diag", "a_dargs", "a_exp", "a_qblk", "a_kb"))
        a_ssq, a_fac, a_hlo, a_sqrt = sem("a_ssq"), sem("a_fac"), sem("a_hlo"), sem("a_sqrt")
        wd_mm, wd_add = sem("wd_mm"), sem("wd_add")
        c_loaded, n_loaded, c_stored = sem("c_loaded"), sem("n_loaded"), sem("c_stored")
        stored = sem("stored")
        g_mm = [sem(f"g_mm{x}") for x in range(2)]
        u_mm = [sem(f"u_mm{x}") for x in range(2)]
        g_scaled = [sem(f"g_scaled{x}") for x in range(2)]
        s_scaled = [sem(f"s_scaled{x}") for x in range(2)]
        g_silu = [sem(f"g_silu{x}") for x in range(2)]
        h_full = [sem(f"h_full{x}") for x in range(2)]
        h_his = [sem(f"h_his{x}") for x in range(2)]
        h_los = [sem(f"h_los{x}") for x in range(2)]
        d_mm = [sem(f"d_mm{x}") for x in range(2)]
        d_add = [sem(f"d_add{x}") for x in range(2)]
        bv_scaled, bu_scaled = sem("bv_scaled"), sem("bu_scaled")
        bv_mm, bv_gelu, bv_tr, bv_tok = sem("bv_mm"), sem("bv_gelu"), sem("bv_tr"), sem("bv_tok")
        b_loaded, b_mixed = sem("b_loaded"), sem("b_mixed")
        bw_tr, bw_copied, mix_ok = sem("bw_tr"), sem("bw_copied"), sem("mix_ok")
        ln_stat, ln_root, ln_scale = sem("ln_stat"), sem("ln_root"), sem("ln_scale")
        ln_dve, ln_act = sem("ln_dve"), sem("ln_act")
        bv_stat = sem("bv_stat")
        mx_mm, mx_act, mx_dve = sem("mx_mm"), sem("mx_act"), sem("mx_dve")
        gv_loaded, row_stored = ([sem(f"{x}{r}") for r in range(2)] for x in ("gv_loaded", "row_stored"))
        gv_done = sem("gv_done")
        bu_mm, bu_gelu, bu_gate, bu_bias = sem("bu_mm"), sem("bu_gelu"), sem("bu_gate"), sem("bu_bias")
        ps_hi, ps_lo = sem("ps_hi"), sem("ps_lo")
        bo_mm, bo_add = sem("bo_mm"), sem("bo_add")
        yt_pe, yt_act, yt_dve = sem("yt_pe"), sem("yt_act"), sem("yt_dve")

        block = ctx.enter_context(nc.Block())

        def tok(t, g):
            return t[..., g * TG:(g + 1) * TG]

        def tiles(ap):
            return ap.rearrange("p (c t) -> p c t", c=TPG)

        @block.sync
        def _(sp):
            def load(phase, i, u, src, width=P):
                ahead = phase.count(i, u, -1)
                if type(ahead) is not int or ahead > 0:
                    sp.wait_ge(split, ahead)
                r = phase.raw(u)
                dst = w_raw[r][:, :, 0:width]
                if len(src.shape) == 2:
                    dst = w_raw[r][:, :, :].rearrange("p k n -> p (k n)")
                sp.dma_start(dst, src).then_inc(raw_loaded[r], 16)

            a_in = a_w_in[0].rearrange("(k p) n -> p k n", p=P)
            for g in range(NG):
                for c in range(TPG * g, TPG * g + TPG):
                    src = x_prompt[0, c * P:(c + 1) * P, :] if c < NP else x_sample.rearrange("b s d -> (b s) d")
                    sp.dma_start(x_in[:, c, :], src).then_inc(x_loaded[g], 16)
                if g == 0:
                    for at, src, n in ((G_MIX, g_mix.rearrange("l (k p) -> (l k) p", p=P), 2 * KD),
                                       (G_FFN, g_ffn.rearrange("l (k p) -> (l k) p", p=P), 2 * KD),
                                       (G_FINAL, g_final.rearrange("(k p) -> k p", p=P), KD),
                                       (G_OUT, a_g_out.rearrange("l (k p) -> (l k) p", p=P), KD),
                                       (G_V, b_g_v.rearrange("l (k p) -> (l k) p", p=P), NF)):
                        sp.dma_start(gain_rows[at:at + n, :], src).then_inc(rows_loaded, 16)
                    sp.wait_ge(raw_clear, 1)
                    load(W_GATES, 0, 0, a_in[:, :, A_PROJ - 2 * H:A_PROJ], 2 * H)

            sp.dma_start(m_in[:, :], state_m[:, 0, :].unsqueeze(1).to_broadcast([DEC_B, DEC_S, H]))\
                .then_inc(small_loaded, 16)
            sp.dma_start(g_bias[:, :], a_b_gate.rearrange("l (g o) -> (l g) o", o=1)).then_inc(small_loaded, 16)

            a_out = a_w_out[0].rearrange("(k p) n -> k p n", p=P)
            c_in = state_C[:, 0].rearrange("b h (j v) d -> h j v b d", j=2)
            c_to = C_sample[:, 0].rearrange("b h (j v) d -> h j v b d", j=2)
            n_in = state_n[:, 0].rearrange("b h d -> h b d")
            n_to = n_sample[:, 0].rearrange("b h d -> h b d")

            def head(h):
                def load_vo(u):
                    at = 2 * QK_W + (u % 2) * P + (V_W if u >= 4 else 0)
                    load(W_HEADS, h, u, a_in[:, :, bass.ds(h * DV + at, P)])

                for u, col in enumerate((h * DK, h * DK + QK_W)):
                    load(W_HEADS, h, u, a_in[:, :, bass.ds(col, P)])
                load_vo(2)
                load_vo(3)
                if type(h) is int:
                    sp.wait_ge(gate_dve, 6)
                    sp.dma_start(m_prompt[0], m_out[0:1, 0, :]).then_inc(stored, 16)
                    sp.dma_start(m_sample[:, 0, :], m_out[0:P:DEC_S, 1, :]).then_inc(stored, 16)
                else:
                    sp.wait_ge(c_stored, h * (16 * 5) + 1)
                for j in range(2):
                    sp.dma_start(c_nat[:, j, :, :], c_in[bass.ds(h, 1), j].rearrange("o v b d -> (o v) b d"))\
                        .then_inc(c_loaded, 16)
                sp.dma_start(n_nat[:, :], n_in[bass.ds(h, 1)].rearrange("o b d -> (o b) d")).then_inc(n_loaded, 16)
                load_vo(4)
                load_vo(5)
                for u in range(6, 8):
                    load(W_HEADS, h, u, a_out[bass.ds(h * 2 + (u - 6), 1)].rearrange("o p n -> (o p) n"))
                sp.wait_ge(t_act, h * N_ACT + taken(ticket("cfin")))
                sp.dma_start(C_prompt[0, 0].rearrange("h (j v) d -> h v j d", j=2)[bass.ds(h, 1)]
                             .rearrange("o v j d -> (o v) j d"), c_out[:, 0:2, :]).then_inc(c_stored, 16)
                sp.dma_start(n_prompt[0, 0].rearrange("h (d o) -> h d o", o=1)[bass.ds(h, 1)]
                             .rearrange("a d o -> (a d) o"), c_out[:, 2, 0:1]).then_inc(c_stored, 16)
                sp.wait_ge(t_dve, h * N_DVE + taken(ticket("un")))
                for j in range(2):
                    sp.dma_start(c_to[bass.ds(h, 1), j].rearrange("o v b d -> (o v) b d"), c_nat[:, j, :, :])\
                        .then_inc(c_stored, 16)
                sp.dma_start(n_to[bass.ds(h, 1)].rearrange("o b d -> (o b) d"), n_nat[:, :]).then_inc(c_stored, 16)

            head(0)
            with sp.Fori(1, H) as h:
                head(h)

            def ffn(layer, phase):
                gu = f_w_gu[layer].rearrange("(k p) n -> p k n", p=P)
                down = f_w_down[layer].rearrange("(k p) n -> k p n", p=P)
                with sp.Fori(0, N_FFN) as i:
                    for c in range(2):
                        load(phase, i, 2 * c, gu[:, :, bass.ds(i * (2 * P) + c * P, P)])
                        load(phase, i, 2 * c + 1, gu[:, :, bass.ds(i * (2 * P) + (D_FF + c * P), P)])
                    for c in range(2):
                        load(phase, i, 4 + c, down[bass.ds(i * 2 + c, 1)].rearrange("o p n -> (o p) n"))

            ffn(0, W_FFN0)

            b_in = b_w_in[0].rearrange("(k p) n -> p k n", p=P)
            with sp.Fori(0, NF // 4) as i:
                for u in range(4):
                    load(W_BV, i, u, b_in[:, :, bass.ds(i * (4 * P) + (INNER + u * P), P)])
            def load_u(i, u):
                load(W_BU, i, u, b_in[:, :, bass.ds(i * (4 * P) + u * P, P)])

            load_u(0, 0)
            load_u(0, 1)
            sp.wait_ge(ln_stat, 1)
            sp.dma_start(w_s_in[:, :, :], b_w_s[0].rearrange("g t s -> t g s")).then_inc(b_loaded, 16)
            sp.wait_ge(bv_tr, 2 + 12 * (NF // 4))
            for b in range(DEC_B):
                sp.dma_start(w_s_smp[b * DEC_S:(b + 1) * DEC_S, :, 0:DEC_S],
                             b_w_s[0, :, 0:DEC_S, 0:DEC_S].rearrange("g t s -> t g s")).then_inc(b_loaded, 16)
            load_u(0, 2)
            load_u(0, 3)
            sp.wait_ge(mix_ok, 1)

            def load_gain(q):
                if q >= 2:
                    sp.wait_ge(row_stored[q % 2], 16)
                sp.dma_start(row_buf[q % 2], b_g_v[0:1, q * RQ:(q + 1) * RQ].to_broadcast([P, RQ]))\
                    .then_inc(gv_loaded[q % 2], 16)

            def store_rows(q):
                sp.wait_ge(gv_done, q + 1)
                sp.dma_start(v_rows.rearrange("b l s f -> (b l s) f")[:, q * RQ:(q + 1) * RQ], row_buf[q % 2])\
                    .then_inc(row_stored[q % 2], 16)

            load_gain(0)
            load_gain(1)
            for q in range(4):
                store_rows(q)
                if q < 2:
                    load_gain(q + 2)
            sp.wait_ge(row_stored[0], 32)
            sp.dma_start(bias_b[:, :, :], b_b_s.unsqueeze(0).to_broadcast([P, 1, G_B, P])
                         .rearrange("p o g t -> p (o g) t")).then_inc(b_mixed, 16)
            with sp.Fori(1, NF // 4) as i:
                for u in range(4):
                    load_u(i, u)
            b_out = b_w_out[0].rearrange("(a k p) n -> a p k n", a=2, p=P)
            with sp.Fori(0, KD // 2) as i:
                for u in range(4):
                    load(W_BO, i, u, b_out[u % 2][:, :, bass.ds(i * (2 * P) + (u // 2) * P, P)])

            ffn(1, W_FFN1)

            for c in range(NT):
                sp.wait_ge(yt_act, c + 1)
                sp.wait_ge(yt_dve, c + 1)
                dst = y_prompt[0, c * P:(c + 1) * P, :] if c < NP else y_sample.rearrange("b s d -> (b s) d")
                sp.dma_start(dst, y_out[:, c, :]).then_inc(stored, 16)
            sp.wait_ge(c_stored, 16 * 5 * H + 1)
            sp.wait_ge(stored, 16 * (2 + NT))

        @block.gpsimd
        def _(pool):
            n = 0

            def link(ins):
                nonlocal n
                n += 1
                ins.then_inc(pool_step, 1)
                pool.wait_ge(pool_step, n)

            nc.gpsimd.memset(w_raw[0][:, :, :], 0.0).then_inc(raw_clear, 1)
            link(nc.gpsimd.memset(ident[:, :], 0.0))
            link(nc.gpsimd.affine_select(out=ident[:, :], in_=ident[:, :], compare_op=ALU.not_equal, fill=1.0,
                                         base=0, pattern=[[-1, P]], channel_multiplier=1))
            nc.gpsimd.memset(eps_t[:, :], EPS)
            link(nc.gpsimd.memset(ones[:, :], 1.0))
            link(nc.gpsimd.affine_select(out=tri[:, :], in_=ones[:, :], compare_op=ALU.is_ge, fill=0.0,
                                         base=0, pattern=[[1, P]], channel_multiplier=-1))

            def by_stream(t):
                return t.rearrange("p (b s) -> p b s", b=DEC_B)

            for dst, src in ((tri_s, tri), (blk, ones)):
                link(nc.gpsimd.affine_select(out=by_stream(dst[:, :]), in_=by_stream(src[:, :]), compare_op=ALU.is_ge,
                                             fill=0.0, base=0, pattern=[[-DEC_S, DEC_B], [0, DEC_S]],
                                             channel_multiplier=1))
            link(nc.gpsimd.affine_select(out=by_stream(blk[:, :]), in_=by_stream(blk[:, :]), compare_op=ALU.is_ge,
                                         fill=0.0, base=DEC_S - 1, pattern=[[DEC_S, DEC_B], [0, DEC_S]],
                                         channel_multiplier=-1))
            link(nc.gpsimd.memset(blk_last[:, :], 0.0))
            link(nc.gpsimd.affine_select(out=by_stream(blk_last[:, :]), in_=by_stream(blk_last[:, :]),
                                         compare_op=ALU.not_equal, fill=1.0, base=-(DEC_S - 1),
                                         pattern=[[-DEC_S, DEC_B], [0, DEC_S]], channel_multiplier=1))
            link(nc.gpsimd.memset(last[:, :], 0.0))
            link(nc.gpsimd.affine_select(out=last[:, :], in_=last[:, :], compare_op=ALU.not_equal, fill=1.0,
                                         base=-(P - 1), pattern=[[0, P]], channel_multiplier=1))
            link(nc.gpsimd.memset(b_first[:, :], 0.0))
            link(nc.gpsimd.affine_select(out=b_first[:, :], in_=b_first[:, :], compare_op=ALU.not_equal, fill=1.0,
                                         base=0, pattern=[[-DEC_S, DEC_B]], channel_multiplier=1))
            link(nc.gpsimd.affine_select(out=b_mem[:, :], in_=ones[:, 0:DEC_B], compare_op=ALU.is_ge, fill=0.0,
                                         base=0, pattern=[[-DEC_S, DEC_B]], channel_multiplier=1))
            link(nc.gpsimd.affine_select(out=b_mem[:, :], in_=b_mem[:, :], compare_op=ALU.is_ge, fill=0.0,
                                         base=DEC_S - 1, pattern=[[DEC_S, DEC_B]], channel_multiplier=-1))
            link(nc.gpsimd.memset(reset[:, :], BIG))
            for h in range(H):
                link(nc.gpsimd.affine_select(out=by_stream(reset[:, :]), in_=by_stream(reset[:, :]),
                                             compare_op=ALU.not_equal, fill=-BIG, base=-1000 * (NT * h + NP),
                                             pattern=[[0, DEC_B], [1, DEC_S]], channel_multiplier=1000))
            nc.gpsimd.drain().then_inc(const_ok, 1)

            def split_unit(phase, i, u):
                r, s = phase.raw(u), phase.slots[u]
                pool.wait_ge(used, phase.count(i, u, 1 + FREE_UNITS - phase.back[u]))
                pool.wait_ge(raw_loaded[r], phase.loads(i, u) * 16)
                nc.gpsimd.tensor_tensor(w_hi[s][:, :, :], w_raw[r][:, :, :],
                                        ones[:, :].unsqueeze(1).to_broadcast([P, KD, P]), ALU.mult)\
                    .then_inc(hi_split, 1)
                pool.wait_ge(hi_split, phase.count(i, u, 1))
                nc.gpsimd.tensor_tensor(w_lo[s][:, :, :], w_raw[r][:, :, :], w_hi[s][:, :, :].bitcast(F32),
                                        ALU.subtract).then_inc(split, 1)

            split_unit(W_GATES, 0, 0)
            with pool.Fori(0, H) as h:
                for u in range(8):
                    split_unit(W_HEADS, h, u)
            with pool.Fori(0, N_FFN) as i:
                for u in range(6):
                    split_unit(W_FFN0, i, u)
            with pool.Fori(0, NF // 4) as i:
                for u in range(4):
                    split_unit(W_BV, i, u)
            with pool.Fori(0, NF // 4) as i:
                for u in range(4):
                    split_unit(W_BU, i, u)
            with pool.Fori(0, KD // 2) as i:
                for u in range(4):
                    split_unit(W_BO, i, u)
            with pool.Fori(0, N_FFN) as i:
                for u in range(6):
                    split_unit(W_FFN1, i, u)

        @block.tensor
        def _(pe):
            for _ in range(FREE_UNITS - 1):
                pe.drain().then_inc(used, 1)

            def passes(out, slot, blocks, hi, lo, first, last_one, frees=False, ready=None):
                n, total = 0, 3 * len(blocks)
                for k in blocks:
                    if ready is not None:
                        ready(k)
                    for w, x in ((w_hi, hi), (w_hi, lo), (w_lo, hi)):
                        ins = pe.matmul(out, w[slot][:, k, :], x(k), start=(first and n == 0),
                                        stop=(last_one and n == total - 1))
                        if n == 0 and frees:
                            ins.then_inc(used, 1)
                        n += 1
                return ins

            def unit_piece(phase, u, g, b, norm=None):
                def ready(k):
                    pe.wait_ge(n_lo, KD * (NG * norm + g) + k + 1)

                return passes(bank(b), phase.slots[u], range(KD), lambda k: tok(xn_hi[:, k, :], g),
                              lambda k: tok(xn_lo[:, k, :], g), True, True, g == 0,
                              None if norm is None else ready)

            def row_sums(n, b=6):
                for c in range(NT):
                    pe.wait_ge(summed, NG * n + c // TPG + 1)
                    for half in range(2):
                        ins = pe.matmul(bank(b, NT)[:, c:c + 1], (ssum_f if n else ssum_a)[:, half, c * P:(c + 1) * P],
                                        ones[:, 0:1], start=half == 0, stop=half == 1)
                ins.then_inc(r_sum, 1)

            def widen(k, src, b=7):
                for g in range(NG):
                    pe.wait_ge(r_diag, NG * k + g + 1)
                    if g == 2:
                        pe.wait_ge(r_ready, NG * k + 1)
                    pe.matmul(bank(b - g % 2), ones[:, :], src(g), start=True, stop=True).then_inc(r_wide, 1)

            pe.wait_ge(const_ok, 1)
            for c in range(NT):
                if c == TPG:
                    pe.wait_ge(rows_loaded, 16 * 5)
                    pe.transpose(ps[6][:, 0:G_ALL], gain_rows[:, :], ident[0:G_ALL, 0:G_ALL])\
                        .then_inc(gains_turned, 1)
                if c % TPG == 0:
                    pe.wait_ge(x_loaded[c // TPG], 16 * TPG)
                if c == TPG:
                    pe.wait_ge(gains_ready, 1)
                for half in range(2):
                    t = 2 * c + half
                    if t >= 8:
                        pe.wait_ge(xt_act if half else xt_dve, (t - 8) // 2 + 1)
                    for k in range(4):
                        ins = pe.transpose(ps[t % 8][:, k * P:(k + 1) * P],
                                           x_in[:, c, (4 * half + k) * P:(4 * half + k + 1) * P], ident[:, :])
                    ins.then_inc(xt_pe, 1)
            pe.wait_ge(xt_dve, NT)
            pe.wait_ge(xt_act, NT)
            pe.wait_ge(split, 1)
            for g in range(NG):
                unit_piece(W_GATES, 0, g, GATE_BANKS[g], 0).then_inc(gt_mm, 1)

            lf = small[:, 0, :, :]
            cm = small[:, 3, :, :]

            def by_head(b, at):
                return ps[b][:, at:at + H * NT].rearrange("p (h c) -> p h c", h=H)

            def gates_turn():
                pe.wait_ge(gt_scaled, 1)
                for c in range(NT):
                    ins = pe.transpose(ps[6][:, c * 8:(c + 1) * 8], gT[0:2 * H, c * P:(c + 1) * P],
                                       ident[0:2 * H, 0:2 * H])
                ins.then_inc(gt_tr, 1)

            def gates_sums():
                pe.wait_ge(gate_dve, 1)
                for col, whole, own in ((0, tri, tri_s), (64, ones, blk)):
                    for c0, c1, m in ((0, NP, whole), (NP, NT, own)):
                        ins = pe.matmul(by_head(7, col)[:, :, c0:c1], m[:, :], lf[:, :, c0:c1], start=True, stop=True)
                ins.then_inc(gate_pe, 1)

            def gates_max():
                pe.wait_ge(gate_dve, 2)
                pe.transpose(ps[6][0:H * NT, 0:P], small[:, 2, :, :].rearrange("p h c -> p (h c)"), ident[:, :])\
                    .then_inc(gate_pe, 1)
                pe.wait_ge(gate_dve, 3)
                pe.transpose(ps[6][:, P:P + H * NT], aT[0:H * NT, P:2 * P], ident[0:H * NT, 0:H * NT])\
                    .then_inc(gate_pe, 1)

            def gates_last():
                pe.wait_ge(gate_dve, 4)
                for c0, c1, m in ((0, NP, last), (NP, NT, blk_last)):
                    ins = pe.matmul(by_head(6, 2 * P)[:, :, c0:c1], m[:, :], cm[:, :, c0:c1], start=True, stop=True)
                ins.then_inc(gate_pe, 1)

            def gates_decay():
                pe.wait_ge(gate_dve, 5)
                pe.matmul(ps[6][:, 0:H * DEC_B], ones[:, :], dmat[:, 0, 0:H * DEC_B], start=True, stop=True)
                pe.matmul(ps[6][0:DEC_B, P:P + H], b_first[:, :], pack[:, :, Q_DECAY, NP], start=True, stop=True)\
                    .then_inc(gate_pe, 1)
                pe.wait_ge(gate_dve, 6)

            def between(n):
                if n == 0:
                    row_sums(0, 4)
                elif n == 1:
                    widen(0, lambda g: sq_a[:, 0, g, :], 4)
                elif n == 2:
                    pe.wait_ge(r_ready, NG)
                    gates_turn()
                elif n == 3:
                    gates_sums()
                elif n == 4:
                    gates_max()
                elif n == 5:
                    gates_last()
                    gates_decay()

            def head(h):
                first = type(h) is int

                def turn(n):
                    if n < 3:
                        pe.wait_ge(a_evac, h * 6 + 3 + n + 1)
                        src = tok(kT[:, :], n)
                    else:
                        pe.wait_ge(a_vtmp, h * 6 + (n - 3) + 1)
                        src = v_tmp[:, (n % 2) * TG:(n % 2 + 1) * TG]
                    if 2 <= n < 5:
                        pe.wait_ge(a_ktok, h * 3 + n - 2 + 1)
                    elif n >= 5:
                        pe.wait_ge(a_vtok, h * 6 + n - 5 + 1)
                    for c in range(TPG):
                        ins = pe.transpose(bank(6 + n % 2)[:, c * P:(c + 1) * P], src[:, c * P:(c + 1) * P],
                                           ident[:, :])
                    ins.then_inc(a_tr, 1)

                for u in range(5):
                    pe.wait_ge(split, W_HEADS.count(h, u, 1))
                    for g in range(NG):
                        if u < 2:
                            pe.wait_ge(wd_add, h * 24 + (3 * u + g + 1))
                        elif u in (2, 3):
                            pe.wait_ge(a_evac, h * 6 + 3 * (u - 2) + g + 1)
                        elif u == 4:
                            pe.wait_ge(a_vtmp, h * 6 + 3 * (u - 4) + g + 1)
                        ins = unit_piece(W_HEADS, u, g, 3 * (u % 2) + g)
                        ins.then_inc(a_mm, 1)
                        at = 3 * u + g
                        if first and at < 6:
                            between(at)
                        elif first and at == 6:
                            for n in range(3):
                                turn(n)
                        elif 4 <= at < 13 and not (first and at < 7):
                            turn(at - 4)

                def wait_bank(t):
                    if t >= 8:
                        if TICKETS[t - 8] in BY_ACT:
                            pe.wait_ge(t_act, h * N_ACT + taken(t - 8))
                        else:
                            pe.wait_ge(t_dve, h * N_DVE + taken(t - 8))
                    elif t < 3:
                        pe.wait_ge(a_sig, h * 3 + t + 1)
                    elif t < 6:
                        pe.wait_ge(a_vtmp, h * 6 + t + 1)
                    else:
                        pe.wait_ge(a_vtok, h * 6 + 6)

                for name, src in (("mb", diag), ("wib", diag2)):
                    pe.wait_ge(a_diag, h * 2 + (1 if name == "mb" else 2))
                    for g in range(NG):
                        t = ticket(name, g)
                        wait_bank(t)
                        pe.matmul(bank(t), ones[:, :], src[:, g * TPG:(g + 1) * TPG, :], start=True, stop=True)\
                            .then_inc(t_pe, 1)
                for g in range(NG):
                    t = ticket("s", g)
                    wait_bank(t)
                    for c in range(g * TPG, (g + 1) * TPG):
                        ins = pe.matmul(bank(t)[:, (c % TPG) * P:(c % TPG + 1) * P], kT[:, c * P:(c + 1) * P],
                                        qT[:, c * P:(c + 1) * P], start=True, stop=True)
                    ins.then_inc(t_pe, 1)
                pe.wait_ge(c_loaded, h * 32 + 32)
                pe.wait_ge(n_loaded, h * 16 + 16)
                wait_bank(ticket("nt"))
                for k in range(4):
                    t = ticket("ctr", k)
                    wait_bank(t)
                    for b in range(2):
                        for j in range(2):
                            ins = pe.transpose(ps[t % 8][:, (2 * b + j) * P:(2 * b + j + 1) * P],
                                               c_nat[:, j, 2 * k + b, :], ident[:, :])
                    ins.then_inc(t_pe, 1)
                t = ticket("nt")
                pe.transpose(ps[t % 8][:, 0:DEC_B], n_nat[:, :], ident[0:DEC_B, 0:DEC_B]).then_inc(t_pe, 1)
                for c in range(NP):
                    t = ticket("u", c)
                    wait_bank(t)
                    pe.matmul(bank(t, DV + 1), k_tok[:, c, :], v_tok[:, c, :], start=True, stop=True)\
                        .then_inc(t_pe, 1)
                pe.wait_ge(a_kb, h + 1)
                for j in range(2):
                    for half in range(2):
                        t = ticket("us", 2 * j + half)
                        wait_bank(t)
                        pe.matmul(ps[t % 8][:, :], v_tok[:, NP, j * P:(j + 1) * P],
                                  k_blk[:, 4 * half:4 * half + 4, :], start=True, stop=True).then_inc(t_pe, 1)
                t = ticket("un")
                wait_bank(t)
                pe.matmul(ps[t % 8][0:DEC_B, 0:DK], b_mem[:, :], k_tok[:, NP, :], start=True, stop=True)\
                    .then_inc(t_pe, 1)
                t = ticket("cfin")
                wait_bank(t)
                pe.wait_ge(t_dve, h * N_DVE + taken(ticket("u", NP - 1)))
                for j in range(2):
                    ins = pe.transpose(ps[t % 8][:, j * P:(j + 1) * P], state[:, NP, j * P:(j + 1) * P], ident[:, :])
                ins.then_inc(t_pe, 1)
                for c in range(NT):
                    t = ticket("pv", c)
                    wait_bank(t)
                    if c == NP:
                        pe.wait_ge(a_qblk, h + 1)
                    pe.matmul(bank(t, DV + 1), dmat[:, c, :], v_tok[:, c, :], start=True, stop=False)
                    if c < NP:
                        ins = pe.matmul(bank(t, DV + 1), qw[:, c * P:(c + 1) * P], state[:, c, :],
                                        start=False, stop=True)
                    else:
                        for b in range(DEC_B):
                            ins = pe.matmul(bank(t, DV + 1), q_blk[:, b, :], c_smp[:, b, :],
                                            start=False, stop=(b == DEC_B - 1))
                    ins.then_inc(t_pe, 1)
                pe.wait_ge(split, W_HEADS.count(h, 5, 1))

                def o_piece(g):
                    t = ticket("o", g)
                    wait_bank(t)
                    unit_piece(W_HEADS, 5, g, t).then_inc(t_pe, 1)

                def output_turn(g):
                    pe.wait_ge(a_fac, h + 2)
                    for j in range(2):
                        t = ticket("ht", 2 * g + j)
                        wait_bank(t)
                        for c in range(TPG):
                            ins = pe.transpose(bank(t)[:, c * P:(c + 1) * P],
                                               num[:, g * TPG + c, j * P:(j + 1) * P], ident[:, :])
                        ins.then_inc(t_pe, 1)

                o_piece(0)
                o_piece(1)
                output_turn(0)
                o_piece(2)
                output_turn(1)
                output_turn(2)
                pe.wait_ge(split, W_HEADS.count(h, 7, 1))
                for g in range(NG):
                    pe.wait_ge(a_hlo, h * 6 + 2 * g + 2)
                    for j in range(KD):
                        n = KD * g + j
                        if n < 6:
                            wait_bank(max(t for t in range(NTICK) if t % 8 == n) + 8)
                        else:
                            pe.wait_ge(wd_add, h * 24 + n + 1)
                        for a in range(2):
                            ins = passes(bank(n % 6), W_HEADS.slots[6 + a], [j], lambda k: tok(h_hi[:, a, :], g),
                                         lambda k: tok(h_lo[:, a, :], g), a == 0, a == 1,
                                         n == (0, NG * KD - 1)[a])
                        ins.then_inc(wd_mm, 1)

            head(0)
            with pe.Fori(1, H) as h:
                head(h)

            def ffn(layer, phase, n, k):
                gm, um, gs, hf, hl, dm, da = (x[layer] for x in (g_mm, u_mm, g_silu, h_full, h_los, d_mm, d_add))

                def body(i):
                    first = type(i) is int
                    for c in range(2):
                        pe.wait_ge(split, phase.count(i, 2 * c, 1))
                        for g in range(NG):
                            if c == 0:
                                pe.wait_ge(da, i * 24 + g + 1)
                            else:
                                pe.wait_ge(gs, i * 6 + g + 1)
                            ins = unit_piece(phase, 2 * c, g, g, n if first and c == 0 else None)
                            ins.then_inc(gm, 1)
                        pe.wait_ge(split, phase.count(i, 2 * c + 1, 1))
                        for g in range(NG):
                            if c == 0:
                                pe.wait_ge(da, i * 24 + 3 + g + 1)
                            else:
                                pe.wait_ge(hf, i * 6 + g + 1)
                            ins = unit_piece(phase, 2 * c + 1, g, 3 + g)
                            ins.then_inc(um, 1)
                            if first and c == 0 and g == 0:
                                row_sums(n)
                            if first and c == 0 and g == 1:
                                widen(k, lambda g: sq_f[:, 0, g, :])
                    pe.wait_ge(split, phase.count(i, 5, 1))
                    for g in range(NG):
                        pe.wait_ge(hl, i * 6 + 3 + g + 1)
                        for j in range(KD):
                            m = KD * g + j
                            if m < 3:
                                pe.wait_ge(gs, i * 6 + 3 + m + 1)
                            elif m < 6:
                                pe.wait_ge(hf, i * 6 + m + 1)
                            else:
                                pe.wait_ge(da, i * 24 + m + 1)
                            for a in range(2):
                                ins = passes(bank(m % 6), phase.slots[4 + a], [j], lambda k: tok(hg_hi[:, a, :], g),
                                             lambda k: tok(hg_lo[:, a, :], g), a == 0, a == 1,
                                             m == (0, NG * KD - 1)[a])
                            ins.then_inc(dm, 1)

                body(0)
                with pe.Fori(1, N_FFN) as i:
                    body(i)

            ffn(0, W_FFN0, 1, 1)

            def v_turn(i, m):
                pe.wait_ge(bv_gelu, i * 12 + m + 1)
                if type(i) is not int or m >= 2:
                    pe.wait_ge(bv_tok, i * 12 + (m - 1))
                for c in range(TPG):
                    ins = pe.transpose(bank(6 + m % 2)[:, c * P:(c + 1) * P],
                                       t_b[:, m % 2, c * P:(c + 1) * P], ident[:, :])
                ins.then_inc(bv_tr, 1)

            for _ in range(2):
                pe.drain().then_inc(bv_tr, 1)
            for n in range(12):
                u, g = n // 3, n % 3
                if g == 0:
                    pe.wait_ge(split, W_BV.count(0, u, 1))
                if n == 0:
                    pe.wait_ge(d_add[0], 6 + 24 * N_FFN)
                if n >= 6:
                    pe.wait_ge(bv_gelu, n - 6 + 1)
                unit_piece(W_BV, u, g, n % 6, 2 if u == 0 else None).then_inc(bv_mm, 1)
                if n == 3:
                    row_sums(2)
                if n == 4:
                    widen(2, lambda g: sq_f[:, 0, g, :])
                    pe.wait_ge(r_ready, NG * 3)
                for m in range(min(2 * (n - 5), n - 1), min(2 * (n - 4), n)):
                    if n >= 5:
                        v_turn(0, m)
            with pe.Fori(1, NF // 4) as i:
                for u in range(4):
                    pe.wait_ge(split, W_BV.count(i, u, 1))
                    for g in range(NG):
                        n = 3 * u + g
                        pe.wait_ge(bv_gelu, i * 12 + (n - 5))
                        unit_piece(W_BV, u, g, n % 6).then_inc(bv_mm, 1)
                        if n == 0:
                            v_turn(i - 1, 11)
                        else:
                            v_turn(i, n - 1)

            def u_piece(i, n):
                u, g = n // 3, n % 3
                if g == 0:
                    pe.wait_ge(split, W_BU.count(i, u, 1))
                pe.wait_ge(bu_gate, i * 12 + (n + 1))
                unit_piece(W_BU, u, g, n % 6).then_inc(bu_mm, 1)

            for n in range(6):
                pe.wait_ge(bv_gelu, 12 * (NF // 4) - 6 + n + 1)
                u_piece(0, n)
                if n == 0:
                    v_turn(NF // 4 - 1, 11)
            pe.wait_ge(b_loaded, 16 * (1 + DEC_B))
            pe.wait_ge(bv_tok, 12 * (NF // 4))
            pe.wait_ge(bw_copied, 1)
            for a, src in enumerate((w_s_in, w_s_smp)):
                for g in range(G_B):
                    ins = pe.transpose(ps[6 + a][:, g * P:(g + 1) * P], src[:, g, :], ident[:, :])
                ins.then_inc(bw_tr, 1)
            pe.wait_ge(mix_ok, 1)
            for c in range(NT):
                if c in LN_ACT:
                    pe.wait_ge(ln_act, LN_ACT.index(c) + 1)
                else:
                    pe.wait_ge(ln_dve, LN_DVE.index(c) + 1)
                for q in range(4):
                    t = 4 * c + q
                    if t >= 2:
                        pe.wait_ge(mx_act if t % 2 else mx_dve, t // 2)
                    for k in range(FPG):
                        f = FPG * q + k
                        ins = pe.matmul(ps[6 + t % 2][:, k * P:(k + 1) * P], vs[:, c, f, :], mix[:, c // NP, q, :],
                                        start=True, stop=True)
                    ins.then_inc(mx_mm, 1)
            pe.wait_ge(mx_act, 2 * NT)
            pe.wait_ge(mx_dve, 2 * NT)
            widen(3, lambda g: t_b[:, g % 2, :])
            for n in range(6, 12):
                u_piece(0, n)
            with pe.Fori(1, NF // 4) as i:
                for n in range(12):
                    u_piece(i, n)
            with pe.Fori(0, KD // 2) as i:
                for u in range(4):
                    j, a = u // 2, u % 2
                    pe.wait_ge(split, W_BO.count(i, u, 1))
                    for g in range(NG):
                        def ready(k):
                            pe.wait_ge(ps_lo, P_ORDER.index((g, KD * a + k)) + 1)

                        if a == 0:
                            pe.wait_ge(bo_add, i * 6 + 3 * j + g + 1)
                        ins = passes(bank(3 * j + g), W_BO.slots[u], range(KD),
                                     lambda k: tok(p_hi[:, KD * a + k, :], g),
                                     lambda k: p_lo[:, TPG * g:TPG * (g + 1), KD * a + k, :], a == 0, a == 1, g == 0,
                                     ready)
                        if a == 1:
                            ins.then_inc(bo_mm, 1)

            ffn(1, W_FFN1, 3, 4)

            pe.wait_ge(d_add[1], 6 + 24 * N_FFN)
            for c in range(NT):
                for half in range(2):
                    t = 2 * c + half
                    if t == 6:
                        row_sums(4)
                        pe.wait_ge(r_done, 5)
                    if t >= 8:
                        pe.wait_ge(yt_act if half else yt_dve, (t - 8) // 2 + 1)
                    pe.wait_ge(n_full, KD * (c // TPG + 1))
                    for k in range(4):
                        ins = pe.transpose(ps[t % 8][:, k * P:(k + 1) * P],
                                           x_gain[:, 4 * half + k, c * P:(c + 1) * P], ident[:, :])
                    ins.then_inc(yt_pe, 1)

        @block.scalar
        def _(act):
            def norm(n, gain, added, squares_free=None):
                def squares(g):
                    act.activation((sq_f if n else sq_a)[:, g, :, :], tok(xT[:, :, :], g), ACT.Square)\
                        .then_inc(squared, 1)

                for g in range(NG):
                    for k in range(KD):
                        added(g, k)
                        out, says = (xn_hi, n_hi) if n < 4 else (x_gain, n_full)
                        act.activation(tok(out[:, k, :], g), tok(xT[:, k, :], g), ACT.Copy,
                                       scale=gains[:, gain + k:gain + k + 1]).then_inc(says, 1)
                    if squares_free is None:
                        squares(g)
                if squares_free is not None:
                    squares_free()
                    for g in range(NG):
                        squares(g)
                act.wait_ge(r_sum, n + 1)
                act.activation(r_tok[:, :] if n else r_tok0, bank(6 if n else 4, NT), ACT.Sqrt, bias=eps_t[:, :],
                               scale=1.0 / D).then_inc(r_root, 1)

            def adds(counter, base):
                return lambda g, k: act.wait_ge(counter, base + KD * g + k + 1)

            def turned(g, k):
                if k == 0:
                    for c in range(g * TPG, (g + 1) * TPG):
                        act.wait_ge(xt_pe, 2 * c + 2)
                        act.activation(xT[:, 4:8, c * P:(c + 1) * P],
                                       ps[(2 * c + 1) % 8][:, :].rearrange("p (k t) -> p k t", k=4), ACT.Copy)\
                            .then_inc(xt_act, 1)
                    if g == 0:
                        act.wait_ge(const_ok, 1)
                        act.wait_ge(gains_ready, 1)
                    act.wait_ge(xt_dve, TPG * (g + 1))
                    act.wait_ge(xt_act, TPG * (g + 1))

            norm(0, G_MIX, turned, lambda: act.wait_ge(xt_pe, 2 * NT))
            for g in range(NG):
                act.wait_ge(gt_rms, g + 1)
                if g == 0:
                    act.wait_ge(small_loaded, 32)
                    act.activation(g_bias[:, :], g_bias[:, :], ACT.Copy, scale=1.0 / CAP).then_inc(act_step, 1)
                    act.wait_ge(act_step, 1)
                act.activation(tok(gT[0:2 * H, :], g), bank(GATE_BANKS[g])[0:2 * H, :], ACT.Tanh, bias=g_bias[:, :],
                               scale=1.0 / CAP).then_inc(gt_act, 1)
            act.wait_ge(gt_scaled, 2)
            act.activation(small[:, 1, :, :], small[:, 1, :, :], ACT.Exp, scale=-1.0).then_inc(act_step, 1)
            act.wait_ge(act_step, 2)
            act.activation(small[:, 1, :, :], small[:, 1, :, :], ACT.Ln, bias=ones[:, 0:1]).then_inc(gate_act, 1)
            act.wait_ge(gt_scaled, 3)
            act.activation(pack[:, :, Q_WI:NQ, :], pack[:, :, Q_WI:NQ, :], ACT.Exp).then_inc(gate_act, 1)
            act.wait_ge(gate_act, 2)

            act.drain().then_inc(c_stored, 1)
            with act.Fori(0, H) as h:
                for n in range(6):
                    act.wait_ge(a_tr, h * 9 + 3 + n + 1)
                    g, j = n % 3, n // 3
                    act.activation(v_tok[:, g * TPG:(g + 1) * TPG, j * P:(j + 1) * P], tiles(bank(6 + (3 + n) % 2)),
                                   ACT.Copy).then_inc(a_vtok, 1)
                for g in range(NG):
                    act.wait_ge(a_oscaled, h * 6 + g + 1)
                    act.activation(tok(sig_o[:, 0, :], g), bank(g), ACT.Sigmoid).then_inc(a_sig, 1)
                for g in range(NG):
                    act.wait_ge(a_dargs, h * 3 + g + 1)
                    act.activation(dmat[:, g * TPG:(g + 1) * TPG, :], dmat[:, g * TPG:(g + 1) * TPG, :], ACT.Exp)\
                        .then_inc(a_exp, 1)
                for k in range(4):
                    t = ticket("ctr", k)
                    act.wait_ge(t_pe, h * NTICK + t + 1)
                    act.activation(c_smp[:, 2 * k:2 * k + 2, 0:DV],
                                   ps[t % 8][:, :].rearrange("p (b v) -> p b v", b=2), ACT.Copy).then_inc(t_act, 1)
                t = ticket("nt")
                act.wait_ge(t_pe, h * NTICK + t + 1)
                act.activation(c_smp[:, :, DV], ps[t % 8][:, 0:DEC_B], ACT.Copy).then_inc(t_act, 1)
                t = ticket("cfin")
                act.wait_ge(t_dve, h * N_DVE + taken(ticket("u", NP - 1)))
                act.wait_ge(c_stored, h * 80 + 1)
                act.activation(c_out[:, 2, 0:1], state[:, NP, DV:DV + 1], ACT.Copy).then_inc(act_step, 1)
                act.wait_ge(t_pe, h * NTICK + t + 1)
                act.activation(c_out[:, 0:2, :], ps[t % 8][:, 0:DV].rearrange("p (j v) -> p j v", j=2), ACT.Copy)\
                    .then_inc(t_act, 1)
                for c in range(NT):
                    act.wait_ge(t_dve, h * N_DVE + taken(ticket("pv", c)))
                    act.activation(v_tok[:, c, 0:DV], num[:, c, 0:DV], ACT.Square, accum_out=nstat[:, 0, c:c + 1])\
                        .then_inc(a_ssq, 1)
                act.wait_ge(a_qblk, h + 1)
                act.wait_ge(a_fac, h + 1)
                act.wait_ge(a_sqrt, h * 2 + 1)
                act.activation(nstat[:, 3, :], nstat[:, 2, :], ACT.Sqrt, bias=eps_t[:, :], scale=1.0 / DV)\
                    .then_inc(a_sqrt, 1)
                for g in range(NG):
                    t = ticket("o", g)
                    act.wait_ge(a_oscaled, h * 6 + 3 + g + 1)
                    act.activation(tok(sig_o[:, 1, :], g), bank(t), ACT.Sigmoid).then_inc(t_act, 1)

            def ffn(layer):
                with act.Fori(0, N_FFN) as i:
                    for c in range(2):
                        for g in range(NG):
                            act.wait_ge(g_scaled[layer], i * 6 + 3 * c + g + 1)
                            act.activation(silu[:, c, g, :], bank(g), ACT.Silu).then_inc(g_silu[layer], 1)

            norm(1, G_FFN, adds(wd_add, 6 + 24 * (H - 1)), lambda: act.wait_ge(c_stored, 80 * H + 1))
            ffn(0)
            norm(2, G_MIX + KD, adds(d_add[0], 6 + 24 * (N_FFN - 1)))
            with act.Fori(0, NF // 4) as i:
                for n in range(12):
                    act.wait_ge(bv_scaled, i * 12 + n + 1)
                    act.wait_ge(bv_tr, i * 12 + n + 1)
                    act.activation(t_b[:, n % 2, :], bank(n % 6), ACT.Gelu_apprx_tanh).then_inc(bv_gelu, 1)
            act.wait_ge(ln_stat, 1)
            act.activation(rs_v[:, :, 0], mv[:, :, 1], ACT.Sqrt, bias=eps_t[:, :]).then_inc(ln_root, 1)
            act.wait_ge(ln_scale, 1)
            for c in LN_ACT:
                tile = vs[:, c, :, :].rearrange("p f t -> p (f t)")
                act.activation(tile, tile, ACT.Identity, scale=rs_v[:, c, 1:2], bias=rs_v[:, c, 2:3])\
                    .then_inc(ln_act, 1)
            act.wait_ge(ln_act, len(LN_ACT))
            for c in range(NT):
                for q in range(1, 4, 2):
                    t = 4 * c + q
                    act.wait_ge(mx_mm, t + 1)
                    if c == NP:
                        act.wait_ge(gv_done, 4)
                    act.activation(vs[:, c, FPG * q:FPG * (q + 1), :],
                                   ps[6 + t % 2][:, :].rearrange("p (f t) -> p f t", f=FPG), ACT.Copy)\
                        .then_inc(mx_act, 1)
            with act.Fori(0, NF // 4) as i:
                for n in range(12):
                    act.wait_ge(bu_scaled, i * 12 + n + 1)
                    act.activation(bank(n % 6), bank(n % 6), ACT.Gelu_apprx_tanh).then_inc(bu_gelu, 1)
            act.wait_ge(bu_gate, 6 + 12 * (NF // 4))
            for g, f in P_ORDER:
                act.activation(tiles(tok(p_hi[:, f, :], g)), vs[:, g * TPG:(g + 1) * TPG, f, :], ACT.Copy)\
                    .then_inc(ps_hi, 1)
            act.wait_ge(bo_add, 6 + NG * KD)
            norm(3, G_FFN + KD, adds(bo_add, 6), lambda: act.wait_ge(bo_add, 6 + NG * KD))
            ffn(1)
            norm(4, G_FINAL, adds(d_add[1], 6 + 24 * (N_FFN - 1)))
            act.wait_ge(r_done, 5)
            for c in range(NT):
                act.wait_ge(yt_pe, 2 * c + 2)
                act.activation(y_out[:, c, D // 2:D], ps[(2 * c + 1) % 8][:, :], ACT.Copy,
                               scale=r_tok[:, c:c + 1]).then_inc(yt_act, 1)

        @block.vector
        def _(dve):
            n_link = 0

            def link(ins):
                nonlocal n_link
                n_link += 1
                ins.then_inc(dve_step, 1)
                dve.wait_ge(dve_step, n_link)

            def add_up(n, g):
                sq, ss = (sq_f[:, g, :, :], ssum_f) if n else (sq_a[:, g, :, :], ssum_a)
                dve.wait_ge(squared, NG * n + g + 1)
                link(dve.tensor_tensor(sq[:, 0:4, :], sq[:, 0:4, :], sq[:, 4:8, :], ALU.add))
                dve.tensor_tensor(tok(ss[:, :, :], g), sq[:, 0:2, :], sq[:, 2:4, :], ALU.add).then_inc(summed, 1)

            def invert(n):
                r = r_tok[:, :] if n else r_tok0
                dve.wait_ge(r_root, n + 1)
                dve.reciprocal(r, r).then_inc(r_done, 1)
                dve.wait_ge(r_done, n + 1)

            def widen(k, dst, buf, buffers, r=r_tok, b=7):
                for g in range(NG):
                    if g >= buffers:
                        dve.wait_ge(r_wide, NG * k + g - buffers + 1)
                    dve.tensor_tensor(tiles(buf(g)), ident[:, :].unsqueeze(1).to_broadcast([P, TPG, P]),
                                      r[:, g * TPG:(g + 1) * TPG].unsqueeze(2).to_broadcast([P, TPG, P]),
                                      ALU.mult).then_inc(r_diag, 1)
                for g in range(NG):
                    dve.wait_ge(r_wide, NG * k + g + 1)
                    dve.tensor_copy(tok(dst[:, :], g), bank(b - g % 2)).then_inc(r_ready, 1)
                dve.wait_ge(r_ready, NG * k + NG)

            def norm(n, gain, k, dst, before=None):
                for g in range(NG):
                    if before is not None:
                        before(g)
                    for j in range(KD):
                        dve.wait_ge(n_hi, KD * (NG * n + g) + j + 1)
                        dve.scalar_tensor_tensor(tok(xn_lo[:, j, :], g), tok(xT[:, j, :], g),
                                                 gains[:, gain + j:gain + j + 1],
                                                 tok(xn_hi[:, j, :], g).bitcast(F32), ALU.mult, ALU.subtract)\
                            .then_inc(n_lo, 1)
                for g in range(NG):
                    add_up(n, g)
                invert(n)
                if n:
                    widen(k, dst, lambda g: sq_f[:, 0, g, :], 3)
                else:
                    widen(k, dst, lambda g: sq_a[:, 0, g, :], 3, r_tok0, 4)

            def turned(g):
                for c in range(g * TPG, (g + 1) * TPG):
                    dve.wait_ge(xt_pe, 2 * c + 1)
                    dve.tensor_copy(xT[:, 0:4, c * P:(c + 1) * P],
                                    ps[(2 * c) % 8][:, :].rearrange("p (k t) -> p k t", k=4)).then_inc(xt_dve, 1)
                if g == 0:
                    dve.wait_ge(gains_turned, 1)
                    dve.tensor_copy(gains[:, :], ps[6][:, 0:G_ALL]).then_inc(gains_ready, 1)
                    dve.wait_ge(gains_ready, 1)
                dve.wait_ge(xt_dve, TPG * (g + 1))

            for _ in range(6):
                dve.drain().then_inc(wd_add, 1)
            dve.drain().then_inc(a_fac, 1)
            norm(0, G_MIX, 0, rstd_a, turned)

            lf, tmp, a, cm = (small[:, k, :, :] for k in range(4))
            bt, mp, mt, mn = (small[:, k, :, :] for k in range(4, 8))
            for g in range(NG):
                piece = bank(GATE_BANKS[g])[0:2 * H, :]
                dve.wait_ge(gt_mm, g + 1)
                dve.tensor_tensor(piece, piece, tok(rstd_a[0:2 * H, :], g), ALU.mult).then_inc(gt_rms, 1)
            dve.wait_ge(gt_act, NG)
            dve.tensor_scalar(gT[0:2 * H, :], gT[0:2 * H, :], CAP, None, ALU.mult).then_inc(gt_scaled, 1)
            dve.wait_ge(gt_tr, 1)
            link(dve.tensor_copy(gtok[:, :, :].rearrange("p c g -> p (c g)"), ps[6][:, 0:NT * 2 * H]))
            ig = gtok[:, :, 0:H].rearrange("p c h -> p h c")
            fg = gtok[:, :, H:2 * H].rearrange("p c h -> p h c")
            link(dve.tensor_scalar(lf, fg, -1.0, None, ALU.mult))
            dve.tensor_tensor(tmp, lf, fg, ALU.max).then_inc(gt_scaled, 1)
            dve.wait_ge(gate_act, 1)
            link(dve.tensor_scalar(lf, fg, 0.0, None, ALU.min))
            dve.tensor_tensor(lf, lf, tmp, ALU.subtract).then_inc(gate_dve, 1)
            dve.wait_ge(gate_pe, 1)
            link(dve.tensor_copy(bt, ps[7][:, 0:H * NT].rearrange("p (h c) -> p h c", h=H)))
            dve.tensor_tensor(a, ig, bt, ALU.subtract).then_inc(gate_dve, 1)
            dve.wait_ge(gate_pe, 2)
            link(dve.tensor_copy(aT[0:H * NT, 0:P], ps[6][0:H * NT, 0:P]))
            dve.tensor_tensor_scan(aT[0:H * NT, P:2 * P], reset[:, :], aT[0:H * NT, 0:P], -BIG, ALU.min, ALU.max)\
                .then_inc(gate_dve, 1)
            dve.wait_ge(gate_pe, 3)
            dve.tensor_copy(cm, ps[6][:, P:P + H * NT].rearrange("p (h c) -> p h c", h=H)).then_inc(gate_dve, 1)
            dve.wait_ge(gate_pe, 4)
            bl, cml = tmp, lf
            link(dve.tensor_copy(bl, ps[7][:, 64:64 + H * NT].rearrange("p (h c) -> p h c", h=H)))
            link(dve.tensor_copy(cml, ps[6][:, 2 * P:2 * P + H * NT].rearrange("p (h c) -> p h c", h=H)))
            link(dve.memset(mp[:, :, 0:1], 0.0))
            link(dve.tensor_copy(mp[:, :, NP], m_in[:, :]))
            for hh in range(H):
                link(dve.tensor_tensor_scan(mn[:, hh, 0:NP], cml[:, hh, 0:NP], bl[:, hh, 0:NP], 0.0, ALU.max, ALU.add))
            link(dve.tensor_copy(mp[:, :, 1:NP], mn[:, :, 0:NP - 1]))
            ml = cml
            link(dve.tensor_tensor(ml, mp, cml, ALU.max))
            link(dve.tensor_tensor(mn[:, :, NP], ml[:, :, NP], bl[:, :, NP], ALU.add))
            link(dve.tensor_tensor(pack[:, :, Q_M, :], mp, cm, ALU.max))
            dve.tensor_copy(pack[:, :, Q_A, :], a)
            dve.tensor_copy(m_out[:, 0, :], mn[:, :, NP - 1])
            link(dve.tensor_copy(m_out[:, 1, :], mn[:, :, NP]))
            dve.tensor_tensor(pack[:, :, Q_WI, :], mp, pack[:, :, Q_M, :], ALU.subtract)
            link(dve.tensor_tensor(mt, bt, pack[:, :, Q_M, :], ALU.add))
            dve.tensor_scalar(pack[:, :, Q_EMT, :], mt, -1.0, None, ALU.mult)
            dve.tensor_tensor(pack[:, :, Q_WS, :], a, ml, ALU.subtract)
            dve.tensor_tensor(pack[:, :, Q_DECAY, :], mp, ml, ALU.subtract).then_inc(gt_scaled, 1)
            dve.wait_ge(gate_act, 2)
            dve.tensor_tensor(dmat[:, 0, 0:H * DEC_B].rearrange("p (h b) -> p h b", h=H),
                              b_first[:, :].unsqueeze(1).to_broadcast([P, H, DEC_B]),
                              pack[:, :, Q_DECAY, NP].unsqueeze(2).to_broadcast([P, H, DEC_B]), ALU.mult)\
                .then_inc(gate_dve, 1)
            dve.wait_ge(gate_pe, 5)
            dve.tensor_copy(dec_s[:, :, :].rearrange("p h b -> p (h b)"), ps[6][:, 0:H * DEC_B])
            dve.tensor_copy(dec8[0:DEC_B, :], ps[6][0:DEC_B, P:P + H])
            dve.tensor_scalar(tri[:, :], tri[:, :], -BIG, BIG, ALU.mult, ALU.add)
            dve.tensor_scalar(tri_s[:, :], tri_s[:, :], -BIG, BIG, ALU.mult, ALU.add)
            dve.memset(v_tok[:, :, DV:DV + 1], 1.0).then_inc(gate_dve, 1)
            dve.wait_ge(gate_dve, 6)

            HEAD_STEPS = 21
            base = n_link
            with dve.Fori(0, H) as h:
                step = 0

                def hlink(ins):
                    nonlocal step
                    step += 1
                    ins.then_inc(dve_step, 1)
                    dve.wait_ge(dve_step, h * HEAD_STEPS + (base + step))

                hlink(dve.tensor_copy(cur[:, :, :].rearrange("p q c -> p (q c)"),
                                      pack[:, :, :, :].rearrange("p h q c -> p (h q c)")
                                      [:, bass.ds(h * (NQ * NT), NQ * NT)]))
                dve.tensor_copy(g_h[:, :], gains[:, bass.ds(h * 2 + G_OUT, 2)])
                dve.tensor_copy(nstat[:, 4, 0:DEC_B],
                                dec_s[:, :, :].rearrange("p h b -> p (h b)")[:, bass.ds(h * DEC_B, DEC_B)])
                hlink(dve.tensor_copy(nstat[0:DEC_B, 5, 0:1], dec8[0:DEC_B, bass.ds(h, 1)]))

                def q(k):
                    return cur[:, k, :].unsqueeze(2)

                def times_rms(out, b, g):
                    return dve.tensor_tensor(out, bank(b), tok(rstd_a[:, :], g), ALU.mult)

                def q_evac(g):
                    dve.wait_ge(a_mm, h * 15 + g + 1)
                    dve.scalar_tensor_tensor(tok(qT[:, :], g), bank(g), float(DK) ** -0.5, tok(rstd_a[:, :], g),
                                             ALU.mult, ALU.mult).then_inc(a_evac, 1)

                def k_evac(g):
                    dve.wait_ge(a_mm, h * 15 + 3 + g + 1)
                    times_rms(tok(kT[:, :], g), 3 + g, g).then_inc(a_evac, 1)

                def v_evac(n):
                    dve.wait_ge(a_mm, h * 15 + 6 + n + 1)
                    if n >= 2:
                        dve.wait_ge(a_tr, h * 9 + 3 + n - 2 + 1)
                    times_rms(v_tmp[:, (n + 1) % 2 * TG:((n + 1) % 2 + 1) * TG], n, n % 3).then_inc(a_vtmp, 1)

                def weigh_k(g):
                    dve.wait_ge(a_tr, h * 9 + g + 1)
                    dve.tensor_tensor(k_tok[:, g * TPG:(g + 1) * TPG, :], tiles(bank(6 + g % 2)),
                                      q(Q_WS)[:, g * TPG:(g + 1) * TPG, :].to_broadcast([P, TPG, P]), ALU.mult)\
                        .then_inc(a_ktok, 1)

                dve.wait_ge(c_stored, h * 80 + 1)
                q_evac(0)
                q_evac(1)
                q_evac(2)
                k_evac(0)
                k_evac(1)
                weigh_k(0)
                k_evac(2)
                weigh_k(1)
                v_evac(0)
                weigh_k(2)
                for n in range(1, 6):
                    v_evac(n)
                dve.tensor_tensor(k_blk, k_tok[:, NP, :].unsqueeze(1).to_broadcast([P, DEC_B, DK]),
                                  b_mem[:, :].unsqueeze(2).to_broadcast([P, DEC_B, DK]), ALU.mult).then_inc(a_kb, 1)
                eye = ident[:, :].unsqueeze(1).to_broadcast([P, NT, P])
                dve.tensor_tensor(diag, eye, q(Q_M).to_broadcast([P, NT, P]), ALU.mult).then_inc(a_diag, 1)
                dve.tensor_tensor(diag2, eye, q(Q_WI).to_broadcast([P, NT, P]), ALU.mult).then_inc(a_diag, 1)
                for g in range(NG):
                    dve.wait_ge(a_mm, h * 15 + 12 + g + 1)
                    times_rms(bank(g), g, g).then_inc(a_oscaled, 1)
                dve.wait_ge(a_tr, h * 9 + 9)
                for g in range(NG):
                    t = ticket("mb", g)
                    dve.wait_ge(t_pe, h * NTICK + t + 1)
                    part = dmat[:, g * TPG:(g + 1) * TPG, :]
                    if g < NG - 1:
                        ins = dve.tensor_tensor(part, tri[:, :].unsqueeze(1).to_broadcast([P, TPG, P]), tiles(bank(t)),
                                                ALU.add)
                    else:
                        dve.tensor_tensor(part[:, 0:2, :], tri[:, :].unsqueeze(1).to_broadcast([P, 2, P]),
                                          tiles(bank(t))[:, 0:2, :], ALU.add)
                        ins = dve.tensor_tensor(part[:, 2, :], tri_s[:, :], tiles(bank(t))[:, 2, :], ALU.add)
                    ins.then_inc(t_dve, 1)
                    dve.wait_ge(t_dve, h * N_DVE + taken(t))
                    dve.tensor_tensor(part, q(Q_A)[:, g * TPG:(g + 1) * TPG, :].to_broadcast([P, TPG, P]), part,
                                      ALU.subtract).then_inc(a_dargs, 1)
                for g in range(NG):
                    t = ticket("wib", g)
                    dve.wait_ge(t_pe, h * NTICK + ticket("wib", NG - 1) + 1)
                    dve.tensor_tensor(tok(qw[:, :], g), tok(qT[:, :], g), bank(t), ALU.mult).then_inc(t_dve, 1)
                dve.wait_ge(t_dve, h * N_DVE + taken(ticket("wib", NG - 1)))
                for g in range(NG):
                    t = ticket("s", g)
                    dve.wait_ge(t_pe, h * NTICK + t + 1)
                    dve.wait_ge(a_exp, h * 3 + g + 1)
                    part = dmat[:, g * TPG:(g + 1) * TPG, :]
                    dve.tensor_tensor(part, part, tiles(bank(t)), ALU.mult).then_inc(t_dve, 1)
                hlink(dve.memset(state[:, 0, :], 0.0))
                for c in range(NP):
                    t = ticket("u", c)
                    dve.wait_ge(t_pe, h * NTICK + t + 1)
                    dve.scalar_tensor_tensor(state[:, c + 1, :], state[:, c, :], cur[:, Q_DECAY, c:c + 1],
                                             bank(t, DV + 1), ALU.mult, ALU.add).then_inc(t_dve, 1)
                    dve.wait_ge(t_dve, h * N_DVE + taken(t))
                for j in range(2):
                    for half in range(2):
                        t = ticket("us", 2 * j + half)
                        bs = slice(4 * half, 4 * half + 4)
                        dve.wait_ge(t_pe, h * NTICK + t + 1)
                        hlink(dve.tensor_tensor(c_nat[:, j, bs, :], c_nat[:, j, bs, :],
                                                nstat[:, 4, bs].unsqueeze(2).to_broadcast([P, 4, DK]), ALU.mult))
                        dve.tensor_tensor(c_nat[:, j, bs, :], c_nat[:, j, bs, :],
                                          ps[t % 8][:, :].rearrange("p (b d) -> p b d", b=4), ALU.add)\
                            .then_inc(t_dve, 1)
                t = ticket("un")
                dve.wait_ge(t_pe, h * NTICK + t + 1)
                dve.scalar_tensor_tensor(n_nat[:, :], n_nat[:, :], nstat[0:DEC_B, 5, 0:1], ps[t % 8][0:DEC_B, 0:DK],
                                         ALU.mult, ALU.add).then_inc(t_dve, 1)
                hlink(dve.memset(q_blk[:, :, :], 0.0))
                for b in range(DEC_B):
                    sl = slice(b * DEC_S, (b + 1) * DEC_S)
                    ins = dve.tensor_copy(q_blk[:, b, sl], qw[:, NP * P + b * DEC_S:NP * P + (b + 1) * DEC_S])
                ins.then_inc(a_qblk, 1)
                for c in range(NT):
                    t = ticket("pv", c)
                    dve.wait_ge(t_pe, h * NTICK + t + 1)
                    dve.tensor_copy(num[:, c, :], bank(t, DV + 1)).then_inc(t_dve, 1)
                dve.wait_ge(t_dve, h * N_DVE + taken(ticket("pv", NT - 1)))
                ssq, r, t2, std = (nstat[:, k, :] for k in range(4))
                den = num[:, :, DV]
                hlink(dve.tensor_scalar(r, den, -1.0, None, ALU.mult))
                hlink(dve.tensor_tensor(r, r, den, ALU.max))
                hlink(dve.tensor_tensor(r, r, cur[:, Q_EMT, :], ALU.max))
                hlink(dve.reciprocal(r, r))
                dve.wait_ge(a_ssq, h * NT + NT)
                hlink(dve.tensor_tensor(t2, ssq, r, ALU.mult))
                dve.tensor_tensor(t2, t2, r, ALU.mult).then_inc(a_sqrt, 1)
                dve.wait_ge(a_sqrt, h * 2 + 2)
                hlink(dve.reciprocal(std, std))
                hlink(dve.tensor_tensor(r, r, std, ALU.mult))
                dve.tensor_tensor(num[:, :, 0:DV], num[:, :, 0:DV], r.unsqueeze(2).to_broadcast([P, NT, DV]), ALU.mult)\
                    .then_inc(a_fac, 1)

                def scale_o(g):
                    t = ticket("o", g)
                    dve.wait_ge(t_pe, h * NTICK + t + 1)
                    times_rms(bank(t), t, g).then_inc(a_oscaled, 1)

                scale_o(0)
                scale_o(1)
                for g in range(NG):
                    if g == 1:
                        scale_o(2)
                    for j in range(2):
                        t = ticket("ht", 2 * g + j)
                        buf = h_f[:, j * TG:(j + 1) * TG]
                        dve.wait_ge(t_pe, h * NTICK + t + 1)
                        if j == 1:
                            dve.wait_ge(t_act, h * N_ACT + taken(ticket("o", g)))
                        dve.scalar_tensor_tensor(buf, bank(t), g_h[:, j:j + 1], tok(sig_o[:, j, :], g),
                                                 ALU.mult, ALU.mult).then_inc(t_dve, 1)
                        dve.wait_ge(t_dve, h * N_DVE + taken(t))
                        hlink(dve.tensor_copy(tok(h_hi[:, j, :], g), buf))
                        dve.tensor_tensor(tok(h_lo[:, j, :], g), buf, tok(h_hi[:, j, :], g).bitcast(F32),
                                          ALU.subtract).then_inc(a_hlo, 1)
                for n in range(24):
                    g, j = n // KD, n % KD
                    dve.wait_ge(wd_mm, h * 24 + n + 1)
                    dve.tensor_tensor(tok(xT[:, j, :], g), tok(xT[:, j, :], g), bank(n % 6), ALU.add)\
                        .then_inc(wd_add, 1)
                assert step == HEAD_STEPS, step
            n_link = base + HEAD_STEPS * H

            def ffn(layer, n, k):
                for _ in range(6):
                    dve.drain().then_inc(d_add[layer], 1)
                norm(n, G_FFN + KD * layer, k, rstd_f)
                with dve.Fori(0, N_FFN) as i:
                    for c in range(2):
                        for g in range(NG):
                            m = 3 * c + g
                            dve.wait_ge(g_mm[layer], i * 6 + m + 1)
                            dve.tensor_tensor(bank(g), bank(g), tok(rstd_f[:, :], g), ALU.mult)\
                                .then_inc(g_scaled[layer], 1)
                        for g in range(NG):
                            m = 3 * c + g
                            buf = h_tmp[:, m % 2, :]
                            dve.wait_ge(g_silu[layer], i * 6 + m + 1)
                            dve.tensor_tensor(silu[:, c, g, :], silu[:, c, g, :], tok(rstd_f[:, :], g), ALU.mult)\
                                .then_inc(s_scaled[layer], 1)
                            dve.wait_ge(s_scaled[layer], i * 6 + m + 1)
                            dve.wait_ge(u_mm[layer], i * 6 + m + 1)
                            dve.tensor_tensor(buf, silu[:, c, g, :], bank(3 + g), ALU.mult).then_inc(h_full[layer], 1)
                            dve.wait_ge(h_full[layer], i * 6 + m + 1)
                            dve.tensor_copy(tok(hg_hi[:, c, :], g), buf).then_inc(h_his[layer], 1)
                            dve.wait_ge(h_his[layer], i * 6 + m + 1)
                            dve.tensor_tensor(tok(hg_lo[:, c, :], g), buf, tok(hg_hi[:, c, :], g).bitcast(F32),
                                              ALU.subtract).then_inc(h_los[layer], 1)
                    for m in range(24):
                        g, j = m // KD, m % KD
                        dve.wait_ge(d_mm[layer], i * 24 + m + 1)
                        dve.tensor_tensor(tok(xT[:, j, :], g), tok(xT[:, j, :], g), bank(m % 6), ALU.add)\
                            .then_inc(d_add[layer], 1)

            ffn(0, 1, 1)
            norm(2, G_MIX + KD, 2, rstd_b)
            for _ in range(6):
                dve.drain().then_inc(bu_gate, 1)
            vrow = vs[:, :, :, :].rearrange("p c f t -> p c (f t)")
            with dve.Fori(0, NF // 4) as i:

                def scale_v(n):
                    dve.wait_ge(bv_mm, i * 12 + n + 1)
                    dve.tensor_tensor(bank(n % 6), bank(n % 6), tok(rstd_b[:, :], n % 3), ALU.mult)\
                        .then_inc(bv_scaled, 1)

                scale_v(0)
                for n in range(12):
                    u, g = n // 3, n % 3
                    if n < 11:
                        scale_v(n + 1)
                    dve.wait_ge(bv_tr, i * 12 + n + 3)
                    chunk = vs[:, g * TPG:(g + 1) * TPG, bass.ds(i * 4 + u, 1), :]
                    dve.tensor_copy(chunk.rearrange("p c o t -> p c (o t)"), tiles(bank(6 + n % 2)))\
                        .then_inc(bv_tok, 1)
                    if u == 3:
                        dve.wait_ge(bv_tok, i * 12 + n + 1)
                        for c in range(g * TPG, (g + 1) * TPG):
                            ins = dve.bn_stats(stat[:, c, bass.ds(i, 1), :].rearrange("p o s -> p (o s)"),
                                               vrow[:, c, bass.ds(i * (4 * P), 4 * P)])
                        ins.then_inc(bv_stat, 1)
            dve.wait_ge(bv_stat, NG * (NF // 4))
            dve.wait_ge(bv_gelu, 12 * (NF // 4))
            for c in range(NT):
                ins = dve.bn_aggr(mv[:, c, :], stat[:, c, :, :].rearrange("p q s -> p (q s)"))
            ins.then_inc(ln_stat, 1)
            dve.wait_ge(ln_root, 1)
            link(dve.reciprocal(rs_v[:, :, 1], rs_v[:, :, 0]))
            dve.scalar_tensor_tensor(rs_v[:, :, 2], mv[:, :, 0], -1.0, rs_v[:, :, 1], ALU.mult, ALU.mult)\
                .then_inc(ln_scale, 1)
            for c in LN_DVE:
                dve.tensor_scalar(vrow[:, c, :], vrow[:, c, :], mv[:, c, 0:1], rs_v[:, c, 1:2], ALU.subtract, ALU.mult)\
                    .then_inc(ln_dve, 1)
            dve.wait_ge(b_loaded, 16 * (1 + DEC_B))
            link(dve.tensor_copy(mix[:, 0, :, 0:DEC_S], w_s_smp[:, :, 0:DEC_S]))
            for b in range(DEC_B):
                ins = dve.tensor_copy(w_s_smp[:, :, b * DEC_S:(b + 1) * DEC_S], mix[:, 0, :, 0:DEC_S])
            ins.then_inc(bw_copied, 1)
            for t_ in (tri, tri_s):
                link(dve.tensor_scalar(t_[:, :], t_[:, :], 0.0, None, ALU.is_equal))
            for k, t_ in enumerate((tri, tri_s)):
                dve.wait_ge(bw_tr, k + 1)
                ins = dve.tensor_tensor(mix[:, k, :, :], ps[6 + k][:, :].rearrange("p (g t) -> p g t", g=G_B),
                                        t_[:, :].unsqueeze(1).to_broadcast([P, G_B, P]), ALU.mult)
            ins.then_inc(mix_ok, 1)

            def gain_rows_of_v(q):
                dve.wait_ge(gv_loaded[q % 2], 16 * (q // 2 + 1))
                dve.wait_ge(ln_dve, 1)
                dve.tensor_tensor(row_buf[q % 2], vrow[:, NP, q * RQ:(q + 1) * RQ], row_buf[q % 2], ALU.mult)\
                    .then_inc(gv_done, 1)

            for c in range(NT):
                if c in (3, 7):
                    gain_rows_of_v(c // 4 * 2)
                    gain_rows_of_v(c // 4 * 2 + 1)
                if c == NP:
                    dve.wait_ge(gv_done, 4)
                for q in range(0, 4, 2):
                    t = 4 * c + q
                    dve.wait_ge(mx_mm, t + 1)
                    dve.tensor_copy(vs[:, c, FPG * q:FPG * (q + 1), :],
                                    ps[6 + t % 2][:, :].rearrange("p (f t) -> p f t", f=FPG)).then_inc(mx_dve, 1)
            dve.wait_ge(b_mixed, 16)
            dve.wait_ge(mx_act, 2 * NT)
            dve.wait_ge(row_stored[1], 32)
            widen(3, rstd_b, lambda g: t_b[:, g % 2, :], 2)
            with dve.Fori(0, NF // 4) as i:
                for n in range(12):
                    u, g = n // 3, n % 3
                    piece = vs[:, g * TPG:(g + 1) * TPG, bass.ds(i * 4 + u, 1), :].rearrange("p c o t -> p c (o t)")
                    buf = t_b[:, n % 2, :]
                    gain = gains[:, bass.ds(i * 4 + (G_V + u), 1)]
                    pr = bias_b[:, bass.ds(i, 1), :]
                    sm = pr[:, :, 0:DEC_S].to_broadcast([P, DEC_B, DEC_S])
                    if g < NG - 1:
                        ins = dve.scalar_tensor_tensor(tiles(buf), piece, gain, pr.to_broadcast([P, TPG, P]),
                                                       ALU.mult, ALU.add)
                    else:
                        dve.scalar_tensor_tensor(tiles(buf)[:, 0:2, :], piece[:, 0:2, :], gain,
                                                 pr.to_broadcast([P, 2, P]), ALU.mult, ALU.add)
                        ins = dve.scalar_tensor_tensor(
                            tiles(buf)[:, 2, :].rearrange("p (b s) -> p b s", b=DEC_B),
                            piece[:, 2, :].rearrange("p (b s) -> p b s", b=DEC_B), gain, sm, ALU.mult, ALU.add)
                    ins.then_inc(bu_bias, 1)
                    dve.wait_ge(bu_mm, i * 12 + n + 1)
                    dve.tensor_tensor(bank(n % 6), bank(n % 6), tok(rstd_b[:, :], g), ALU.mult).then_inc(bu_scaled, 1)
                    dve.wait_ge(bu_bias, i * 12 + n + 1)
                    dve.wait_ge(bu_gelu, i * 12 + n + 1)
                    dve.tensor_tensor(piece, tiles(buf), tiles(bank(n % 6)), ALU.mult).then_inc(bu_gate, 1)
            for _ in range(6):
                dve.drain().then_inc(bo_add, 1)
            dve.wait_ge(bu_gate, 6 + 12 * (NF // 4))
            for n, (g, f) in enumerate(P_ORDER):
                dve.wait_ge(ps_hi, n + 1)
                dve.tensor_tensor(p_lo[:, g * TPG:(g + 1) * TPG, f, :], vs[:, g * TPG:(g + 1) * TPG, f, :],
                                  tiles(tok(p_hi[:, f, :], g)).bitcast(F32), ALU.subtract).then_inc(ps_lo, 1)
            with dve.Fori(0, KD // 2) as i:
                for n in range(6):
                    j, g = n // 3, n % 3
                    dve.wait_ge(bo_mm, i * 6 + n + 1)
                    out = tok(xT[:, :, :], g)[:, bass.ds(i * 2 + j, 1), :].rearrange("p o t -> p (o t)")
                    dve.tensor_tensor(out, out, bank(n), ALU.add).then_inc(bo_add, 1)

            ffn(1, 3, 4)
            for g in range(NG):
                add_up(4, g)
            invert(4)
            for c in range(NT):
                dve.wait_ge(yt_pe, 2 * c + 1)
                dve.tensor_scalar(y_out[:, c, 0:D // 2], ps[(2 * c) % 8][:, :], r_tok[:, c:c + 1], None,
                                  ALU.mult).then_inc(yt_dve, 1)


_INS = ['x_prompt', 'x_sample', 'state_C', 'state_n', 'state_m', 'g_mix', 'g_ffn', 'g_final',
        'a_w_in', 'a_b_gate', 'a_g_out', 'a_w_out', 'b_w_in', 'b_g_v', 'b_w_s', 'b_b_s', 'b_w_out',
        'f_w_gu', 'f_w_down']
_OUTS = [(1, SEQ, D), (DEC_B, DEC_S, D), (1, 1, H, DV, DK), (1, 1, H, DK), (1, 1, H),
         (DEC_B, 1, H, DV, DK), (DEC_B, 1, H, DK), (DEC_B, 1, H), (DEC_B, 1, DEC_S, INNER)]


def kernel(**inputs):
    import numpy as _np
    import concourse.bacc as _bacc
    from concourse.bass_utils import run_bass_kernel_spmd as _run

    nc = _bacc.Bacc("TRN2", target_bir_lowering=False, num_devices=1, dynamic_dma_scratch_size=64)
    arrays, args = {}, []
    for name in _INS:
        a = _np.ascontiguousarray(inputs[name])
        arrays[f"in_{name}_dram"] = a
        args.append(nc.dram_tensor(f"in_{name}_dram", a.shape, mybir.dt.from_np(a.dtype), kind="ExternalInput").ap())
    for i, shape in enumerate(_OUTS):
        args.append(nc.dram_tensor(f"out_{i}_dram", shape, F32, kind="ExternalOutput").ap())
    build(nc, *args)
    r = _run(nc, [arrays], core_ids=[0])
    return tuple(r.results[0][f"out_{i}_dram"] for i in range(len(_OUTS)))
```
